# Optimizing a Trainium2 kernel written in Bass

```python
import jax, jax.numpy as jnp
from jax import lax
import numpy as np

D_MODEL = 1024
BATCH = 1
SEQ = 256
DEPTH = 2
DEC_BATCH = 8
DEC_SEQ = 1
PAST_LEN = 2048
PAGE_SIZE = 128

MIX_DIM = 2 * D_MODEL
RWKV_DIM = MIX_DIM // 2
RWKV_HEAD = 64
RWKV_HEADS = RWKV_DIM // RWKV_HEAD
DECAY_LORA = 64
AAA_LORA = 64
GATE_LORA = 160
RWKV_PROJ = 3 * RWKV_DIM + DECAY_LORA + AAA_LORA + GATE_LORA
RWKV_GN_EPS = 64e-5
SC_DIM = MIX_DIM // 4
SC_WIDTH = 3
SC_PROJ = 3 * SC_DIM
SSM_DIM = MIX_DIM // 4
SSM_HEADDIM = 64
SSM_HEADS = SSM_DIM // SSM_HEADDIM
SSM_GROUPS = 2
SSM_STATE = 128
SSM_CONV = 4
SSM_CONV_DIM = SSM_DIM + 2 * SSM_GROUPS * SSM_STATE
SSM_PROJ = SSM_DIM + SSM_CONV_DIM + SSM_HEADS
SSD_CHUNK = 128
IN_COLS = RWKV_PROJ + SC_PROJ + SSM_PROJ
D_FF = 2816
NORM_EPS = 1e-6

kernel_name = 'hymba_rwkv7_shortconv_mamba2_macaron_step'

def rmsnorm(x, g):
    xf = x.astype(jnp.float32)
    y = xf * lax.rsqrt(jnp.mean(xf * xf, axis=-1, keepdims=True) + NORM_EPS)
    return (y * g.astype(jnp.float32)).astype(x.dtype)

def swiglu(x, w_in, w_out):
    gate, up = jnp.split(x @ w_in, 2, axis=-1)
    return (jax.nn.silu(gate) * up) @ w_out

def causal_depthwise_conv(u, buf, w):
    width = w.shape[0]
    L = u.shape[1]
    padded = jnp.concatenate([buf.astype(u.dtype), u], axis=1)
    out = sum(padded[:, j:j + L] * w[j] for j in range(width))
    return out, padded[:, L:]

def rwkv7_mix(proj, shift_prev, wkv0, mu, w0, w2, a0, a2, g2, k_k, k_a, r_k, ln_w, ln_b):
    f32 = jnp.float32
    Bsz, L, _ = proj.shape
    prev = jnp.concatenate([shift_prev[:, None].astype(proj.dtype), proj[:, :-1]], axis=1)
    xs = proj + (prev - proj) * mu
    new_shift = proj[:, -1]
    r, k, v, w_lr, a_lr, g_lr = jnp.split(
        xs, [RWKV_DIM, 2 * RWKV_DIM, 3 * RWKV_DIM, 3 * RWKV_DIM + DECAY_LORA,
             3 * RWKV_DIM + DECAY_LORA + AAA_LORA], axis=-1)
    w = -jax.nn.softplus(-(w0 + jnp.tanh(w_lr) @ w2).astype(f32)) - 0.5
    decay = jnp.exp(-jnp.exp(w))
    a = jax.nn.sigmoid((a0 + a_lr @ a2).astype(f32))
    g = jax.nn.sigmoid(g_lr) @ g2
    heads = lambda t: t.astype(f32).reshape(Bsz, L, RWKV_HEADS, RWKV_HEAD)
    r, k, v, decay, a = heads(r), heads(k), heads(v), heads(decay), heads(a)
    kk = k * k_k.astype(f32).reshape(RWKV_HEADS, RWKV_HEAD)
    kk = kk * lax.rsqrt(jnp.maximum(jnp.sum(kk * kk, axis=-1, keepdims=True), 1e-24))
    k = k * (1.0 + (a - 1.0) * k_a.astype(f32).reshape(RWKV_HEADS, RWKV_HEAD))
    b = kk * a

    def step(S, inp):
        r_t, w_t, k_t, v_t, kk_t, b_t = inp
        Sa = jnp.einsum('bhij,bhj->bhi', S, -kk_t)
        S = S * w_t[:, :, None, :] + Sa[..., None] * b_t[:, :, None, :] + v_t[..., None] * k_t[:, :, None, :]
        return S, jnp.einsum('bhij,bhj->bhi', S, r_t)

    seq_in = tuple(jnp.moveaxis(t, 1, 0) for t in (r, decay, k, v, kk, b))
    S_final, y = lax.scan(step, wkv0.astype(f32), seq_in)
    y = jnp.moveaxis(y, 0, 1)
    mean = jnp.mean(y, axis=-1, keepdims=True)
    var = jnp.mean(jnp.square(y - mean), axis=-1, keepdims=True)
    y = ((y - mean) * lax.rsqrt(var + RWKV_GN_EPS)).reshape(Bsz, L, RWKV_DIM)
    y = y * ln_w.astype(f32) + ln_b.astype(f32)
    bonus = jnp.sum(r * k * r_k.astype(f32), axis=-1, keepdims=True) * v
    y = (y + bonus.reshape(Bsz, L, RWKV_DIM)) * g.astype(f32)
    return y.astype(proj.dtype), new_shift, S_final.astype(wkv0.dtype)

def short_conv_mix(proj, buf, conv_w, norm_g):
    b_gate, c_gate, xt = jnp.split(proj, 3, axis=-1)
    conv, new_buf = causal_depthwise_conv(c_gate * xt, buf, conv_w)
    return rmsnorm(b_gate * conv, norm_g), new_buf

def ssd_scan(x, dt, A, Bm, Cm, h0):
    Bsz, L, H, P = x.shape
    Q = min(SSD_CHUNK, L)
    nc = -(-L // Q)
    pad = nc * Q - L
    if pad:
        padw = lambda t: jnp.pad(t, [(0, 0), (0, pad)] + [(0, 0)] * (t.ndim - 2))
        x, dt, Bm, Cm = padw(x), padw(dt), padw(Bm), padw(Cm)
    chunk = lambda t: t.reshape((Bsz, nc, Q) + t.shape[2:])
    x, dt, Bm, Cm = chunk(x), chunk(dt), chunk(Bm), chunk(Cm)
    cum = jnp.cumsum(dt * A, axis=2)
    seg = cum[:, :, :, None, :] - cum[:, :, None, :, :]
    causal = jnp.tril(jnp.ones((Q, Q), dtype=bool))[None, None, :, :, None]
    decay_mask = jnp.exp(jnp.where(causal, seg, -jnp.inf))
    xdt = x * dt[..., None]
    scores = jnp.einsum('bcihn,bcjhn->bcijh', Cm, Bm) * decay_mask
    y_diag = jnp.einsum('bcijh,bcjhp->bcihp', scores, xdt)
    decay_end = jnp.exp(cum[:, :, -1:, :] - cum)
    chunk_states = jnp.einsum('bcjhn,bcjh,bcjhp->bchpn', Bm, decay_end, xdt)
    chunk_decay = jnp.exp(cum[:, :, -1, :])

    def step(h, inp):
        s, d = inp
        return h * d[:, :, None, None] + s, h

    h_final, h_prev = lax.scan(step, h0, (jnp.moveaxis(chunk_states, 1, 0), jnp.moveaxis(chunk_decay, 1, 0)))
    h_prev = jnp.moveaxis(h_prev, 0, 1)
    y_off = jnp.einsum('bcihn,bchpn,bcih->bcihp', Cm, h_prev, jnp.exp(cum))
    y = (y_diag + y_off).reshape(Bsz, nc * Q, H, P)[:, :L]
    return y, h_final

def mamba2_mix(proj, conv_buf, h0, conv_w, conv_b, dt_bias, A_log, D, norm_g):
    f32 = jnp.float32
    Bsz, L, _ = proj.shape
    z, xbc, dt = jnp.split(proj, [SSM_DIM, SSM_DIM + SSM_CONV_DIM], axis=-1)
    xbc_c, new_buf = causal_depthwise_conv(xbc, conv_buf, conv_w)
    xbc_c = jax.nn.silu(xbc_c + conv_b)
    xh, Bm, Cm = jnp.split(xbc_c, [SSM_DIM, SSM_DIM + SSM_GROUPS * SSM_STATE], axis=-1)
    xh = xh.astype(f32).reshape(Bsz, L, SSM_HEADS, SSM_HEADDIM)
    rep = SSM_HEADS // SSM_GROUPS
    Bm = jnp.repeat(Bm.astype(f32).reshape(Bsz, L, SSM_GROUPS, SSM_STATE), rep, axis=2)
    Cm = jnp.repeat(Cm.astype(f32).reshape(Bsz, L, SSM_GROUPS, SSM_STATE), rep, axis=2)
    dt = jax.nn.softplus((dt + dt_bias).astype(f32))
    A = -jnp.exp(A_log.astype(f32))
    y, h_final = ssd_scan(xh, dt, A, Bm, Cm, h0.astype(f32))
    y = (y + D.astype(f32)[:, None] * xh).reshape(Bsz, L, SSM_DIM)
    y = y * jax.nn.silu(z.astype(f32))
    yg = y.reshape(Bsz, L, SSM_GROUPS, SSM_DIM // SSM_GROUPS)
    yg = yg * lax.rsqrt(jnp.mean(yg * yg, axis=-1, keepdims=True) + NORM_EPS)
    y = yg.reshape(Bsz, L, SSM_DIM) * norm_g.astype(f32)
    return y.astype(proj.dtype), new_buf, h_final.astype(h0.dtype)

def decoder_layer(x, shift, wkv, sc_buf, ssm_conv, ssm, lp):
    x = x + 0.5 * swiglu(rmsnorm(x, lp['norm_ffn1']), lp['ffn1_w_in'], lp['ffn1_w_out'])
    h = rmsnorm(x, lp['norm_mix'])
    proj = h @ lp['w_in']
    p_rwkv, p_sc, p_ssm = jnp.split(proj, [RWKV_PROJ, RWKV_PROJ + SC_PROJ], axis=-1)
    y_rwkv, shift, wkv = rwkv7_mix(p_rwkv, shift, wkv, lp['rwkv_mu'], lp['rwkv_w0'], lp['rwkv_w2'],
                                   lp['rwkv_a0'], lp['rwkv_a2'], lp['rwkv_g2'], lp['rwkv_k_k'],
                                   lp['rwkv_k_a'], lp['rwkv_r_k'], lp['rwkv_ln_w'], lp['rwkv_ln_b'])
    y_sc, sc_buf = short_conv_mix(p_sc, sc_buf, lp['sc_conv_w'], lp['sc_norm'])
    y_ssm, ssm_conv, ssm = mamba2_mix(p_ssm, ssm_conv, ssm, lp['ssm_conv_w'], lp['ssm_conv_b'],
                                      lp['ssm_dt_bias'], lp['ssm_A_log'], lp['ssm_D'], lp['ssm_norm'])
    x = x + jnp.concatenate([y_rwkv, y_sc, y_ssm], axis=-1) @ lp['w_out']
    x = x + 0.5 * swiglu(rmsnorm(x, lp['norm_ffn2']), lp['ffn2_w_in'], lp['ffn2_w_out'])
    return x, (shift, wkv, sc_buf, ssm_conv, ssm)

def run_trunk(x, states, weights, norm_final):
    new = ([], [], [], [], [])
    for i in range(DEPTH):
        lp = {name: w[i] for name, w in weights.items()}
        x, layer_states = decoder_layer(x, states[0][i], states[1][i], states[2][i], states[3][i], states[4][i], lp)
        for lst, s in zip(new, layer_states):
            lst.append(s)
    return rmsnorm(x, norm_final), tuple(jnp.stack(lst) for lst in new)

def setup_inputs(seed: int = 0) -> dict:
    key = jax.random.key(seed)
    keys = iter(jax.random.split(key, 64))
    nrm = lambda shape, scale=1.0: scale * jax.random.normal(next(keys), shape, jnp.float32)
    gain = lambda shape: 1.0 + nrm(shape, 0.02)
    uni = lambda shape, lo, hi: jax.random.uniform(next(keys), shape, jnp.float32, lo, hi)
    dt_init = jnp.exp(uni((DEPTH, SSM_HEADS), float(np.log(1e-3)), float(np.log(1e-1))))
    return {
        'x_prompt': nrm((BATCH, SEQ, D_MODEL)),
        'x_sample': nrm((DEC_BATCH, DEC_SEQ, D_MODEL)),
        'state_rwkv_shift': nrm((DEPTH, DEC_BATCH, RWKV_PROJ)),
        'state_rwkv_wkv': nrm((DEPTH, DEC_BATCH, RWKV_HEADS, RWKV_HEAD, RWKV_HEAD), 0.5),
        'state_sc_buf': nrm((DEPTH, DEC_BATCH, SC_WIDTH - 1, SC_DIM)),
        'state_ssm_conv': nrm((DEPTH, DEC_BATCH, SSM_CONV - 1, SSM_CONV_DIM)),
        'state_ssm': nrm((DEPTH, DEC_BATCH, SSM_HEADS, SSM_HEADDIM, SSM_STATE), 0.5),
        'norm_ffn1': gain((DEPTH, D_MODEL)),
        'ffn1_w_in': nrm((DEPTH, D_MODEL, 2 * D_FF), D_MODEL ** -0.5),
        'ffn1_w_out': nrm((DEPTH, D_FF, D_MODEL), D_FF ** -0.5),
        'norm_mix': gain((DEPTH, D_MODEL)),
        'w_in': nrm((DEPTH, D_MODEL, IN_COLS), D_MODEL ** -0.5),
        'rwkv_mu': uni((DEPTH, RWKV_PROJ), 0.0, 1.0),
        'rwkv_w0': uni((DEPTH, RWKV_DIM), -6.0, 0.0),
        'rwkv_w2': nrm((DEPTH, DECAY_LORA, RWKV_DIM), 0.5 * DECAY_LORA ** -0.5),
        'rwkv_a0': nrm((DEPTH, RWKV_DIM), 0.1),
        'rwkv_a2': nrm((DEPTH, AAA_LORA, RWKV_DIM), AAA_LORA ** -0.5),
        'rwkv_g2': nrm((DEPTH, GATE_LORA, RWKV_DIM), GATE_LORA ** -0.5),
        'rwkv_k_k': 0.85 + nrm((DEPTH, RWKV_DIM), 0.05),
        'rwkv_k_a': 1.0 + nrm((DEPTH, RWKV_DIM), 0.05),
        'rwkv_r_k': nrm((DEPTH, RWKV_HEADS, RWKV_HEAD), 0.1),
        'rwkv_ln_w': gain((DEPTH, RWKV_DIM)),
        'rwkv_ln_b': nrm((DEPTH, RWKV_DIM), 0.02),
        'sc_conv_w': nrm((DEPTH, SC_WIDTH, SC_DIM), SC_WIDTH ** -0.5),
        'sc_norm': gain((DEPTH, SC_DIM)),
        'ssm_conv_w': nrm((DEPTH, SSM_CONV, SSM_CONV_DIM), SSM_CONV ** -0.5),
        'ssm_conv_b': nrm((DEPTH, SSM_CONV_DIM), 0.02),
        'ssm_dt_bias': dt_init + jnp.log(-jnp.expm1(-dt_init)),
        'ssm_A_log': jnp.log(uni((DEPTH, SSM_HEADS), 1.0, 16.0)),
        'ssm_D': 1.0 + nrm((DEPTH, SSM_HEADS), 0.1),
        'ssm_norm': gain((DEPTH, SSM_DIM)),
        'w_out': nrm((DEPTH, MIX_DIM, D_MODEL), MIX_DIM ** -0.5),
        'norm_ffn2': gain((DEPTH, D_MODEL)),
        'ffn2_w_in': nrm((DEPTH, D_MODEL, 2 * D_FF), D_MODEL ** -0.5),
        'ffn2_w_out': nrm((DEPTH, D_FF, D_MODEL), D_FF ** -0.5),
        'norm_final': gain((D_MODEL,)),
    }

def reference(x_prompt, x_sample, state_rwkv_shift, state_rwkv_wkv, state_sc_buf, state_ssm_conv, state_ssm,
              norm_ffn1, ffn1_w_in, ffn1_w_out, norm_mix, w_in, rwkv_mu, rwkv_w0, rwkv_w2, rwkv_a0, rwkv_a2,
              rwkv_g2, rwkv_k_k, rwkv_k_a, rwkv_r_k, rwkv_ln_w, rwkv_ln_b, sc_conv_w, sc_norm, ssm_conv_w,
              ssm_conv_b, ssm_dt_bias, ssm_A_log, ssm_D, ssm_norm, w_out, norm_ffn2, ffn2_w_in, ffn2_w_out,
              norm_final):
    weights = {
        'norm_ffn1': norm_ffn1, 'ffn1_w_in': ffn1_w_in, 'ffn1_w_out': ffn1_w_out, 'norm_mix': norm_mix,
        'w_in': w_in, 'rwkv_mu': rwkv_mu, 'rwkv_w0': rwkv_w0, 'rwkv_w2': rwkv_w2, 'rwkv_a0': rwkv_a0,
        'rwkv_a2': rwkv_a2, 'rwkv_g2': rwkv_g2, 'rwkv_k_k': rwkv_k_k, 'rwkv_k_a': rwkv_k_a,
        'rwkv_r_k': rwkv_r_k, 'rwkv_ln_w': rwkv_ln_w, 'rwkv_ln_b': rwkv_ln_b, 'sc_conv_w': sc_conv_w,
        'sc_norm': sc_norm, 'ssm_conv_w': ssm_conv_w, 'ssm_conv_b': ssm_conv_b, 'ssm_dt_bias': ssm_dt_bias,
        'ssm_A_log': ssm_A_log, 'ssm_D': ssm_D, 'ssm_norm': ssm_norm, 'w_out': w_out,
        'norm_ffn2': norm_ffn2, 'ffn2_w_in': ffn2_w_in, 'ffn2_w_out': ffn2_w_out,
    }
    nb, dt_ = x_prompt.shape[0], x_prompt.dtype
    zero_states = (
        jnp.zeros((DEPTH, nb, RWKV_PROJ), dt_),
        jnp.zeros((DEPTH, nb, RWKV_HEADS, RWKV_HEAD, RWKV_HEAD), dt_),
        jnp.zeros((DEPTH, nb, SC_WIDTH - 1, SC_DIM), dt_),
        jnp.zeros((DEPTH, nb, SSM_CONV - 1, SSM_CONV_DIM), dt_),
        jnp.zeros((DEPTH, nb, SSM_HEADS, SSM_HEADDIM, SSM_STATE), dt_),
    )
    y_prompt, p_states = run_trunk(x_prompt, zero_states, weights, norm_final)
    sample_states = (state_rwkv_shift, state_rwkv_wkv, state_sc_buf, state_ssm_conv, state_ssm)
    y_sample, s_states = run_trunk(x_sample, sample_states, weights, norm_final)
    p_rwkv_shift, p_rwkv_wkv, p_sc_buf, p_ssm_conv, p_ssm = p_states
    s_rwkv_shift, s_rwkv_wkv, s_sc_buf, s_ssm_conv, s_ssm = s_states
    return (y_prompt, y_sample, p_rwkv_shift, p_rwkv_wkv, p_sc_buf, p_ssm_conv, p_ssm,
            s_rwkv_shift, s_rwkv_wkv, s_sc_buf, s_ssm_conv, s_ssm)


_drawn_inputs = setup_inputs


def setup_inputs(seed=0):
    import zlib

    import numpy as np

    out = dict(_drawn_inputs(seed))
    spreads = {}
    factors = {'norm_ffn1': 2.882,
     'rwkv_ln_w': 6.584,
     'rwkv_ln_b': 6.029,
     'sc_norm': 4.858,
     'ssm_norm': 2.76,
     'norm_ffn2': 4.95,
     'norm_final': 2.915}
    for name, (base, spread) in spreads.items():
        noise = np.random.default_rng([zlib.crc32(name.encode()), seed]).standard_normal(out[name].shape)
        drawn = base * np.exp(spread * noise) if base else spread * noise
        out[name] = __import__('jax').numpy.asarray(drawn.astype(out[name].dtype))
    for name, factor in factors.items():
        out[name] = (out[name] * factor).astype(out[name].dtype)
    return out
```

```python
from contextlib import ExitStack

import numpy as np

import concourse.bass as bass
from concourse import mybir

F32 = mybir.dt.float32
F32R = mybir.dt.float32r
ALU = mybir.AluOpType
ACT = mybir.ActivationFunctionType
AX = mybir.AxisListType

P = 128
D = 1024
T = 256
NS = 8
N = T + NS
DEPTH = 2
KT = D // P
FF = 2816
FT = FF // P
HS = 64
RT = 8
RWKV_PROJ = 3 * D + 64 + 64 + 160
XT = 27
SC = 512
ST = SC // P
SC_PROJ = 3 * SC
SSM_PROJ = 512 + 1024 + 8
IN_COLS = RWKV_PROJ + SC_PROJ + SSM_PROJ
MT = 2 * KT
C = 64
NCH = T // C
NORM_EPS = 1e-6
GN_EPS = 64e-5
DECAY = float(np.exp(-0.5))
LN_SCALE = 2.0 ** 20
LEVELS = (2, 4, 8, 16, 32)

ROWS_A = (("norm_ffn1", 8), ("norm_mix", 8), ("norm_ffn2", 8), ("rwkv_mu", 27), ("rwkv_w0", 8), ("rwkv_a0", 8),
          ("rwkv_k_k", 8), ("rwkv_k_a", 8), ("rwkv_r_k", 8), ("rwkv_ln_w", 8), ("rwkv_ln_b", 8))
ROWS_B = (("sc_conv_w", 12), ("sc_norm", 4), ("ssm_conv_w", 32), ("ssm_conv_b", 8), ("ssm_norm", 4))
COL = {}
for _rows, _base in ((ROWS_A, 0), (ROWS_B, P)):
    _at = _base
    for _name, _n in _rows:
        COL[_name] = _at
        _at += _n
NCOLS = P + sum(n for _, n in ROWS_B)


def shape_constants():
    i = np.arange(P)
    same = (i[:, None] // C) == (i[None, :] // C)
    parts = {}
    parts["ident"] = np.eye(P)
    parts["mean"] = np.full((P, P), 1.0 / D)
    parts["ones"] = np.ones((P, P))
    parts["head"] = same * 1.0
    parts["cau"] = np.concatenate([same & (i[:, None] < i[None, :]), same & (i[:, None] <= i[None, :])], 1) * 1.0
    parts["low"] = (same & (i[:, None] > i[None, :])) * 1.0

    def level(b):
        return ((i[:, None] // (2 * b)) == (i[None, :] // (2 * b))) & (i[:, None] % (2 * b) >= b) & (i[None, :] % (2 * b) < b)

    parts["first"] = np.concatenate([level(1), level(1).T], 1) * 1.0
    parts["levels"] = np.concatenate([level(b).T for b in LEVELS], 1) * 1.0
    t = np.arange(T)
    parts["neg"] = np.concatenate([np.where(t[None, :] >= i[:, None], 0.0, -1e30),
                                   np.where(i[None, :] >= i[:, None], 0.0, -1e30)], 1)
    one = np.zeros((P, 8, P))
    pair = np.zeros((P, 4, P))
    for h in range(8):
        one[h, h] = 1.0
        pair[h, h // 2, (h % 2) * HS:(h % 2 + 1) * HS] = 1.0
    parts["row8"] = one.reshape(P, -1)
    parts["pair8"] = pair.reshape(P, -1)
    parts["scan"] = np.tile((np.arange(C + 1) > 0) * 1.0, NCH)[None, :].repeat(P, 0)
    at, where = 0, {}
    for name, a in parts.items():
        where[name] = (at, a.shape[1])
        at += a.shape[1]
    return np.concatenate(list(parts.values()), 1).astype(np.float32), where


CONST_WHERE = shape_constants()[1]


class Stage:

    def __init__(self, nc, tag):
        self.nc, self.tag, self.ctx, self.sems, self.named = nc, tag, ExitStack(), [], {}

    def __enter__(self):
        return self

    def sem(self, name):
        s = self.ctx.enter_context(self.nc.semaphore(f"{self.tag}_{name}"))
        self.sems.append(s)
        return s

    def s(self, name):
        if name not in self.named:
            self.named[name] = self.sem(name)
        return self.named[name]

    def sb(self, name, shape, dt=F32):
        return self.ctx.enter_context(self.nc.sbuf_tensor(f"{self.tag}_{name}", shape, dt))

    def __exit__(self, *exc):
        if exc[0] is None:
            with self.nc.Block() as block:
                @block.gpsimd
                def _(pool):
                    for s in self.sems:
                        pool.sem_clear(s)
        self.ctx.close()


class Stream:
    RING = 4

    def __init__(self, st, kp, pieces, halves):
        self.pieces, self.halves = pieces, halves
        self.raw = st.sb("raw", [P, self.RING, kp, 2 * P])
        self.hi = st.sb("hi", [P, self.RING, kp, P], F32R)
        self.lo = st.sb("lo", [P, self.RING, kp, P], F32R)
        self.loaded = [st.sem(f"raw_loaded{i}") for i in range(self.RING)]
        self.hi_ready = st.sem("hi_ready")
        self.lo_ready = [st.sem("lo_ready_pool"), st.sem("lo_ready_dve")]
        self.used = st.sem("half_used")
        self.last, self.landed, total = {}, [], [0] * self.RING
        for n, h in enumerate(halves):
            self.last[h[0]] = n
        for p, dmas in enumerate(pieces):
            total[p % self.RING] += 16 * len(dmas)
            self.landed.append(total[p % self.RING])

    def load(self, sp, p):
        if p >= self.RING:
            n = max(self.last[q] for q in range(p - self.RING + 1)) + 1
            sp.wait_ge(self.hi_ready, n)
            sp.wait_ge(self.lo_ready[0], (n + 1) // 2)
            if n // 2:
                sp.wait_ge(self.lo_ready[1], n // 2)
        for (k, c0, w), src in self.pieces[p]:
            sp.dma_start(self.raw[:, p % self.RING, 0:k, c0:c0 + w], src).then_inc(self.loaded[p % self.RING], 16)

    def _raw(self, n):
        p, c0, w, k = self.halves[n]
        return self.raw[:, p % self.RING, 0:k, c0:c0 + w]

    def split_hi(self, act, n):
        if n >= len(self.halves):
            return
        p, _, w, k = self.halves[n]
        act.wait_ge(self.loaded[p % self.RING], self.landed[p])
        if n >= self.RING:
            act.wait_ge(self.used, n - self.RING + 1)
        act.activation(self.hi[:, n % self.RING, 0:k, 0:w], self._raw(n), ACT.Copy).then_inc(self.hi_ready, 1)

    def split_lo(self, eng, n):
        if n >= len(self.halves):
            return
        _, _, w, k = self.halves[n]
        eng.wait_ge(self.hi_ready, n + 1)
        eng.tensor_tensor(self.lo[:, n % self.RING, 0:k, 0:w], self._raw(n),
                          self.hi[:, n % self.RING, 0:k, 0:w].bitcast(F32), ALU.subtract).then_inc(self.lo_ready[n % 2], 1)

    def product(self, pe, n, out, x_hi, x_lo, start=True, stop=True):
        _, _, w, k = self.halves[n]
        pe.wait_ge(self.hi_ready, n + 1)
        pe.wait_ge(self.lo_ready[n % 2], n // 2 + 1)
        s = n % self.RING
        for j in range(k):
            pe.matmul(out, self.hi[:, s, j, 0:w], x_hi[:, j], start=start and j == 0, stop=False)
            pe.matmul(out, self.hi[:, s, j, 0:w], x_lo[:, j], start=False, stop=False)
            mm = pe.matmul(out, self.lo[:, s, j, 0:w], x_hi[:, j], start=False, stop=stop and j == k - 1)
        mm.then_inc(self.used, 1)


class Env:

    def const(self, name):
        at, n = CONST_WHERE[name]
        return self.cst[:, at:at + n]

    def col(self, name, i=0, n=1):
        return self.cols[:, COL[name] + i:COL[name] + i + n]


def normed_input(st, env, gain, bank):
    h_hi = st.sb("h_hi", [P, KT, N], F32R)
    h_lo = st.sb("h_lo", [P, KT, N], F32R)
    sq = st.sb("norm_sq", [P, KT, N])
    rt = st.sb("norm_root", [P, N])
    rs = st.sb("norm_rs", [P, N])
    squared, summed, rooted = st.sem("squared"), st.sem("mean_summed"), st.sem("rooted")
    inverted, scaled = st.sem("root_inverted"), st.sem("normed")
    hi_done, lo_done = st.sem("h_hi_done"), st.sem("h_lo_done")
    x = env.x

    def act_square(act):
        act.activation(sq[:], x[:], ACT.Square).then_inc(squared, 1)

    def pe_mean(pe):
        pe.wait_ge(squared, 1)
        for k in range(KT):
            mm = pe.matmul(env.ps[:, bank, 0:N], env.const("mean"), sq[:, k], start=k == 0, stop=k == KT - 1)
        mm.then_inc(summed, 1)

    def act_root(act):
        act.wait_ge(summed, 1)
        act.activation(rt[:], env.ps[:, bank, 0:N], ACT.Sqrt, bias=env.eps[:, 0:1]).then_inc(rooted, 1)

    def dve_scale(dve):
        dve.wait_ge(rooted, 1)
        dve.reciprocal(rs[:], rt[:]).then_inc(inverted, 1)
        dve.wait_ge(inverted, 1)
        for k in range(KT):
            dve.scalar_tensor_tensor(out=sq[:, k], in0=x[:, k], scalar=env.col(gain, k), in1=rs[:],
                                     op0=ALU.mult, op1=ALU.mult).then_inc(scaled, 1)

    def act_hi(act):
        for k in range(KT):
            act.wait_ge(scaled, k + 1)
            act.activation(h_hi[:, k], sq[:, k], ACT.Copy).then_inc(hi_done, 1)

    def dve_lo(dve):
        for k in range(KT):
            dve.wait_ge(hi_done, k + 1)
            dve.tensor_tensor(h_lo[:, k], sq[:, k], h_hi[:, k].bitcast(F32), ALU.subtract).then_inc(lo_done, 1)

    def pe_ready(pe):
        pe.wait_ge(hi_done, KT)
        pe.wait_ge(lo_done, KT)

    return h_hi, h_lo, act_square, pe_mean, act_root, dve_scale, act_hi, dve_lo, pe_ready


def ffn_stage(nc, env, layer, tag, gain, w_in, w_out):
    with Stage(nc, tag) as st:
        KP = FT // 2
        wi = w_in[layer].rearrange("(k p) c -> p k c", p=P)
        wo = w_out[layer].rearrange("(k p) c -> p k c", p=P)
        pieces, halves = [], []
        for it in range(FT // 2):
            for part in range(2):
                c0 = part * FF + it * 2 * P
                pieces.append([((KT, 0, 2 * P), wi[:, :, c0:c0 + 2 * P])])
            for off in range(2):
                halves += [(2 * it, off * P, P, KT), (2 * it + 1, off * P, P, KT)]
        for c in range(KT // 2):
            for kh in range(2):
                halves += [(len(pieces), off * P, P, KP) for off in range(2)]
                pieces.append([((KP, 0, 2 * P), wo[:, kh * KP:(kh + 1) * KP, c * 2 * P:(c + 1) * 2 * P])])
        ws = Stream(st, KP, pieces, halves)
        h_hi, h_lo, act_square, pe_mean, act_root, dve_scale, act_hi, dve_lo, pe_ready = normed_input(st, env, gain, 7)
        g_hi = st.sb("hid_hi", [P, FT, N], F32R)
        g_lo = st.sb("hid_lo", [P, FT, N], F32R)
        sg = st.sb("silu_gate", [P, 2, N])
        hid = st.sb("hidden", [P, 2, N])
        silu_done, hid_done = st.sem("silu_done"), st.sem("hidden_done")
        ghi_done, glo_done, x_added = st.sem("hid_hi_done"), st.sem("hid_lo_done"), st.sem("x_added")
        IN = 2 * FT
        OUT = len(halves)

        with nc.Block() as block:
            @block.sync
            def _(sp):
                for p in range(len(pieces)):
                    ws.load(sp, p)

            @block.gpsimd
            def _(pool):
                for n in range(0, OUT, 2):
                    ws.split_lo(pool, n)

            @block.scalar
            def _(act):
                act_square(act)
                for n in range(4):
                    ws.split_hi(act, n)
                act_root(act)
                act_hi(act)

                def silu(m):
                    act.wait_ge(ws.used, 2 * m + 1)
                    if m >= 2:
                        act.wait_ge(hid_done, m - 1)
                    act.activation(sg[:, m % 2], env.ps[:, (2 * m) % 4, 0:N], ACT.Silu).then_inc(silu_done, 1)

                def hidden_hi(m):
                    act.wait_ge(hid_done, m + 1)
                    act.activation(g_hi[:, m], hid[:, m % 2], ACT.Copy).then_inc(ghi_done, 1)

                for m in range(FT):
                    ws.split_hi(act, 2 * m + 4)
                    silu(m)
                    ws.split_hi(act, 2 * m + 5)
                    if m:
                        hidden_hi(m - 1)
                hidden_hi(FT - 1)
                for n in range(IN + 4, OUT):
                    ws.split_hi(act, n)

            @block.vector
            def _(dve):
                ws.split_lo(dve, 1)
                ws.split_lo(dve, 3)
                dve_scale(dve)
                dve_lo(dve)

                def hidden(m):
                    dve.wait_ge(silu_done, m + 1)
                    dve.wait_ge(ws.used, 2 * m + 2)
                    if m >= 2:
                        dve.wait_ge(ghi_done, m - 1)
                        dve.wait_ge(glo_done, m - 1)
                    dve.tensor_tensor(hid[:, m % 2], sg[:, m % 2], env.ps[:, (2 * m + 1) % 4, 0:N],
                                      ALU.mult).then_inc(hid_done, 1)

                def hidden_lo(m):
                    dve.wait_ge(ghi_done, m + 1)
                    dve.tensor_tensor(g_lo[:, m], hid[:, m % 2], g_hi[:, m].bitcast(F32),
                                      ALU.subtract).then_inc(glo_done, 1)

                for m in range(FT):
                    hidden(m)
                    ws.split_lo(dve, 2 * m + 5)
                    if m:
                        hidden_lo(m - 1)
                hidden_lo(FT - 1)
                for mt in range(KT):
                    c, off = mt // 2, mt % 2
                    n = IN + 4 * c + 2 + off
                    if off == 0:
                        ws.split_lo(dve, n + 3)
                        ws.split_lo(dve, n + 5)
                    dve.wait_ge(ws.used, n + 1)
                    dve.scalar_tensor_tensor(out=env.x[:, mt], in0=env.ps[:, mt % 4, 0:N], scalar=0.5, in1=env.x[:, mt],
                                             op0=ALU.mult, op1=ALU.add).then_inc(x_added, 1)

            @block.tensor
            def _(pe):
                pe_mean(pe)
                pe_ready(pe)
                for n in range(IN):
                    m = n // 2
                    if m >= 2:
                        pe.wait_ge(hid_done, m - 1)
                    ws.product(pe, n, env.ps[:, n % 4, 0:N], h_hi, h_lo)
                pe.wait_ge(ghi_done, FT)
                pe.wait_ge(glo_done, FT)
                for n in range(IN, OUT):
                    c, kh, off = (n - IN) // 4, (n - IN) // 2 % 2, n % 2
                    mt = 2 * c + off
                    if mt >= 4 and kh == 0:
                        pe.wait_ge(x_added, mt - 3)
                    ws.product(pe, n, env.ps[:, mt % 4, 0:N], g_hi[:, kh * KP:(kh + 1) * KP],
                               g_lo[:, kh * KP:(kh + 1) * KP], start=kh == 0, stop=kh == 1)


def load_stage(nc, env, d):
    with Stage(nc, "load") as st:
        xp = st.sb("x_rows", [P, 2, D])
        xs = st.sb("x_sample_rows", [NS, D])
        cst_in, rows_in, turned = st.sem("cst_in"), st.sem("rows_in"), st.sem("x_turned")
        eps_set, copied = st.sem("eps_set"), st.sem("x_copied")
        with nc.Block() as block:
            @block.sync
            def _(sp):
                sp.dma_start(env.cst[:], d["cst"]).then_inc(cst_in, 16)
                sp.dma_start(xp[:], d["x_prompt"][0].rearrange("(a p) f -> p a f", p=P)).then_inc(rows_in, 16)
                sp.dma_start(xs[:], d["x_sample"].rearrange("b a f -> (b a) f")).then_inc(rows_in, 16)

            @block.gpsimd
            def _(pool):
                for i, v in enumerate((NORM_EPS, GN_EPS, 1.0)):
                    pool.memset(env.eps[:, i:i + 1], v).then_inc(eps_set, 1)

            @block.tensor
            def _(pe):
                pe.wait_ge(cst_in, 16)
                pe.wait_ge(rows_in, 32)
                for k in range(KT):
                    for a in range(2):
                        pe.transpose(env.ps[:, k, a * P:(a + 1) * P], xp[:, a, k * P:(k + 1) * P], env.const("ident"))
                    pe.transpose(env.ps[:, k, T:N], xs[:, k * P:(k + 1) * P],
                                 env.const("ident")[0:NS, 0:NS]).then_inc(turned, 1)

            @block.vector
            def _(dve):
                for k in range(KT):
                    dve.wait_ge(turned, k + 1)
                    dve.tensor_copy(env.x[:, k], env.ps[:, k, 0:N]).then_inc(copied, 1)


def vector_stage(nc, env, layer, d):
    with Stage(nc, "vec") as st:
        rows = st.sb("vector_rows", [P, 2, P])
        shift = st.sb("shift_rows", [NS, XT * P])
        scb = st.sb("sc_rows", [2 * NS, SC])
        conv = st.sb("conv_rows", [3 * NS, D])
        zeroed, landed = st.sem("rows_zeroed"), st.sem("rows_landed")
        turned, copied, derived = st.sem("rows_turned"), st.sem("cols_copied"), st.sem("cols_derived")
        a_done = st.sem("ssm_a_done")
        loads = []
        for which, group in ((0, ROWS_A), (1, ROWS_B)):
            for name, n in group:
                src = d[name][layer]
                at = COL[name] - which * P
                if name in ("rwkv_r_k", "sc_conv_w", "ssm_conv_w"):
                    src = src.rearrange("a b -> (a b)")
                full = n if name != "rwkv_mu" else n - 1
                loads.append((rows[at:at + full, which, :], src[0:full * P].rearrange("(r f) -> r f", f=P)))
                if full < n:
                    loads.append((rows[at + full:at + n, which, 0:RWKV_PROJ - full * P],
                                  src[full * P:RWKV_PROJ].rearrange("(r f) -> r f", r=1)))
        loads.append((shift[:, 0:RWKV_PROJ], d["state_rwkv_shift"][layer]))
        loads.append((scb[:], d["state_sc_buf"][layer].rearrange("b j f -> (b j) f")))
        loads.append((conv[:], d["state_ssm_conv"][layer].rearrange("b j f -> (b j) f")))
        for i, name in enumerate(("ssm_dt_bias", "ssm_A_log", "ssm_D")):
            loads.append((env.heads[:, i:i + 1], d[name][layer].rearrange("(h o) -> h o", o=1)))
        ps = env.ps
        nb = sum(n for _, n in ROWS_B)
        with nc.Block() as block:
            @block.gpsimd
            def _(pool):
                pool.memset(rows[:], 0.0).then_inc(zeroed, 1)
                pool.memset(shift[:, RWKV_PROJ:XT * P], 0.0).then_inc(zeroed, 1)

            @block.sync
            def _(sp):
                sp.wait_ge(zeroed, 2)
                for dst, src in loads[0::2]:
                    sp.dma_start(dst, src).then_inc(landed, 16)

            @block.scalar
            def _(act):
                act.wait_ge(zeroed, 2)
                for dst, src in loads[1::2]:
                    act.dma_start(dst, src).then_inc(landed, 16)
                act.wait_ge(landed, 16 * len(loads))
                act.activation(env.heads[:, 3:4], env.heads[:, 1:2], ACT.Exp).then_inc(a_done, 1)

            @block.tensor
            def _(pe):
                ident = env.const("ident")
                pe.wait_ge(landed, 16 * len(loads))
                pe.transpose(ps[:, 0, 0:P], rows[:, 0, :], ident)
                pe.transpose(ps[:, 0, P:P + nb], rows[0:nb, 1, :], ident[0:nb, 0:nb])
                for m in range(XT):
                    pe.transpose(ps[:, 1, m * NS:(m + 1) * NS], shift[:, m * P:(m + 1) * P], ident[0:NS, 0:NS])
                for m in range(ST):
                    pe.transpose(ps[:, 2, m * 16:(m + 1) * 16], scb[:, m * P:(m + 1) * P], ident[0:16, 0:16])
                for m in range(8):
                    pe.transpose(ps[:, 3, m * 24:(m + 1) * 24], conv[:, m * P:(m + 1) * P], ident[0:24, 0:24])
                for m in range(4):
                    mm = pe.matmul(ps[:, 4, m:m + 1], env.const("pair8")[0:8, m * P:(m + 1) * P], env.heads[:, 2:3],
                                   start=True, stop=True)
                mm.then_inc(turned, 1)

            @block.vector
            def _(dve):
                dve.wait_ge(turned, 1)
                dve.tensor_copy(env.cols[:, 0:P + nb], ps[:, 0, 0:P + nb]).then_inc(copied, 1)
                dve.tensor_copy(env.shift[:], ps[:, 1, 0:XT * NS].rearrange("p (m b) -> p m b", b=NS)).then_inc(copied, 1)
                dve.tensor_copy(env.scb[:], ps[:, 2, 0:64].rearrange("p (m j) -> p m j", m=ST)).then_inc(copied, 1)
                dve.tensor_copy(env.conv[:], ps[:, 3, 0:192].rearrange("p (m j) -> p m j", m=8)).then_inc(copied, 1)
                dve.tensor_copy(env.dcol[:], ps[:, 4, 0:4]).then_inc(copied, 1)
                dve.wait_ge(copied, 5)
                dve.tensor_scalar(env.omu[:], env.col("rwkv_mu", 0, XT), -1.0, 1.0, ALU.mult, ALU.add).then_inc(derived, 1)
                dve.tensor_scalar(env.oka[:], env.col("rwkv_k_a", 0, RT), -1.0, 1.0, ALU.mult, ALU.add).then_inc(derived, 1)
                dve.wait_ge(a_done, 1)
                dve.tensor_scalar(env.heads[:, 4:5], env.heads[:, 3:4], -1.0, None, ALU.mult).then_inc(derived, 1)


def final_stage(nc, env, d):
    with Stage(nc, "fin") as st:
        sq, rt, rs = st.sb("fin_sq", [P, KT, N]), st.sb("fin_root", [P, N]), st.sb("fin_rs", [P, N])
        rows, gain = st.sb("gain_rows", [KT, P]), st.sb("gain_cols", [P, KT])
        yp, ys = st.sb("y_rows", [P, 2, D]), st.sb("y_sample_rows", [NS, D])
        squared, summed, rooted, gain_in = st.sem("squared"), st.sem("summed"), st.sem("rooted"), st.sem("gain_in")
        gain_turned, ready, scaled = st.sem("gain_turned"), st.sem("rs_ready"), st.sem("y_scaled")
        turned, copied, stored = st.sem("y_turned"), st.sem("y_copied"), st.sem("y_stored")
        ps = env.ps
        with nc.Block() as block:
            @block.sync
            def _(sp):
                sp.dma_start(rows[:], d["norm_final"].rearrange("(r f) -> r f", f=P)).then_inc(gain_in, 16)
                sp.wait_ge(copied, KT)
                sp.dma_start(d["y_prompt"][0].rearrange("(a p) f -> p a f", p=P), yp[:]).then_inc(stored, 16)
                sp.dma_start(d["y_sample"].rearrange("b a f -> (b a) f"), ys[:]).then_inc(stored, 16)
                sp.wait_ge(stored, 32)

            @block.scalar
            def _(act):
                act.activation(sq[:], env.x[:], ACT.Square).then_inc(squared, 1)
                act.wait_ge(summed, 1)
                act.activation(rt[:], ps[:, 6, 0:N], ACT.Sqrt, bias=env.eps[:, 0:1]).then_inc(rooted, 1)

            @block.tensor
            def _(pe):
                ident = env.const("ident")
                pe.wait_ge(gain_in, 16)
                pe.transpose(ps[:, 7, 0:KT], rows[:], ident[0:KT, 0:KT]).then_inc(gain_turned, 1)
                pe.wait_ge(squared, 1)
                for k in range(KT):
                    mm = pe.matmul(ps[:, 6, 0:N], env.const("mean"), sq[:, k], start=k == 0, stop=k == KT - 1)
                mm.then_inc(summed, 1)
                for k in range(KT):
                    pe.wait_ge(scaled, k + 1)
                    if k >= 2:
                        pe.wait_ge(copied, k - 1)
                    b = 3 * (k % 2)
                    for a in range(2):
                        pe.transpose(ps[:, b + a, 0:P], sq[:, k, a * P:(a + 1) * P], ident)
                    pe.transpose(ps[0:NS, b + 2, 0:P], sq[:, k, T:N], ident).then_inc(turned, 1)

            @block.vector
            def _(dve):
                dve.wait_ge(gain_turned, 1)
                dve.tensor_copy(gain[:], ps[:, 7, 0:KT]).then_inc(ready, 1)
                dve.wait_ge(rooted, 1)
                dve.reciprocal(rs[:], rt[:]).then_inc(ready, 1)
                dve.wait_ge(ready, 2)
                for k in range(KT):
                    dve.scalar_tensor_tensor(out=sq[:, k], in0=env.x[:, k], scalar=gain[:, k:k + 1], in1=rs[:],
                                             op0=ALU.mult, op1=ALU.mult).then_inc(scaled, 1)
                for k in range(KT):
                    dve.wait_ge(turned, k + 1)
                    b = 3 * (k % 2)
                    dve.tensor_copy(yp[:, :, k * P:(k + 1) * P], ps[:, b:b + 2, 0:P])
                    dve.tensor_copy(ys[:, k * P:(k + 1) * P], ps[0:NS, b + 2, 0:P]).then_inc(copied, 1)


def projection_stage(nc, env, mix, layer, d):
    with Stage(nc, "proj") as st:
        w = d["w_in"][layer].rearrange("(k p) c -> p k c", p=P)
        pieces, halves, tiles = [], [], []

        def add(c0, widths, kinds):
            for i, (wd, kind) in enumerate(zip(widths, kinds)):
                halves.append((len(pieces), sum(widths[:i]), wd, KT))
                tiles.append(kind)

        for m in range(0, XT - 1, 2):
            add(m * P, (P, P), (("rwkv", m), ("rwkv", m + 1)))
            pieces.append([((KT, 0, 2 * P), w[:, :, m * P:(m + 2) * P])])
        add(0, (32, 8), (("rwkv", XT - 1), ("dt", 0)))
        pieces.append([((KT, 0, 32), w[:, :, RWKV_PROJ - 32:RWKV_PROJ]), ((KT, 32, 8), w[:, :, IN_COLS - 8:IN_COLS])])
        for m in range(0, 24, 2):
            c0 = RWKV_PROJ + m * P
            kind = "sc" if m < 12 else ("z" if m < 16 else "xbc")
            add(c0, (P, P), ((kind, m), (kind, m + 1)))
            pieces.append([((KT, 0, 2 * P), w[:, :, c0:c0 + 2 * P])])
        ws = Stream(st, KT, pieces, halves)
        h_hi, h_lo, act_square, pe_mean, act_root, dve_scale, act_hi, dve_lo, pe_ready = normed_input(
            st, env, "norm_mix", 7)
        prev = st.sb("prev", [P, 2, 1 + N])
        shift_mu = st.sb("shift_mu", [P, XT, NS])
        zeroed, prev_in, act_read = st.sem("zeroed"), st.sem("prev_in"), st.sem("act_read")
        last_in, shifted, mu_done = st.sem("last_in"), st.sem("shifted"), st.sem("shift_mu_done")
        H = len(halves)
        ps = env.ps

        with nc.Block() as block:
            @block.sync
            def _(sp):
                for p in range(len(pieces)):
                    ws.load(sp, p)

            @block.gpsimd
            def _(pool):
                pool.memset(prev[:, :, 0:1], 0.0).then_inc(zeroed, 1)
                pool.memset(mix.xs[:, XT - 1], 0.0).then_inc(zeroed, 1)
                pool.memset(mix.last[:, XT - 1], 0.0).then_inc(zeroed, 1)
                pool.memset(mix.xbc[:, :, 0:3], 0.0).then_inc(zeroed, 1)
                for n in range(0, H, 2):
                    ws.split_lo(pool, n)

            @block.scalar
            def _(act):
                act_square(act)
                for n in range(4):
                    ws.split_hi(act, n)
                act_root(act)
                act_hi(act)
                act.wait_ge(zeroed, 4)
                for n, (kind, m) in enumerate(tiles):
                    ws.split_hi(act, n + 4)
                    act.wait_ge(ws.used, n + 1)
                    bank, r = ps[:, n % 4, 0:N], halves[n][2]
                    if kind == "rwkv":
                        if m >= 2:
                            act.wait_ge(shifted, m - 1)
                            act.wait_ge(last_in, m - 1)
                        act.activation(prev[0:r, m % 2, 1:1 + N], bank[0:r], ACT.Copy).then_inc(prev_in, 1)
                        act.activation(mix.xs[0:r, m], bank[0:r], ACT.Copy,
                                       scale=env.omu[0:r, m:m + 1]).then_inc(act_read, 1)
                    else:
                        dst = {"dt": lambda: mix.dt[:], "sc": lambda: mix.sc[:, m], "z": lambda: mix.z[:, m - 12],
                               "xbc": lambda: mix.xbc[:, m - 16, 3:3 + N]}[kind]()
                        act.activation(dst, bank[0:r], ACT.Copy).then_inc(act_read, 1)

            @block.vector
            def _(dve):
                ws.split_lo(dve, 1)
                ws.split_lo(dve, 3)
                dve_scale(dve)
                dve_lo(dve)
                dve.wait_ge(zeroed, 4)
                for n, (kind, m) in enumerate(tiles):
                    r = halves[n][2]
                    if kind == "rwkv":
                        dve.wait_ge(prev_in, m + 1)
                        dve.tensor_copy(mix.last[0:r, m], prev[0:r, m % 2, T:T + 9]).then_inc(last_in, 1)
                        dve.wait_ge(act_read, n + 1)
                        dve.scalar_tensor_tensor(out=mix.xs[0:r, m, 0:T], in0=prev[0:r, m % 2, 0:T],
                                                 scalar=env.col("rwkv_mu", m)[0:r], in1=mix.xs[0:r, m, 0:T],
                                                 op0=ALU.mult, op1=ALU.add).then_inc(shifted, 1)
                    if n % 2 == 0:
                        ws.split_lo(dve, n + 5)
                mu = env.col("rwkv_mu", 0, XT).unsqueeze(2).to_broadcast([P, XT, NS])
                dve.tensor_tensor(shift_mu[:], env.shift[:], mu, ALU.mult).then_inc(mu_done, 1)
                dve.wait_ge(mu_done, 1)
                dve.wait_ge(shifted, XT)
                dve.tensor_tensor(mix.xs[:, :, T:N], mix.xs[:, :, T:N], shift_mu[:], ALU.add).then_inc(shifted, 1)

            @block.tensor
            def _(pe):
                pe_mean(pe)
                pe_ready(pe)
                for n in range(H):
                    if n >= 4:
                        pe.wait_ge(act_read, n - 3)
                    ws.product(pe, n, ps[0:halves[n][2], n % 4, 0:N], h_hi, h_lo)


def causal_conv(dve, st, name, dst, src, state, taps, m, width, after):
    s = st.s(name)
    base = after
    for j in range(width):
        last_of_samples = src[:, width - 1 + T:width - 1 + N]
        smp = state[:, :, j] if j < width - 1 else last_of_samples
        for out, x in ((dst[:, 0:T], src[:, j:j + T]), (dst[:, T:N], smp)):
            if j == 0:
                dve.tensor_scalar(out, x, taps(j), None, ALU.mult).then_inc(s, 1)
            else:
                dve.scalar_tensor_tensor(out=out, in0=x, scalar=taps(j), in1=out, op0=ALU.mult,
                                         op1=ALU.add).then_inc(s, 1)
        base += 2
        if j < width - 1:
            dve.wait_ge(s, base)
    return base


def short_mixers_stage(nc, env, mix, layer, d):
    with Stage(nc, "ssm") as st:
        s, ps = st.s, env.ps
        ident, ones, mean = env.const("ident"), env.const("ones"), env.const("mean")
        neg, row8, pair8 = env.const("neg"), env.const("row8"), env.const("pair8")
        u = st.sb("gated", [P, ST, 2 + N])
        acc = st.sb("sc_conv", [P, ST, N])
        sq = st.sb("squares", [P, ST, N])
        root, rs = st.sb("root", [P, 2, N]), st.sb("rs", [P, 2, N])
        xa = st.sb("xbc_conv", [P, 8, N])
        dv, da = st.sb("dt_abs", [8, N]), st.sb("dt_a", [8, N])
        one_row, cum = st.sb("one_row", [8, T]), st.sb("cum", [8, T])
        das = st.sb("dt_sample", [8, 2 * NS])
        tok = st.sb("tok_cum_dt", [P, 4, 8])
        lastc, dend = st.sb("cum_last", [P, 8]), st.sb("decay_end", [P, 2, 8])
        xdt, xde = st.sb("xdt", [P, 2, 8, HS]), st.sb("xdt_end", [P, 2, 8, HS])
        btok = st.sb("b_tok", [P, 2, 2, P])
        seg, score = st.sb("segments", [P, 2, 384]), st.sb("scores", [P, 2, 384])
        hst = st.sb("sample_state", [P, 4, NS, P])
        outer = st.sb("outer", [P, NS, P])
        diag = st.sb("diag", [P, NS, P])
        spread, xs_dt = st.sb("spread", [P, 4, 2 * NS]), st.sb("sample_xdt", [P, 4, NS])
        ym, hfin = st.sb("y_ssm", [P, 4, N]), st.sb("p_state", [P, 4, P])
        scn, cvn = st.sb("sc_new", [P, ST, 18]), st.sb("conv_new", [P, 8, 27])
        sc_rows, cv_rows = st.sb("sc_new_rows", [18, SC]), st.sb("conv_new_rows", [27, D])
        sh_rows = st.sb("shift_new_rows", [9, XT * P])
        hs_in = d["state_ssm"][layer].rearrange("b (m h) p n -> m (h p) b n", h=2)
        hs_out = d["s_ssm"][layer].rearrange("b (m h) p n -> m (h p) b n", h=2)
        stores = []

        with nc.Block() as block:
            @block.sync
            def _(sp):
                for m in range(4):
                    sp.dma_start(hst[:, m], hs_in[m]).then_inc(s("state_in"), 16)

                def store(dst, src):
                    sp.dma_start(dst, src).then_inc(s("stored"), 16)
                    stores.append(1)

                sp.wait_ge(s("hfin_done"), 1)
                store(d["p_ssm"][layer, 0].rearrange("(m h) p n -> (h p) m n", h=2), hfin[:])
                for m in range(4):
                    sp.wait_ge(s("hst_done"), m + 1)
                    store(hs_out[m], hst[:, m])
                sp.wait_ge(s("rows_done"), 3)
                store(d["p_sc"][layer, 0], sc_rows[0:2, :])
                store(d["s_sc"][layer].rearrange("b j f -> (b j) f"), sc_rows[2:18, :])
                store(d["p_conv"][layer, 0], cv_rows[0:3, :])
                store(d["s_conv"][layer].rearrange("b j f -> (b j) f"), cv_rows[3:27, :])
                sp.wait_ge(s("shift_rows_done"), 7)
                store(d["p_shift"][layer], sh_rows[0:1, 0:RWKV_PROJ])
                store(d["s_shift"][layer], sh_rows[1:9, 0:RWKV_PROJ])
                sp.wait_ge(s("stored"), 16 * len(stores))

            @block.gpsimd
            def _(pool):
                pool.memset(u[:, :, 0:2], 0.0).then_inc(s("u_zero"), 1)
                pool.memset(one_row[:], 1.0).then_inc(s("one_row"), 1)
                pool.wait_ge(s("spread_in"), 1)
                pool.wait_ge(s("state_in"), 64)
                for m in range(4):
                    dec = spread[:, m, 0:NS].unsqueeze(2).to_broadcast([P, NS, P])
                    pool.tensor_tensor(hst[:, m], hst[:, m], dec, ALU.mult).then_inc(s("hst_decayed"), 1)

            @block.scalar
            def _(act):
                for i in range(8):
                    act.wait_ge(s("xconv"), 8 * (i + 1))
                    act.activation(xa[:, i], xa[:, i], ACT.Silu, bias=env.col("ssm_conv_b", i)).then_inc(s("xa_done"), 1)
                act.activation(mix.z[:], mix.z[:], ACT.Silu).then_inc(s("z_silu"), 1)
                act.wait_ge(s("dt_step"), 2)
                act.activation(da[:], dv[:], ACT.Exp, scale=-1.0).then_inc(s("dt_act"), 1)
                act.wait_ge(s("dt_act"), 1)
                act.activation(dv[:], da[:], ACT.Ln, bias=env.eps[0:8, 2:3]).then_inc(s("dt_act"), 1)
                act.wait_ge(s("dt_step"), 4)
                act.activation(das[:, 0:NS], da[:, T:N], ACT.Exp).then_inc(s("das_exp"), 1)
                for h in range(8):
                    act.wait_ge(s("seg_done"), 2 * h + 2)
                    act.activation(seg[:, h % 2], seg[:, h % 2], ACT.Exp).then_inc(s("seg_exp"), 1)
                act.wait_ge(s("dend_sub"), 1)
                act.activation(dend[:], dend[:], ACT.Exp).then_inc(s("dend_exp"), 1)
                act.wait_ge(s("hfin_ps"), 1)
                act.activation(hfin[:], ps[:, 3, :].rearrange("p (m n) -> p m n", m=4), ACT.Copy).then_inc(s("hfin_done"), 1)
                act.wait_ge(s("sc_gated"), 1)
                act.activation(sq[:], acc[:], ACT.Square).then_inc(s("sc_sq"), 1)
                act.wait_ge(s("sc_ms"), 1)
                act.activation(root[:, 0], ps[:, 0, 0:N], ACT.Sqrt, bias=env.eps[:, 0:1], scale=D / SC).then_inc(s("sc_root"), 1)
                for i in range(ST):
                    act.wait_ge(s("sc_scaled"), i + 1)
                    act.activation(mix.ys_hi[:, i], acc[:, i], ACT.Copy).then_inc(s("sc_hi"), 1)
                act.wait_ge(s("y_gated"), 1)
                act.wait_ge(s("sc_ms"), 1)
                act.activation(sq[:], ym[:], ACT.Square).then_inc(s("ssm_sq"), 1)
                for g in range(2):
                    act.wait_ge(s("ssm_ms"), g + 1)
                    act.wait_ge(s("sc_inv"), 1)
                    act.activation(root[:, g], ps[:, 4 + g, 0:N], ACT.Sqrt, bias=env.eps[:, 0:1],
                                   scale=D / 256).then_inc(s("ssm_root"), 1)
                for m in range(4):
                    act.wait_ge(s("ssm_scaled"), m + 1)
                    act.activation(mix.ys_hi[:, ST + m], ym[:, m], ACT.Copy).then_inc(s("ssm_hi"), 1)

            @block.vector
            def _(dve):
                n = 0
                for i in range(8):
                    n = causal_conv(dve, st, "xconv", xa[:, i], mix.xbc[:, i],
                                    env.conv[:, i].rearrange("p (b j) -> p b j", j=3),
                                    lambda j: env.col("ssm_conv_w", 8 * j + i), i, 4, n)
                dve.tensor_scalar(mix.dt[:], mix.dt[:], env.heads[:, 0:1], None, ALU.add).then_inc(s("dt_step"), 1)
                dve.wait_ge(s("dt_step"), 1)
                dve.scalar_tensor_tensor(out=dv[:], in0=mix.dt[:], scalar=-1.0, in1=mix.dt[:], op0=ALU.mult,
                                         op1=ALU.max).then_inc(s("dt_step"), 1)
                dve.wait_ge(s("dt_act"), 2)
                dve.scalar_tensor_tensor(out=mix.dt[:], in0=mix.dt[:], scalar=0.0, in1=dv[:], op0=ALU.max,
                                         op1=ALU.add).then_inc(s("dt_step"), 1)
                dve.wait_ge(s("dt_step"), 3)
                dve.tensor_scalar(da[:], mix.dt[:], env.heads[:, 4:5], None, ALU.mult).then_inc(s("dt_step"), 1)
                dve.wait_ge(s("dt_step"), 4)
                dve.wait_ge(s("one_row"), 1)
                dve.tensor_tensor_scan(cum[:], one_row[:], da[:, 0:T], 0.0, ALU.mult, ALU.add).then_inc(s("cum_done"), 1)
                dve.tensor_copy(das[:, NS:2 * NS], mix.dt[:, T:N]).then_inc(s("das_dt"), 1)
                dve.wait_ge(s("tok_ps"), 1)
                dve.tensor_copy(tok[:], ps[:, 4, 0:32].rearrange("p (a h) -> p a h", a=4)).then_inc(s("tok_in"), 1)
                dve.wait_ge(s("tok_in"), 1)
                dve.wait_ge(s("xtok_ps"), 1)
                for c in range(2):
                    dve.tensor_tensor(xdt[:, c], ps[:, 1 + c, :].rearrange("p (h e) -> p h e", h=8),
                                      tok[:, 2 + c].unsqueeze(2).to_broadcast([P, 8, HS]), ALU.mult).then_inc(s("xdt_done"), 1)
                dve.tensor_copy(btok[:].rearrange("p c g n -> p (c g n)"), ps[:, 3, :]).then_inc(s("btok_done"), 1)
                for h in range(8):
                    g, b = h // 4, 7 if h % 2 else 0
                    dve.wait_ge(s("row_ps"), h + 1)
                    dve.scalar_tensor_tensor(out=seg[:, h % 2, 0:T], in0=ps[:, b, 0:T], scalar=tok[:, 0, h:h + 1],
                                             in1=neg[:, 0:T], op0=ALU.subtract, op1=ALU.add).then_inc(s("seg_done"), 1)
                    dve.scalar_tensor_tensor(out=seg[:, h % 2, T:384], in0=ps[:, b, P:T], scalar=tok[:, 1, h:h + 1],
                                             in1=neg[:, T:384], op0=ALU.subtract, op1=ALU.add).then_inc(s("seg_done"), 1)
                    dve.tensor_copy(lastc[:, h:h + 1], ps[:, b, T - 1:T]).then_inc(s("row_read"), 1)
                    dve.wait_ge(s("seg_exp"), h + 1)
                    if h >= 2:
                        dve.wait_ge(s("y_ps"), h - 1)
                    if h == 0:
                        dve.wait_ge(s("g_ps"), 1)
                    dve.tensor_tensor(score[:, h % 2], ps[:, 5 + g, 0:384], seg[:, h % 2], ALU.mult).then_inc(s("score_done"), 1)
                dve.wait_ge(s("row_read"), 8)
                dve.tensor_tensor(dend[:], lastc[:].unsqueeze(1).to_broadcast([P, 2, 8]), tok[:, 0:2],
                                  ALU.subtract).then_inc(s("dend_sub"), 1)
                dve.wait_ge(s("dend_exp"), 1)
                dve.wait_ge(s("xdt_done"), 2)
                for c in range(2):
                    dve.tensor_tensor(xde[:, c], xdt[:, c], dend[:, c].unsqueeze(2).to_broadcast([P, 8, HS]),
                                      ALU.mult).then_inc(s("xde_done"), 1)
                for m in range(4):
                    dve.wait_ge(s("y_ps"), 4 * (m // 2) + 4)
                    dve.scalar_tensor_tensor(out=ym[:, m, 0:T], in0=xa[:, m, 0:T], scalar=env.dcol[:, m:m + 1],
                                             in1=ps[:, 1 + m // 2, (m % 2) * T:(m % 2) * T + T], op0=ALU.mult,
                                             op1=ALU.add).then_inc(s("y_done"), 1)
                dve.wait_ge(s("spread_ps"), 1)
                dve.tensor_copy(spread[:], ps[:, 4, 0:64].rearrange("p (m e) -> p m e", m=4)).then_inc(s("spread_in"), 1)
                dve.wait_ge(s("spread_in"), 1)
                dve.tensor_tensor(xs_dt[:], xa[:, 0:4, T:N], spread[:, :, NS:2 * NS], ALU.mult).then_inc(s("xs_dt"), 1)
                dve.wait_ge(s("xs_dt"), 1)
                for v in range(4):
                    g, bc = v // 2, v % 2
                    if v:
                        dve.wait_ge(s("bc_ps"), v)
                    dve.tensor_tensor(diag[:], ident.unsqueeze(1).to_broadcast([P, NS, P]),
                                      xa[:, 4 + 2 * bc + g, T:N].unsqueeze(2).to_broadcast([P, NS, P]),
                                      ALU.mult).then_inc(s("diag_done"), 1)
                    if bc == 0:
                        continue
                    dve.wait_ge(s("bc_ps"), 2 * g + 2)
                    for m in (2 * g, 2 * g + 1):
                        k = 3 * m
                        brow = ps[:, 5:7, :].rearrange("p a (b n) -> p (a b) n", n=P)
                        dve.wait_ge(s("smp"), k)
                        dve.tensor_tensor(outer[:], brow, xs_dt[:, m].unsqueeze(2).to_broadcast([P, NS, P]),
                                          ALU.mult).then_inc(s("smp"), 1)
                        dve.wait_ge(s("smp"), k + 1)
                        dve.wait_ge(s("hst_decayed"), m + 1)
                        dve.tensor_tensor(hst[:, m], hst[:, m], outer[:], ALU.add).then_inc(s("hst_done"), 1)
                        dve.wait_ge(s("hst_done"), m + 1)
                        for half in range(2):
                            crow = ps[:, 7 if half else 0, :].rearrange("p (b n) -> p b n", n=P)
                            dve.tensor_tensor(outer[:, 4 * half:4 * half + 4], hst[:, m, 4 * half:4 * half + 4], crow,
                                              ALU.mult).then_inc(s("smp_c"), 1)
                        dve.wait_ge(s("smp_c"), 2 * m + 2)
                        dve.tensor_reduce(ym[:, m, T:N], outer[:], AX.X, ALU.add).then_inc(s("smp"), 1)
                        dve.wait_ge(s("smp"), k + 2)
                        dve.scalar_tensor_tensor(out=ym[:, m, T:N], in0=xa[:, m, T:N], scalar=env.dcol[:, m:m + 1],
                                                 in1=ym[:, m, T:N], op0=ALU.mult, op1=ALU.add).then_inc(s("smp"), 1)
                dve.wait_ge(s("smp"), 12)
                dve.wait_ge(s("y_done"), 4)
                dve.wait_ge(s("z_silu"), 1)
                dve.tensor_tensor(ym[:], ym[:], mix.z[:], ALU.mult).then_inc(s("y_gated"), 1)
                dve.wait_ge(s("u_zero"), 1)
                dve.tensor_tensor(u[:, :, 2:2 + N], mix.sc[:, 4:8], mix.sc[:, 8:12], ALU.mult).then_inc(s("u_done"), 1)
                dve.wait_ge(s("u_done"), 1)
                n = 0
                for i in range(ST):
                    n = causal_conv(dve, st, "uconv", acc[:, i], u[:, i], env.scb[:, i].rearrange("p (b j) -> p b j", j=2),
                                    lambda j: env.col("sc_conv_w", 4 * j + i), i, 3, n)
                dve.wait_ge(s("uconv"), n)
                dve.tensor_tensor(acc[:], acc[:], mix.sc[:, 0:4], ALU.mult).then_inc(s("sc_gated"), 1)
                scb = env.scb[:].rearrange("p m (b j) -> p m b j", j=2)
                cvb = env.conv[:].rearrange("p m (b j) -> p m b j", j=3)
                scw = scn[:, :, 2:18].rearrange("p m (b j) -> p m b j", j=2)
                cvw = cvn[:, :, 3:27].rearrange("p m (b j) -> p m b j", j=3)
                dve.tensor_copy(scn[:, :, 0:2], u[:, :, T:T + 2]).then_inc(s("new_in"), 1)
                dve.tensor_copy(scw[:, :, :, 0], scb[:, :, :, 1]).then_inc(s("new_in"), 1)
                dve.tensor_copy(scw[:, :, :, 1], u[:, :, T + 2:N + 2]).then_inc(s("new_in"), 1)
                dve.tensor_copy(cvn[:, :, 0:3], mix.xbc[:, :, T:T + 3]).then_inc(s("new_in"), 1)
                dve.tensor_copy(cvw[:, :, :, 0], cvb[:, :, :, 1]).then_inc(s("new_in"), 1)
                dve.tensor_copy(cvw[:, :, :, 1], cvb[:, :, :, 2]).then_inc(s("new_in"), 1)
                dve.tensor_copy(cvw[:, :, :, 2], mix.xbc[:, :, T + 3:N + 3]).then_inc(s("new_in"), 1)
                dve.wait_ge(s("sc_root"), 1)
                dve.reciprocal(rs[:, 0], root[:, 0]).then_inc(s("sc_inv"), 1)
                dve.wait_ge(s("sc_inv"), 1)
                dve.wait_ge(s("sc_gated"), 1)
                for i in range(ST):
                    dve.scalar_tensor_tensor(out=acc[:, i], in0=acc[:, i], scalar=env.col("sc_norm", i), in1=rs[:, 0],
                                             op0=ALU.mult, op1=ALU.mult).then_inc(s("sc_scaled"), 1)
                for i in range(ST):
                    dve.wait_ge(s("sc_hi"), i + 1)
                    dve.tensor_tensor(mix.ys_lo[:, i], acc[:, i], mix.ys_hi[:, i].bitcast(F32),
                                      ALU.subtract).then_inc(s("sc_lo"), 1)
                dve.wait_ge(s("sc_scaled"), ST)
                for g in range(2):
                    dve.wait_ge(s("ssm_root"), g + 1)
                    dve.reciprocal(rs[:, g], root[:, g]).then_inc(s("ssm_inv"), 1)
                    dve.wait_ge(s("ssm_inv"), g + 1)
                    for m in (2 * g, 2 * g + 1):
                        dve.scalar_tensor_tensor(out=ym[:, m], in0=ym[:, m], scalar=env.col("ssm_norm", m), in1=rs[:, g],
                                                 op0=ALU.mult, op1=ALU.mult).then_inc(s("ssm_scaled"), 1)
                for m in range(4):
                    dve.wait_ge(s("ssm_hi"), m + 1)
                    dve.tensor_tensor(mix.ys_lo[:, ST + m], ym[:, m], mix.ys_hi[:, ST + m].bitcast(F32),
                                      ALU.subtract).then_inc(s("ssm_lo"), 1)
                dve.wait_ge(s("new_ps"), 1)
                dve.tensor_copy(sc_rows[:], ps[0:18, 1, :]).then_inc(s("rows_done"), 1)
                for a in range(2):
                    dve.tensor_copy(cv_rows[:, a * 512:(a + 1) * 512], ps[0:27, 2 + a, :]).then_inc(s("rows_done"), 1)
                for q in range(7):
                    w = min(4, XT - 4 * q) * P
                    dve.wait_ge(s("shift_ps"), q + 1)
                    dve.tensor_copy(sh_rows[:, 512 * q:512 * q + w], ps[0:9, 4 + q % 4, 0:w]).then_inc(s("shift_rows_done"), 1)

            @block.tensor
            def _(pe):
                pe.wait_ge(s("cum_done"), 1)
                for c in range(2):
                    pe.transpose(ps[:, 4, 8 * c:8 * c + 8], cum[:, c * P:(c + 1) * P], ident[0:8, 0:8])
                    mm = pe.transpose(ps[:, 4, 16 + 8 * c:24 + 8 * c], mix.dt[:, c * P:(c + 1) * P], ident[0:8, 0:8])
                mm.then_inc(s("tok_ps"), 1)
                pe.wait_ge(s("xa_done"), 8)
                for c in range(2):
                    for m in range(4):
                        pe.transpose(ps[:, 1 + c, m * P:(m + 1) * P], xa[:, m, c * P:(c + 1) * P], ident)
                    for g in range(2):
                        mm = pe.transpose(ps[:, 3, (2 * c + g) * P:(2 * c + g + 1) * P], xa[:, 4 + g, c * P:(c + 1) * P], ident)
                mm.then_inc(s("xtok_ps"), 1)
                for g in range(2):
                    pe.matmul(ps[:, 5 + g, 0:T], xa[:, 4 + g, 0:P], xa[:, 6 + g, 0:T], start=True, stop=True)
                    mm = pe.matmul(ps[:, 5 + g, T:384], xa[:, 4 + g, P:T], xa[:, 6 + g, P:T], start=True, stop=True)
                mm.then_inc(s("g_ps"), 1)

                def row(h):
                    if h >= 2:
                        pe.wait_ge(s("row_read"), h - 1)
                        pe.wait_ge(s("seg_done"), 2 * (h - 1))
                    pe.matmul(ps[:, 7 if h % 2 else 0, 0:T], row8[0:8, h * P:(h + 1) * P], cum[:], start=True,
                              stop=True).then_inc(s("row_ps"), 1)

                row(0)
                row(1)
                pe.wait_ge(s("xdt_done"), 2)
                for h in range(8):
                    if h + 2 < 8:
                        row(h + 2)
                    pe.wait_ge(s("score_done"), h + 1)
                    m, q = h // 2, (h % 2) * HS
                    y = ps[q:q + HS, 1 + m // 2, (m % 2) * T:(m % 2) * T + T]
                    pe.matmul(y, xdt[:, 0, h], score[:, h % 2, 0:T], start=True, stop=False, skip_group_check=True)
                    pe.matmul(y[:, P:T], xdt[:, 1, h], score[:, h % 2, T:384], start=False, stop=True,
                              skip_group_check=True).then_inc(s("y_ps"), 1)
                pe.wait_ge(s("das_exp"), 1)
                pe.wait_ge(s("das_dt"), 1)
                pe.wait_ge(s("tok_in"), 1)
                for m in range(4):
                    mm = pe.matmul(ps[:, 4, 16 * m:16 * m + 16], pair8[0:8, m * P:(m + 1) * P], das[:], start=True, stop=True)
                mm.then_inc(s("spread_ps"), 1)
                pe.wait_ge(s("xde_done"), 2)
                pe.wait_ge(s("btok_done"), 1)
                for m in range(4):
                    for c in range(2):
                        mm = pe.matmul(ps[:, 3, m * P:(m + 1) * P], xde[:, c, 2 * m:2 * m + 2].rearrange("p h e -> p (h e)"),
                                       btok[:, c, m // 2], start=c == 0, stop=c == 1)
                mm.then_inc(s("hfin_ps"), 1)
                for v in range(4):
                    pe.wait_ge(s("diag_done"), v + 1)
                    if v == 0:
                        pe.wait_ge(s("score_done"), 8)
                        pe.wait_ge(s("row_read"), 8)
                    if v == 2:
                        pe.wait_ge(s("smp"), 6)
                    for half in range(2):
                        b = 5 + half if v % 2 == 0 else (7 if half else 0)
                        mm = pe.matmul(ps[:, b, :], ones, diag[:, 4 * half:4 * half + 4].rearrange("p b n -> p (b n)"),
                                       start=True, stop=True)
                    mm.then_inc(s("bc_ps"), 1)
                pe.wait_ge(s("sc_sq"), 1)
                pe.wait_ge(s("smp"), 12)
                for i in range(ST):
                    mm = pe.matmul(ps[:, 0, 0:N], mean, sq[:, i], start=i == 0, stop=i == ST - 1)
                mm.then_inc(s("sc_ms"), 1)
                pe.wait_ge(s("ssm_sq"), 1)
                pe.wait_ge(s("spread_in"), 1)
                for g in range(2):
                    for i in range(2):
                        mm = pe.matmul(ps[:, 4 + g, 0:N], mean, sq[:, 2 * g + i], start=i == 0, stop=i == 1)
                    mm.then_inc(s("ssm_ms"), 1)
                pe.wait_ge(s("new_in"), 7)
                pe.wait_ge(s("y_done"), 4)
                pe.wait_ge(s("hfin_done"), 1)
                for i in range(ST):
                    pe.transpose(ps[0:18, 1, i * P:(i + 1) * P], scn[:, i], ident)
                for i in range(8):
                    mm = pe.transpose(ps[0:27, 2 + i // 4, (i % 4) * P:(i % 4 + 1) * P], cvn[:, i], ident)
                mm.then_inc(s("new_ps"), 1)
                pe.wait_ge(s("ssm_root"), 2)
                for q in range(7):
                    if q >= 4:
                        pe.wait_ge(s("shift_rows_done"), q - 3)
                    for i in range(4 * q, min(4 * q + 4, XT)):
                        mm = pe.transpose(ps[0:9, 4 + q % 4, (i % 4) * P:(i % 4 + 1) * P], mix.last[:, i], ident)
                    mm.then_inc(s("shift_ps"), 1)


def output_stage(nc, env, mix, layer, d):
    with Stage(nc, "out") as st:
        w = d["w_out"][layer].rearrange("(k p) c -> p k c", p=P)
        pieces, halves = [], []
        for c in range(KT // 2):
            for kh in range(2):
                halves += [(len(pieces), off * P, P, KT) for off in range(2)]
                pieces.append([((KT, 0, 2 * P), w[:, kh * KT:(kh + 1) * KT, c * 2 * P:(c + 1) * 2 * P])])
        ws = Stream(st, KT, pieces, halves)
        x_added = st.sem("x_added")
        with nc.Block() as block:
            @block.sync
            def _(sp):
                for p in range(len(pieces)):
                    ws.load(sp, p)

            @block.gpsimd
            def _(pool):
                for n in range(0, len(halves), 2):
                    ws.split_lo(pool, n)

            @block.scalar
            def _(act):
                for n in range(len(halves)):
                    ws.split_hi(act, n)

            @block.vector
            def _(dve):
                ws.split_lo(dve, 1)
                for mt in range(KT):
                    n = 4 * (mt // 2) + 2 + mt % 2
                    if mt % 2 == 0:
                        ws.split_lo(dve, n + 1)
                        ws.split_lo(dve, n + 3)
                    dve.wait_ge(ws.used, n + 1)
                    dve.tensor_tensor(env.x[:, mt], env.ps[:, mt % 4, 0:N], env.x[:, mt], ALU.add).then_inc(x_added, 1)

            @block.tensor
            def _(pe):
                for n in range(len(halves)):
                    c, kh, off = n // 4, n // 2 % 2, n % 2
                    mt = 2 * c + off
                    if mt >= 4 and kh == 0:
                        pe.wait_ge(x_added, mt - 3)
                    ws.product(pe, n, env.ps[:, mt % 4, 0:N], (mix.yr_hi, mix.ys_hi)[kh], (mix.yr_lo, mix.ys_lo)[kh],
                               start=kh == 0, stop=kh == 1)


class Mix:
    pass


def mix_stages(nc, env, layer, d):
    mix = Mix()

    def make(ctx, name, shape, dt=F32):
        return ctx.enter_context(nc.sbuf_tensor(name, shape, dt))

    with ExitStack() as ctx:
        mix.xs = make(ctx, "xs", [P, XT, N])
        mix.last = make(ctx, "last_rows", [P, XT, 9])
        mix.ys_hi = make(ctx, "y_short_hi", [P, MT - RT, N], F32R)
        mix.ys_lo = make(ctx, "y_short_lo", [P, MT - RT, N], F32R)
        with ExitStack() as short:
            mix.sc = make(short, "sc_proj", [P, 12, N])
            mix.z = make(short, "z", [P, 4, N])
            mix.xbc = make(short, "xbc", [P, 8, 3 + N])
            mix.dt = make(short, "dt", [8, N])
            projection_stage(nc, env, mix, layer, d)
            short_mixers_stage(nc, env, mix, layer, d)
        mix.yr_hi = make(ctx, "y_rwkv_hi", [P, RT, N], F32R)
        mix.yr_lo = make(ctx, "y_rwkv_lo", [P, RT, N], F32R)
        rwkv_stage(nc, env, mix, layer, d)
        output_stage(nc, env, mix, layer, d)


def rwkv_stage(nc, env, mix, layer, d):
    with ExitStack() as ctx:
        def make(name, shape, dt=F32):
            return ctx.enter_context(nc.sbuf_tensor(name, shape, dt))

        mix.kkn = make("kk_normed", [P, RT, N])
        mix.nb = make("minus_b", [P, RT, N])
        mix.cum = make("cum_decay", [P, RT, NCH, C + 1])
        mix.sws = make("decay_gate_sample", [P, RT, NS])
        mix.g = make("gate", [P, RT, N])
        mix.bonus = make("bonus", [P, RT, N])
        rwkv_prepare(nc, env, mix, layer, d)
        rwkv_pairs(nc, env, mix, layer, d)
        rwkv_finish(nc, env, mix, layer, d)


def rwkv_prepare(nc, env, mix, layer, d):
    with Stage(nc, "rprep") as st:
        s, ps = st.s, env.ps
        wa2 = st.sb("w2_a2", [P, D])
        g2, g2b = st.sb("g2", [P, D]), st.sb("g2_tail", [32, D])
        gates = st.sb("decay_gate", [P, RT, NCH, C + 1])
        sq, nrm = st.sb("kk_sq", [P, RT, N]), st.sb("kk_norm", [P, RT, N])
        fac, rk = st.sb("key_factor", [P, 2, N]), st.sb("r_k", [P, 2, N])
        lnb = st.sb("ln_bias", [P, 1])
        r, k, v = mix.xs[:, 0:8], mix.xs[:, 8:16], mix.xs[:, 16:24]
        head = env.const("head")

        with nc.Block() as block:
            @block.sync
            def _(sp):
                sp.dma_start(wa2[0:64, :], d["rwkv_w2"][layer]).then_inc(s("lora_in"), 16)
                sp.dma_start(wa2[64:P, :], d["rwkv_a2"][layer]).then_inc(s("lora_in"), 16)
                sp.dma_start(g2[:], d["rwkv_g2"][layer][0:P]).then_inc(s("lora_in"), 16)
                sp.dma_start(g2b[:], d["rwkv_g2"][layer][P:160]).then_inc(s("lora_in"), 16)

            @block.gpsimd
            def _(pool):
                pool.memset(gates[:, :, :, 0:1], 0.0).then_inc(s("gates_zero"), 1)
                pool.memset(lnb[:], 0.5 * float(np.log(LN_SCALE))).then_inc(s("ln_bias"), 1)

            @block.scalar
            def _(act):
                act.activation(mix.xs[0:64, 24], mix.xs[0:64, 24], ACT.Tanh).then_inc(s("lr_done"), 1)
                act.activation(mix.xs[:, 25], mix.xs[:, 25], ACT.Sigmoid).then_inc(s("lr_done"), 1)
                act.activation(mix.xs[0:32, 26], mix.xs[0:32, 26], ACT.Sigmoid).then_inc(s("lr_done"), 1)
                act.wait_ge(s("gates_zero"), 1)
                for p in range(RT):
                    w_ps, a_ps, g_ps = (ps[:, 2 * i + p % 2, 0:N] for i in range(3))
                    act.wait_ge(s("lora_ps"), 3 * p + 1)
                    act.activation(gates[:, p, :, 1:C + 1], w_ps[:, 0:T].rearrange("p (c t) -> p c t", c=NCH),
                                   ACT.Sigmoid, bias=env.col("rwkv_w0", p)).then_inc(s("gate_in"), 1)
                    act.activation(mix.sws[:, p], w_ps[:, T:N], ACT.Sigmoid,
                                   bias=env.col("rwkv_w0", p)).then_inc(s("lora_read"), 1)
                    act.wait_ge(s("lora_ps"), 3 * p + 2)
                    act.activation(mix.nb[:, p], a_ps, ACT.Sigmoid, bias=env.col("rwkv_a0", p)).then_inc(s("lora_read"), 1)
                    act.wait_ge(s("lora_ps"), 3 * p + 3)
                    act.activation(mix.g[:, p], g_ps, ACT.Copy).then_inc(s("lora_read"), 1)
                act.wait_ge(s("kk_done"), 1)
                act.activation(sq[:], mix.kkn[:], ACT.Square).then_inc(s("kk_sq"), 1)
                act.wait_ge(s("norm_max"), RT)
                act.wait_ge(s("ln_bias"), 1)
                act.activation(nrm[:], nrm[:], ACT.Ln, scale=LN_SCALE).then_inc(s("norm_ln"), 1)
                act.wait_ge(s("norm_ln"), 1)
                act.activation(nrm[:], nrm[:], ACT.Exp, scale=-0.5, bias=lnb[:, 0:1]).then_inc(s("norm_inv"), 1)

            @block.tensor
            def _(pe):
                pe.wait_ge(s("lora_in"), 64)
                pe.wait_ge(s("lr_done"), 3)
                for p in range(RT):
                    w_ps, a_ps, g_ps = (ps[:, 2 * i + p % 2, 0:N] for i in range(3))
                    c = slice(p * P, (p + 1) * P)
                    if p >= 2:
                        pe.wait_ge(s("lora_read"), 3 * (p - 1))
                    pe.matmul(w_ps, wa2[0:64, c], mix.xs[0:64, 24], start=True, stop=True).then_inc(s("lora_ps"), 1)
                    pe.matmul(a_ps, wa2[64:P, c], mix.xs[64:P, 24], start=True, stop=True).then_inc(s("lora_ps"), 1)
                    pe.matmul(g_ps, g2[:, c], mix.xs[:, 25], start=True, stop=False)
                    pe.matmul(g_ps, g2b[:, c], mix.xs[0:32, 26], start=False, stop=True).then_inc(s("lora_ps"), 1)
                pe.wait_ge(s("kk_sq"), 1)
                for p in range(RT):
                    if p >= 2:
                        pe.wait_ge(s("norm_max"), p - 1)
                    pe.matmul(ps[:, 6 + p % 2, 0:N], head, sq[:, p], start=True, stop=True).then_inc(s("norm_ps"), 1)
                pe.wait_ge(s("norm_max"), RT)
                for p in range(RT):
                    pe.wait_ge(s("rk_done"), p + 1)
                    if p >= 2:
                        pe.wait_ge(s("bonus_done"), p - 1)
                    pe.matmul(ps[:, 6 + p % 2, 0:N], head, rk[:, p % 2], start=True, stop=True).then_inc(s("bonus_ps"), 1)

            @block.vector
            def _(dve):
                dve.tensor_tensor(mix.kkn[:], k, env.col("rwkv_k_k", 0, RT).unsqueeze(2).to_broadcast([P, RT, N]),
                                  ALU.mult).then_inc(s("kk_done"), 1)
                for p in range(RT):
                    dve.wait_ge(s("norm_ps"), p + 1)
                    dve.tensor_scalar(nrm[:, p], ps[:, 6 + p % 2, 0:N], 1e-24, None, ALU.max).then_inc(s("norm_max"), 1)
                dve.wait_ge(s("gate_in"), RT)
                for p in range(RT):
                    dve.tensor_tensor_scan(mix.cum[:, p].rearrange("p c t -> p (c t)"), env.const("scan"),
                                           gates[:, p].rearrange("p c t -> p (c t)"), 0.0, ALU.mult,
                                           ALU.add).then_inc(s("cum_done"), 1)
                dve.wait_ge(s("lora_read"), 3 * RT)
                for p in range(RT):
                    if p >= 2:
                        dve.wait_ge(s("k_done"), p - 1)
                    dve.tensor_scalar(fac[:, p % 2], mix.nb[:, p], env.col("rwkv_k_a", p), env.oka[:, p:p + 1],
                                      ALU.mult, ALU.add).then_inc(s("fac_done"), 1)
                    dve.wait_ge(s("fac_done"), p + 1)
                    dve.wait_ge(s("kk_done"), 1)
                    dve.tensor_tensor(k[:, p], k[:, p], fac[:, p % 2], ALU.mult).then_inc(s("k_done"), 1)
                    dve.wait_ge(s("k_done"), p + 1)
                    if p >= 2:
                        dve.wait_ge(s("bonus_ps"), p - 1)
                    dve.scalar_tensor_tensor(out=rk[:, p % 2], in0=r[:, p], scalar=env.col("rwkv_r_k", p), in1=k[:, p],
                                             op0=ALU.mult, op1=ALU.mult).then_inc(s("rk_done"), 1)
                    if p:
                        dve.wait_ge(s("bonus_ps"), p)
                        dve.tensor_tensor(mix.bonus[:, p - 1], v[:, p - 1], ps[:, 6 + (p - 1) % 2, 0:N],
                                          ALU.mult).then_inc(s("bonus_done"), 1)
                dve.wait_ge(s("bonus_ps"), RT)
                dve.tensor_tensor(mix.bonus[:, RT - 1], v[:, RT - 1], ps[:, 6 + (RT - 1) % 2, 0:N],
                                  ALU.mult).then_inc(s("bonus_done"), 1)
                dve.wait_ge(s("norm_inv"), 1)
                dve.tensor_tensor(mix.kkn[:], mix.kkn[:], nrm[:], ALU.mult).then_inc(s("kkn_done"), 1)
                dve.wait_ge(s("kkn_done"), 1)
                dve.scalar_tensor_tensor(out=mix.nb[:], in0=mix.kkn[:], scalar=-1.0, in1=mix.nb[:], op0=ALU.mult,
                                         op1=ALU.mult).then_inc(s("nb_done"), 1)


def rwkv_pairs(nc, env, mix, layer, d):
    LV = len(LEVELS)
    with Stage(nc, "pair") as st:
        s, ps = st.s, env.ps
        pq = st.sb("decays", [P, 3, 2, NCH, C + 1])
        ar = st.sb("a_r", [P, 3, 2, T])
        bk = st.sb("b_k", [P, 3, 2, T])
        tok = st.sb("tok", [P, 2, 3, 2, P])
        nbr = st.sb("n_br", [P, 2, 2, 2, 2, P])
        akr = st.sb("ak_kr", [P, 2, 2, 2, 2, P])
        low = st.sb("n_low", [P, 4, P])
        lev = st.sb("n_levels", [P, 4, LV, P])
        x = st.sb("inverse", [P, 2, 2, 4, P])
        t1 = st.sb("n_x", [P, 4, P])
        rhs = st.sb("rhs", [P, P])
        sa = st.sb("sa", [P, 2, 2, P])
        s0 = st.sb("state", [P, P])
        fin = st.sb("final_state", [P, RT, C])
        r, k, v = mix.xs[:, 0:8], mix.xs[:, 8:16], mix.xs[:, 16:24]
        ident, cau, lowm = env.const("ident"), env.const("cau"), env.const("low")
        first, levels = env.const("first"), env.const("levels")

        with nc.Block() as block:
            @block.sync
            def _(sp):
                sp.wait_ge(s("fin_in"), 2 * RT)
                sp.dma_start(d["p_wkv"][layer, 0].rearrange("(m h) i j -> (h i) m j", h=2), fin[:]).then_inc(s("stored"), 16)
                sp.wait_ge(s("stored"), 16)

            @block.gpsimd
            def _(pool):
                def weigh(p):
                    b3 = p % 3
                    pool.wait_ge(s("pq_done"), 2 * p + 2)
                    if p >= 3:
                        pool.wait_ge(s("y_ps"), p - 2)
                    c4 = lambda a: a.rearrange("p (c t) -> p c t", c=NCH)
                    dec, inv = pq[:, b3, 0], pq[:, b3, 1, :, 1:C + 1]
                    for out, x0, x1 in ((ar[:, b3, 0], mix.kkn[:, p, 0:T], dec[:, :, 0:C]),
                                        (bk[:, b3, 0], mix.nb[:, p, 0:T], inv),
                                        (ar[:, b3, 1], r[:, p, 0:T], dec[:, :, 1:C + 1]),
                                        (bk[:, b3, 1], k[:, p, 0:T], inv)):
                        pool.tensor_tensor(c4(out), c4(x0), x1, ALU.mult).then_inc(s("weighed"), 1)

                pool.memset(s0[:], 0.0).then_inc(s("s0_zero"), 1)
                weigh(0)
                for p in range(RT):
                    pool.wait_ge(s("masked"), 6 * p + 6)
                    nt = nbr[:, p % 2, :, :, 0].rearrange("p q c t -> p (q c) t")
                    if p >= 2:
                        pool.wait_ge(s("sa_ps"), 4 * (p - 1))
                    pool.tensor_tensor(x[:, p % 2, 0], low[:], first[:, 0:P].unsqueeze(1).to_broadcast([P, 4, P]),
                                       ALU.mult).then_inc(s("first_done"), 1)
                    pool.tensor_tensor(x[:, p % 2, 1], nt, first[:, P:2 * P].unsqueeze(1).to_broadcast([P, 4, P]),
                                       ALU.mult).then_inc(s("first_done"), 1)
                    if p:
                        pool.wait_ge(s("t1_ps"), LV * p)
                    for i in range(LV):
                        pool.tensor_tensor(lev[:, :, i], nt, levels[:, i * P:(i + 1) * P].unsqueeze(1).to_broadcast([P, 4, P]),
                                           ALU.mult).then_inc(s("lev_done"), 1)
                    if p + 1 < RT:
                        weigh(p + 1)

            @block.scalar
            def _(act):
                def decays(p):
                    if p >= 3:
                        act.wait_ge(s("st_in"), 8 * (p - 2))
                        act.wait_ge(s("weighed"), 4 * (p - 2))
                    for i, sign in enumerate((-DECAY, DECAY)):
                        act.activation(pq[:, p % 3, i], mix.cum[:, p], ACT.Exp, scale=sign).then_inc(s("pq_done"), 1)

                def tokens(p):
                    act.wait_ge(s("tok_ps"), 2 * p + 1)
                    if p >= 2:
                        act.wait_ge(s("y_ps"), p - 1)
                    act.activation(tok[:, p % 2, 0:2].rearrange("p a c f -> p (a c f)"), ps[:, 6, :],
                                   ACT.Copy).then_inc(s("tok_in"), 1)
                    act.wait_ge(s("tok_ps"), 2 * p + 2)
                    act.activation(tok[:, p % 2, 2].rearrange("p c f -> p (c f)"), ps[:, 6, 0:T],
                                   ACT.Copy).then_inc(s("tok_in"), 1)

                def t1_copy(p, i):
                    n = LV * p + i
                    act.wait_ge(s("t1_ps"), n + 1)
                    if n:
                        act.wait_ge(s("u_ps"), n)
                    act.activation(t1[:].rearrange("p q t -> p (q t)"), ps[:, 0, :], ACT.Copy).then_inc(s("t1_in"), 1)

                def rhs_copy(p, c):
                    w, n = slice(C * (c % 2), C * (c % 2) + C), 4 * p + c
                    act.wait_ge(s("rhs_ps"), n + 1)
                    act.activation(rhs[w], ps[w, 3, 0:P], ACT.Copy).then_inc(s("rhs_in"), 1)

                def sa_copy(p, c):
                    w, n = slice(C * (c % 2), C * (c % 2) + C), 4 * p + c
                    act.wait_ge(s("sa_ps"), n + 1)
                    act.activation(sa[w, p % 2, c // 2], ps[w, 4, 0:P], ACT.Copy).then_inc(s("sa_in"), 1)

                def state_copy(p, c):
                    n = 4 * p + c
                    act.wait_ge(s("st_ps"), n + 1)
                    act.wait_ge(s("s0_zero"), 1)
                    if p and c == 0:
                        act.wait_ge(s("fin_ps"), p)
                    for h in range(2):
                        q = slice(C * h, C * h + C)
                        act.activation(s0[q, q], ps[q, 7, q], ACT.Copy,
                                       scale=pq[q, p % 3, 0, c, C:C + 1]).then_inc(s("st_in"), 1)

                def final_copy(p):
                    act.wait_ge(s("fin_ps"), p + 1)
                    for h in range(2):
                        q = slice(C * h, C * h + C)
                        act.activation(fin[q, p], ps[q, 7, q], ACT.Copy).then_inc(s("fin_in"), 1)

                decays(0)
                for p in range(RT + 1):
                    if p < RT:
                        tokens(p)
                    if p + 1 < RT:
                        decays(p + 1)
                    for i in range(LV):
                        if p < RT:
                            t1_copy(p, i)
                        if p and i:
                            state_copy(p - 1, i - 1)
                        if p and i < NCH:
                            rhs_copy(p - 1, i)
                            sa_copy(p - 1, i)
                    if p:
                        final_copy(p - 1)

            @block.vector
            def _(dve):
                for p in range(RT + 1):
                    if p < RT:
                        if p >= 2:
                            dve.wait_ge(s("y_ps"), p - 1)
                        if p:
                            dve.wait_ge(s("first_done"), 2 * p)
                        for q in range(2):
                            dve.wait_ge(s("g_ps"), 2 * p + q + 1)
                            two = lambda a: a.unsqueeze(1).to_broadcast([P, 2, 2 * P])
                            for b, dst in ((0, nbr), (1, akr)):
                                dve.tensor_tensor(dst[:, p % 2, q].rearrange("p c k t -> p c (k t)"),
                                                  ps[:, b, :].rearrange("p (c t) -> p c t", c=2), two(cau),
                                                  ALU.mult).then_inc(s("masked"), 1)
                            dve.tensor_tensor(low[:, 2 * q:2 * q + 2], ps[:, 2, 0:2 * P].rearrange("p (c t) -> p c t", c=2),
                                              lowm.unsqueeze(1).to_broadcast([P, 2, P]), ALU.mult).then_inc(s("masked"), 1)
                        dve.wait_ge(s("first_done"), 2 * p + 2)
                        xt = x[:, p % 2].rearrange("p a q t -> p (a q) t")
                        dve.tensor_tensor(xt, xt, ident.unsqueeze(1).to_broadcast([P, 8, P]), ALU.add).then_inc(s("x_up"), 1)
                        for i in range(LV):
                            dve.wait_ge(s("x_up"), (LV + 1) * p + i + 1)
                            dve.wait_ge(s("u_ps"), LV * p + i + 1)
                            if i < LV - 1:
                                dve.tensor_tensor(xt, xt, ps[:, 1:3, :].rearrange("p a (q t) -> p (a q) t", q=4),
                                                  ALU.add).then_inc(s("x_up"), 1)
                            else:
                                dve.tensor_tensor(x[:, p % 2, 1], x[:, p % 2, 1],
                                                  ps[:, 2, :].rearrange("p (q t) -> p q t", q=4), ALU.add).then_inc(s("x_up"), 1)
                    if p:
                        dve.wait_ge(s("y_ps"), p)
                        dve.tensor_copy(r[:, p - 1, 0:T], ps[:, 5, 0:T]).then_inc(s("y_in"), 1)

            @block.tensor
            def _(pe):
                def turn(p):
                    pe.wait_ge(s("weighed"), 4 * p + 4)
                    if p:
                        pe.wait_ge(s("tok_in"), 2 * p)
                    for i in range(2):
                        for cp in range(2):
                            mm = pe.transpose(ps[:, 6, (2 * i + cp) * P:(2 * i + cp + 1) * P],
                                              bk[:, p % 3, i, cp * P:(cp + 1) * P], ident)
                    mm.then_inc(s("tok_ps"), 1)
                    pe.wait_ge(s("tok_in"), 2 * p + 1)
                    for cp in range(2):
                        mm = pe.transpose(ps[:, 6, cp * P:(cp + 1) * P], v[:, p, cp * P:(cp + 1) * P], ident)
                    mm.then_inc(s("tok_ps"), 1)

                def gram(p, q):
                    h = slice(C * q, C * q + C)
                    if q:
                        pe.wait_ge(s("masked"), 6 * p + 3)
                    elif p:
                        pe.wait_ge(s("x_up"), (LV + 1) * p)
                    for cp in range(2):
                        c = slice(cp * P, cp * P + P)
                        pe.matmul(ps[:, 0, cp * T:cp * T + T], bk[h, p % 3, 0, c], ar[h, p % 3, :, c], start=True, stop=True)
                        pe.matmul(ps[:, 1, cp * T:cp * T + T], bk[h, p % 3, 1, c], ar[h, p % 3, :, c], start=True, stop=True)
                        mm = pe.matmul(ps[:, 2, c], ar[h, p % 3, 0, c], bk[h, p % 3, 0, c], start=True, stop=True)
                    mm.then_inc(s("g_ps"), 1)

                def level_t1(p, i):
                    pe.wait_ge(s("x_up"), (LV + 1) * p + i + 1)
                    pe.wait_ge(s("lev_done"), LV * p + i + 1)
                    if i == 0:
                        pe.wait_ge(s("masked"), 6 * p + 6)
                    else:
                        pe.wait_ge(s("t1_in"), LV * p + i)
                    for q in range(4):
                        mm = pe.matmul(ps[:, 0, q * P:(q + 1) * P], lev[:, q, i], x[:, p % 2, 0, q], start=True, stop=True)
                    mm.then_inc(s("t1_ps"), 1)

                def level_u(p, i):
                    pe.wait_ge(s("t1_in"), LV * p + i + 1)
                    for q in range(4):
                        c = slice(q * P, (q + 1) * P)
                        if i < LV - 1:
                            pe.matmul(ps[:, 1, c], x[:, p % 2, 1, q], t1[:, q], start=True, stop=True)
                        mm = pe.matmul(ps[:, 2, c], t1[:, q], x[:, p % 2, 1, q], start=True, stop=True)
                    mm.then_inc(s("u_ps"), 1)

                def chunk_rhs(p, c):
                    cp, w, n = c // 2, slice(C * (c % 2), C * (c % 2) + C), 4 * p + c
                    if c == 0:
                        pe.wait_ge(s("x_up"), (LV + 1) * (p + 1))
                        pe.wait_ge(s("tok_in"), 2 * p + 2)
                    if n:
                        pe.wait_ge(s("rhs_in"), n)
                    for h in range(2):
                        f = slice(C * h, C * h + C)
                        mm = pe.matmul(ps[w, 3, f], akr[:, p % 2, h, cp, 0, w], tok[:, p % 2, 2, cp, f], start=h == 0,
                                       stop=c == 0, skip_group_check=True)
                    if c:
                        pe.wait_ge(s("st_in"), 2 * n)
                        mm = pe.matmul(ps[w, 3, 0:P], ar[:, p % 3, 0, c * C:c * C + C], s0[:], start=False, stop=True,
                                       skip_group_check=True)
                    mm.then_inc(s("rhs_ps"), 1)
                    if c % 2 == 0:
                        if p and c == 0:
                            pe.wait_ge(s("y_in"), p)
                        for h in range(2):
                            f = slice(C * h, C * h + C)
                            pe.matmul(ps[f, 5, cp * P:cp * P + P], tok[:, p % 2, 2, cp, f], akr[:, p % 2, h, cp, 1],
                                      start=c == 0, stop=False, skip_group_check=True)
                    if c:
                        pe.matmul(ps[:, 5, c * C:c * C + C], s0[:], ar[:, p % 3, 1, c * C:c * C + C], start=False, stop=False,
                                  skip_group_check=True)

                def chunk_sa(p, c):
                    cp, w, n = c // 2, slice(C * (c % 2), C * (c % 2) + C), 4 * p + c
                    pe.wait_ge(s("rhs_in"), n + 1)
                    if n:
                        pe.wait_ge(s("sa_in"), n)
                    for h in range(2):
                        f = slice(C * h, C * h + C)
                        mm = pe.matmul(ps[w, 4, f], x[w, p % 2, 1, 2 * h + cp, w], rhs[w, f], start=True, stop=True)
                    mm.then_inc(s("sa_ps"), 1)

                def chunk_state(p, c):
                    cp, w, n = c // 2, slice(C * (c % 2), C * (c % 2) + C), 4 * p + c
                    if c == 0 and p:
                        pe.wait_ge(s("fin_in"), 2 * p)
                    if c:
                        pe.matmul(ps[:, 7, 0:P], ident, s0[:], start=True, stop=False)
                    pe.matmul(ps[:, 7, 0:P], tok[w, p % 2, 1, cp], tok[w, p % 2, 2, cp], start=c == 0, stop=False)
                    pe.wait_ge(s("sa_in"), n + 1)
                    pe.matmul(ps[:, 7, 0:P], tok[w, p % 2, 0, cp], sa[w, p % 2, cp], start=False,
                              stop=True).then_inc(s("st_ps"), 1)
                    if c % 2:
                        for h in range(2):
                            f = slice(C * h, C * h + C)
                            mm = pe.matmul(ps[f, 5, cp * P:cp * P + P], sa[:, p % 2, cp, f], nbr[:, p % 2, h, cp, 1],
                                           start=False, stop=c == 3, skip_group_check=True)
                        if c == 3:
                            mm.then_inc(s("y_ps"), 1)

                for p in range(RT + 1):
                    if p < RT:
                        turn(p)
                        gram(p, 0)
                        gram(p, 1)
                    for i in range(LV):
                        if p < RT:
                            level_t1(p, i)
                        if p and i:
                            chunk_state(p - 1, i - 1)
                        if p and i < NCH:
                            chunk_rhs(p - 1, i)
                        if p < RT:
                            level_u(p, i)
                        if p and i < NCH:
                            chunk_sa(p - 1, i)
                    if p:
                        pe.wait_ge(s("st_in"), 8 * p)
                        pe.transpose(ps[:, 7, 0:P], s0[:], ident).then_inc(s("fin_ps"), 1)


def rwkv_finish(nc, env, mix, layer, d):
    with Stage(nc, "rfin") as st:
        s, ps = st.s, env.ps
        state = st.sb("sample_wkv", [P, RT, NS, HS])
        eye = st.sb("eye64", [P, HS])
        diag = st.sb("diag", [P, 2, NS, HS])
        prod, outer = st.sb("prod", [P, NS, HS]), st.sb("outer", [P, NS, HS])
        sav = st.sb("sample_sa", [P, RT, NS])
        wdec = st.sb("sample_decay", [P, RT, NS])
        dev, sq = st.sb("deviation", [P, RT, N]), st.sb("dev_sq", [P, RT, N])
        y, k, v = mix.xs[:, 0:8], mix.xs[:, 8:16], mix.xs[:, 16:24]
        ident, head = env.const("ident"), env.const("head")
        sin = d["state_rwkv_wkv"][layer].rearrange("b (m h) i j -> m (h i) b j", h=2)
        sout = d["s_wkv"][layer].rearrange("b (m h) i j -> m (h i) b j", h=2)
        V = 5

        with nc.Block() as block:
            @block.sync
            def _(sp):
                for m in range(RT):
                    sp.dma_start(state[:, m], sin[m]).then_inc(s("state_in"), 16)
                for m in range(RT):
                    sp.wait_ge(s("state_new"), m + 1)
                    sp.dma_start(sout[m], state[:, m]).then_inc(s("stored"), 16)
                sp.wait_ge(s("stored"), 16 * RT)

            @block.scalar
            def _(act):
                act.activation(wdec[:], mix.sws[:], ACT.Exp, scale=-DECAY).then_inc(s("wdec_done"), 1)
                act.wait_ge(s("dev_done"), RT)
                act.activation(sq[:], dev[:], ACT.Square).then_inc(s("dev_sq"), 1)
                for m in range(RT):
                    act.wait_ge(s("var_ps"), m + 1)
                    act.activation(sq[:, m], ps[:, m % 4, 0:N], ACT.Ln, bias=env.eps[:, 1:2], scale=1.0 / HS).then_inc(s("var_ln"), 1)
                act.wait_ge(s("var_ln"), RT)
                act.activation(sq[:], sq[:], ACT.Exp, scale=-0.5).then_inc(s("rstd"), 1)
                for m in range(RT):
                    act.wait_ge(s("y_out"), m + 1)
                    act.activation(mix.yr_hi[:, m], dev[:, m], ACT.Copy).then_inc(s("y_hi"), 1)

            @block.tensor
            def _(pe):
                for n in range(RT * V):
                    pe.wait_ge(s("diag_done"), n + 1)
                    if n >= 4:
                        pe.wait_ge(s("row_used"), n - 3)
                    pe.matmul(ps[:, n % 4, :], head, diag[:, n % 2].rearrange("p b j -> p (b j)"), start=True,
                              stop=True).then_inc(s("row_ps"), 1)
                pe.wait_ge(s("row_used"), RT * V)
                for m in range(RT):
                    pe.wait_ge(s("y_ready"), 1)
                    if m >= 4:
                        pe.wait_ge(s("dev_done"), m - 3)
                    pe.matmul(ps[:, 4 + m % 4, 0:N], head, y[:, m], start=True, stop=True).then_inc(s("mean_ps"), 1)
                pe.wait_ge(s("dev_sq"), 1)
                for m in range(RT):
                    if m >= 4:
                        pe.wait_ge(s("var_ln"), m - 3)
                    pe.matmul(ps[:, m % 4, 0:N], head, sq[:, m], start=True, stop=True).then_inc(s("var_ps"), 1)

            @block.vector
            def _(dve):
                dve.tensor_tensor(eye[:], ident[:, 0:HS], ident[:, HS:P], ALU.add).then_inc(s("eye"), 1)
                dve.wait_ge(s("eye"), 1)
                dve.wait_ge(s("wdec_done"), 1)
                n = [0]

                def row_diag(vec):
                    i = n[0]
                    if i >= 2:
                        dve.wait_ge(s("row_ps"), i - 1)
                    dve.tensor_tensor(diag[:, i % 2], eye[:].unsqueeze(1).to_broadcast([P, NS, HS]),
                                      vec.unsqueeze(2).to_broadcast([P, NS, HS]), ALU.mult).then_inc(s("diag_done"), 1)
                    n[0] += 1

                chain = [0]

                def step(ins):
                    chain[0] += 1
                    ins.then_inc(s("step"), 1)
                    dve.wait_ge(s("step"), chain[0])

                def row(i):
                    return ps[:, i % 4, :].rearrange("p (b j) -> p b j", b=NS)

                for m in range(RT):
                    i = V * m
                    vecs = (mix.kkn[:, m, T:N], wdec[:, m], mix.nb[:, m, T:N], k[:, m, T:N], y[:, m, T:N])
                    stt = state[:, m]
                    bc = lambda a: a.unsqueeze(2).to_broadcast([P, NS, HS])
                    row_diag(vecs[0])
                    row_diag(vecs[1])
                    dve.wait_ge(s("row_ps"), i + 1)
                    if m == 0:
                        dve.wait_ge(s("state_in"), 16 * RT)
                    dve.tensor_tensor(prod[:], stt, row(i), ALU.mult).then_inc(s("row_used"), 1)
                    row_diag(vecs[2])
                    dve.wait_ge(s("row_used"), i + 1)
                    step(dve.tensor_reduce(sav[:, m], prod[:], AX.X, ALU.add))
                    dve.wait_ge(s("row_ps"), i + 2)
                    dve.tensor_tensor(stt, stt, row(i + 1), ALU.mult).then_inc(s("row_used"), 1)
                    row_diag(vecs[3])
                    dve.wait_ge(s("row_ps"), i + 3)
                    dve.tensor_tensor(outer[:], row(i + 2), bc(sav[:, m]), ALU.mult).then_inc(s("row_used"), 1)
                    row_diag(vecs[4])
                    dve.wait_ge(s("row_used"), i + 3)
                    step(dve.tensor_tensor(stt, stt, outer[:], ALU.add))
                    dve.wait_ge(s("row_ps"), i + 4)
                    dve.tensor_tensor(outer[:], row(i + 3), bc(v[:, m, T:N]), ALU.mult).then_inc(s("row_used"), 1)
                    dve.wait_ge(s("row_used"), i + 4)
                    dve.tensor_tensor(stt, stt, outer[:], ALU.add).then_inc(s("state_new"), 1)
                    dve.wait_ge(s("state_new"), m + 1)
                    dve.wait_ge(s("row_ps"), i + 5)
                    dve.tensor_tensor(prod[:], stt, row(i + 4), ALU.mult).then_inc(s("row_used"), 1)
                    dve.wait_ge(s("row_used"), i + 5)
                    step(dve.tensor_reduce(sav[:, m], prod[:], AX.X, ALU.add))
                dve.tensor_copy(y[:, :, T:N], sav[:]).then_inc(s("y_ready"), 1)
                for m in range(RT):
                    dve.wait_ge(s("mean_ps"), m + 1)
                    dve.scalar_tensor_tensor(out=dev[:, m], in0=ps[:, 4 + m % 4, 0:N], scalar=-1.0 / HS, in1=y[:, m],
                                             op0=ALU.mult, op1=ALU.add).then_inc(s("dev_done"), 1)
                dve.wait_ge(s("rstd"), 1)
                dve.tensor_tensor(dev[:], dev[:], sq[:], ALU.mult).then_inc(s("normed"), 1)
                dve.wait_ge(s("normed"), 1)
                for m in range(RT):
                    dve.tensor_scalar(dev[:, m], dev[:, m], env.col("rwkv_ln_w", m), env.col("rwkv_ln_b", m), ALU.mult,
                                      ALU.add).then_inc(s("affine"), 1)
                dve.wait_ge(s("affine"), RT)
                step(dve.tensor_tensor(dev[:], dev[:], mix.bonus[:], ALU.add))
                for m in range(RT):
                    dve.tensor_tensor(dev[:, m], dev[:, m], mix.g[:, m], ALU.mult).then_inc(s("y_out"), 1)
                for m in range(RT):
                    dve.wait_ge(s("y_hi"), m + 1)
                    dve.tensor_tensor(mix.yr_lo[:, m], dev[:, m], mix.yr_hi[:, m].bitcast(F32), ALU.subtract).then_inc(s("y_lo"), 1)


OUTS = {
    "y_prompt": (1, T, D), "y_sample": (NS, 1, D),
    "p_shift": (DEPTH, 1, RWKV_PROJ), "p_wkv": (DEPTH, 1, 16, HS, HS), "p_sc": (DEPTH, 1, 2, SC),
    "p_conv": (DEPTH, 1, 3, D), "p_ssm": (DEPTH, 1, 8, HS, P),
    "s_shift": (DEPTH, NS, RWKV_PROJ), "s_wkv": (DEPTH, NS, 16, HS, HS), "s_sc": (DEPTH, NS, 2, SC),
    "s_conv": (DEPTH, NS, 3, D), "s_ssm": (DEPTH, NS, 8, HS, P),
}


def trunk(nc, d, stages=("ffn1", "mix", "ffn2")):
    with ExitStack() as ctx:
        def sb(name, shape, dt=F32):
            return ctx.enter_context(nc.sbuf_tensor(name, shape, dt))

        env = Env()
        env.cst = sb("cst", [P, sum(n for _, n in CONST_WHERE.values())])
        env.x = sb("x", [P, KT, N])
        env.eps = sb("eps", [P, 3])
        env.cols = sb("cols", [P, NCOLS])
        env.omu = sb("one_minus_mu", [P, XT])
        env.oka = sb("one_minus_ka", [P, RT])
        env.shift = sb("shift_state", [P, XT, NS])
        env.scb = sb("sc_state", [P, ST, 2 * NS])
        env.conv = sb("conv_state", [P, 8, 3 * NS])
        env.heads = sb("ssm_heads", [8, 5])
        env.dcol = sb("ssm_d", [P, 4])
        env.ps = ctx.enter_context(nc.psum_tensor("ps", [P, 8, 512], F32))
        load_stage(nc, env, d)
        with nc.Fori(0, DEPTH) as layer:
            vector_stage(nc, env, layer, d)
            if "ffn1" in stages:
                ffn_stage(nc, env, layer, "ffn1", "norm_ffn1", d["ffn1_w_in"], d["ffn1_w_out"])
            if "mix" in stages:
                mix_stages(nc, env, layer, d)
            if "ffn2" in stages:
                ffn_stage(nc, env, layer, "ffn2", "norm_ffn2", d["ffn2_w_in"], d["ffn2_w_out"])
        final_stage(nc, env, d)


def kernel(**inputs):
    import concourse.bacc as bacc
    from concourse.bass_utils import run_bass_kernel_spmd

    nc = bacc.Bacc("TRN2", target_bir_lowering=False, num_devices=1)
    arrays, d = {}, {}
    for name, a in inputs.items():
        a = np.ascontiguousarray(a)
        arrays[f"in_{name}"] = a
        d[name] = nc.dram_tensor(f"in_{name}", a.shape, mybir.dt.from_np(a.dtype), kind="ExternalInput").ap()
    cst = shape_constants()[0]
    arrays["in_cst"] = cst
    d["cst"] = nc.dram_tensor("in_cst", cst.shape, F32, kind="ExternalInput").ap()
    for name, shape in OUTS.items():
        d[name] = nc.dram_tensor(f"out_{name}", shape, F32, kind="ExternalOutput").ap()
    trunk(nc, d)
    r = run_bass_kernel_spmd(nc, [arrays], core_ids=[0])
    return tuple(r.results[0][f"out_{name}"] for name in OUTS)
```

```python
from contextlib import ExitStack

import numpy as np

import concourse.bass as bass
from concourse import mybir

F32 = mybir.dt.float32
F32R = mybir.dt.float32r
ALU = mybir.AluOpType
ACT = mybir.ActivationFunctionType
AX = mybir.AxisListType

P = 128
D = 1024
T = 256
NS = 8
N = T + NS
DEPTH = 2
KT = D // P
FF = 2816
FT = FF // P
HS = 64
RT = 8
RWKV_PROJ = 3 * D + 64 + 64 + 160
XT = 27
SC = 512
ST = SC // P
SC_PROJ = 3 * SC
SSM_PROJ = 512 + 1024 + 8
IN_COLS = RWKV_PROJ + SC_PROJ + SSM_PROJ
MT = 2 * KT
C = 64
NCH = T // C
NORM_EPS = 1e-6
GN_EPS = 64e-5
DECAY = float(np.exp(-0.5))
LN_SCALE = 2.0 ** 20
LEVELS = (2, 4, 8, 16, 32)

ROWS_A = (("norm_ffn1", 8), ("norm_mix", 8), ("norm_ffn2", 8), ("rwkv_mu", 27), ("rwkv_w0", 8), ("rwkv_a0", 8),
          ("rwkv_k_k", 8), ("rwkv_k_a", 8), ("rwkv_r_k", 8), ("rwkv_ln_w", 8), ("rwkv_ln_b", 8))
ROWS_B = (("sc_conv_w", 12), ("sc_norm", 4), ("ssm_conv_w", 32), ("ssm_conv_b", 8), ("ssm_norm", 4))
COL = {}
for _rows, _base in ((ROWS_A, 0), (ROWS_B, P)):
    _at = _base
    for _name, _n in _rows:
        COL[_name] = _at
        _at += _n
NCOLS = P + sum(n for _, n in ROWS_B)


def shape_constants():
    i = np.arange(P)
    same = (i[:, None] // C) == (i[None, :] // C)
    parts = {}
    parts["ident"] = np.eye(P)
    parts["mean"] = np.full((P, P), 1.0 / D)
    parts["ones"] = np.ones((P, P))
    parts["head"] = same * 1.0
    parts["cau2"] = np.concatenate([same & (i[:, None] < i[None, :]), same & (i[:, None] <= i[None, :])], 1) * 1.0

    def level(b):
        return ((i[:, None] // (2 * b)) == (i[None, :] // (2 * b))) & (i[:, None] % (2 * b) >= b) & (i[None, :] % (2 * b) < b)

    parts["first"] = level(1).T * 1.0
    parts["levels"] = np.concatenate([level(b).T for b in LEVELS], 1) * 1.0
    t = np.arange(T)
    parts["neg"] = np.concatenate([np.where(t[None, :] >= i[:, None], 0.0, -1e30),
                                   np.where(i[None, :] >= i[:, None], 0.0, -1e30)], 1)
    one = np.zeros((P, 8, P))
    pair = np.zeros((P, 4, P))
    for h in range(8):
        one[h, h] = 1.0
        pair[h, h // 2, (h % 2) * HS:(h % 2 + 1) * HS] = 1.0
    parts["row8"] = one.reshape(P, -1)
    parts["pair8"] = pair.reshape(P, -1)
    parts["scan"] = np.tile((np.arange(C + 1) > 0) * 1.0, NCH)[None, :].repeat(P, 0)
    at, where = 0, {}
    for name, a in parts.items():
        where[name] = (at, a.shape[1])
        at += a.shape[1]
    return np.concatenate(list(parts.values()), 1).astype(np.float32), where


CONST_WHERE = shape_constants()[1]


class Stage:

    def __init__(self, nc, tag):
        self.nc, self.tag, self.ctx, self.sems, self.named = nc, tag, ExitStack(), [], {}

    def __enter__(self):
        return self

    def sem(self, name):
        s = self.ctx.enter_context(self.nc.semaphore(f"{self.tag}_{name}"))
        self.sems.append(s)
        return s

    def s(self, name):
        if name not in self.named:
            self.named[name] = self.sem(name)
        return self.named[name]

    def sb(self, name, shape, dt=F32):
        return self.ctx.enter_context(self.nc.sbuf_tensor(f"{self.tag}_{name}", shape, dt))

    def __exit__(self, *exc):
        if exc[0] is None:
            with self.nc.Block() as block:
                @block.gpsimd
                def _(pool):
                    for s in self.sems:
                        pool.sem_clear(s)
        self.ctx.close()


class Stream:
    RING = 4

    def __init__(self, st, kp, pieces, halves):
        self.pieces, self.halves = pieces, halves
        self.raw = st.sb("raw", [P, self.RING, kp, 2 * P])
        self.hi = st.sb("hi", [P, self.RING, kp, P], F32R)
        self.lo = st.sb("lo", [P, self.RING, kp, P], F32R)
        self.loaded = [st.sem(f"raw_loaded{i}") for i in range(self.RING)]
        self.hi_ready = st.sem("hi_ready")
        self.lo_ready = [st.sem("lo_ready_pool"), st.sem("lo_ready_dve")]
        self.used = st.sem("half_used")
        self.last, self.landed, total = {}, [], [0] * self.RING
        for n, h in enumerate(halves):
            self.last[h[0]] = n
        for p, dmas in enumerate(pieces):
            total[p % self.RING] += 16 * len(dmas)
            self.landed.append(total[p % self.RING])

    def load(self, sp, p):
        if p >= self.RING:
            n = max(self.last[q] for q in range(p - self.RING + 1)) + 1
            sp.wait_ge(self.hi_ready, n)
            sp.wait_ge(self.lo_ready[0], (n + 1) // 2)
            if n // 2:
                sp.wait_ge(self.lo_ready[1], n // 2)
        for (k, c0, w), src in self.pieces[p]:
            sp.dma_start(self.raw[:, p % self.RING, 0:k, c0:c0 + w], src).then_inc(self.loaded[p % self.RING], 16)

    def _raw(self, n):
        p, c0, w, k = self.halves[n]
        return self.raw[:, p % self.RING, 0:k, c0:c0 + w]

    def split_hi(self, act, n):
        if n >= len(self.halves):
            return
        p, _, w, k = self.halves[n]
        act.wait_ge(self.loaded[p % self.RING], self.landed[p])
        if n >= self.RING:
            act.wait_ge(self.used, n - self.RING + 1)
        act.activation(self.hi[:, n % self.RING, 0:k, 0:w], self._raw(n), ACT.Copy).then_inc(self.hi_ready, 1)

    def split_lo(self, eng, n):
        if n >= len(self.halves):
            return
        _, _, w, k = self.halves[n]
        eng.wait_ge(self.hi_ready, n + 1)
        eng.tensor_tensor(self.lo[:, n % self.RING, 0:k, 0:w], self._raw(n),
                          self.hi[:, n % self.RING, 0:k, 0:w].bitcast(F32), ALU.subtract).then_inc(self.lo_ready[n % 2], 1)

    def product(self, pe, n, out, x_hi, x_lo, start=True, stop=True):
        _, _, w, k = self.halves[n]
        pe.wait_ge(self.hi_ready, n + 1)
        pe.wait_ge(self.lo_ready[n % 2], n // 2 + 1)
        s = n % self.RING
        for j in range(k):
            pe.matmul(out, self.hi[:, s, j, 0:w], x_hi[:, j], start=start and j == 0, stop=False)
            pe.matmul(out, self.hi[:, s, j, 0:w], x_lo[:, j], start=False, stop=False)
            mm = pe.matmul(out, self.lo[:, s, j, 0:w], x_hi[:, j], start=False, stop=stop and j == k - 1)
        mm.then_inc(self.used, 1)


class Env:

    def const(self, name):
        at, n = CONST_WHERE[name]
        return self.cst[:, at:at + n]

    def col(self, name, i=0, n=1):
        return self.cols[:, COL[name] + i:COL[name] + i + n]


def normed_input(st, env, gain, bank):
    h_hi = st.sb("h_hi", [P, KT, N], F32R)
    h_lo = st.sb("h_lo", [P, KT, N], F32R)
    sq = st.sb("norm_sq", [P, KT, N])
    rt = st.sb("norm_root", [P, N])
    rs = st.sb("norm_rs", [P, N])
    squared, summed, rooted = st.sem("squared"), st.sem("mean_summed"), st.sem("rooted")
    inverted, scaled = st.sem("root_inverted"), st.sem("normed")
    hi_done, lo_done = st.sem("h_hi_done"), st.sem("h_lo_done")
    x = env.x

    def act_square(act):
        act.activation(sq[:], x[:], ACT.Square).then_inc(squared, 1)

    def pe_mean(pe):
        pe.wait_ge(squared, 1)
        for k in range(KT):
            mm = pe.matmul(env.ps[:, bank, 0:N], env.const("mean"), sq[:, k], start=k == 0, stop=k == KT - 1)
        mm.then_inc(summed, 1)

    def act_root(act):
        act.wait_ge(summed, 1)
        act.activation(rt[:], env.ps[:, bank, 0:N], ACT.Sqrt, bias=env.eps[:, 0:1]).then_inc(rooted, 1)

    def dve_scale(dve):
        dve.wait_ge(rooted, 1)
        dve.reciprocal(rs[:], rt[:]).then_inc(inverted, 1)
        dve.wait_ge(inverted, 1)
        for k in range(KT):
            dve.scalar_tensor_tensor(out=sq[:, k], in0=x[:, k], scalar=env.col(gain, k), in1=rs[:],
                                     op0=ALU.mult, op1=ALU.mult).then_inc(scaled, 1)

    def act_hi(act):
        for k in range(KT):
            act.wait_ge(scaled, k + 1)
            act.activation(h_hi[:, k], sq[:, k], ACT.Copy).then_inc(hi_done, 1)

    def dve_lo(dve):
        for k in range(KT):
            dve.wait_ge(hi_done, k + 1)
            dve.tensor_tensor(h_lo[:, k], sq[:, k], h_hi[:, k].bitcast(F32), ALU.subtract).then_inc(lo_done, 1)

    def pe_ready(pe):
        pe.wait_ge(hi_done, KT)
        pe.wait_ge(lo_done, KT)

    return h_hi, h_lo, act_square, pe_mean, act_root, dve_scale, act_hi, dve_lo, pe_ready


def ffn_stage(nc, env, layer, tag, gain, w_in, w_out):
    with Stage(nc, tag) as st:
        KP = FT // 2
        wi = w_in[layer].rearrange("(k p) c -> p k c", p=P)
        wo = w_out[layer].rearrange("(k p) c -> p k c", p=P)
        pieces, halves = [], []
        for it in range(FT // 2):
            for part in range(2):
                c0 = part * FF + it * 2 * P
                pieces.append([((KT, 0, 2 * P), wi[:, :, c0:c0 + 2 * P])])
            for off in range(2):
                halves += [(2 * it, off * P, P, KT), (2 * it + 1, off * P, P, KT)]
        for c in range(KT // 2):
            for kh in range(2):
                halves += [(len(pieces), off * P, P, KP) for off in range(2)]
                pieces.append([((KP, 0, 2 * P), wo[:, kh * KP:(kh + 1) * KP, c * 2 * P:(c + 1) * 2 * P])])
        ws = Stream(st, KP, pieces, halves)
        h_hi, h_lo, act_square, pe_mean, act_root, dve_scale, act_hi, dve_lo, pe_ready = normed_input(st, env, gain, 7)
        g_hi = st.sb("hid_hi", [P, FT, N], F32R)
        g_lo = st.sb("hid_lo", [P, FT, N], F32R)
        sg = st.sb("silu_gate", [P, 2, N])
        hid = st.sb("hidden", [P, 2, N])
        silu_done, hid_done = st.sem("silu_done"), st.sem("hidden_done")
        ghi_done, glo_done, x_added = st.sem("hid_hi_done"), st.sem("hid_lo_done"), st.sem("x_added")
        IN = 2 * FT
        OUT = len(halves)

        with nc.Block() as block:
            @block.sync
            def _(sp):
                for p in range(len(pieces)):
                    ws.load(sp, p)

            @block.gpsimd
            def _(pool):
                for n in range(0, OUT, 2):
                    ws.split_lo(pool, n)

            @block.scalar
            def _(act):
                act_square(act)
                for n in range(4):
                    ws.split_hi(act, n)
                act_root(act)
                act_hi(act)

                def silu(m):
                    act.wait_ge(ws.used, 2 * m + 1)
                    if m >= 2:
                        act.wait_ge(hid_done, m - 1)
                    act.activation(sg[:, m % 2], env.ps[:, (2 * m) % 4, 0:N], ACT.Silu).then_inc(silu_done, 1)

                def hidden_hi(m):
                    act.wait_ge(hid_done, m + 1)
                    act.activation(g_hi[:, m], hid[:, m % 2], ACT.Copy).then_inc(ghi_done, 1)

                for m in range(FT):
                    ws.split_hi(act, 2 * m + 4)
                    silu(m)
                    ws.split_hi(act, 2 * m + 5)
                    if m:
                        hidden_hi(m - 1)
                hidden_hi(FT - 1)
                for n in range(IN + 4, OUT):
                    ws.split_hi(act, n)

            @block.vector
            def _(dve):
                ws.split_lo(dve, 1)
                ws.split_lo(dve, 3)
                dve_scale(dve)
                dve_lo(dve)

                def hidden(m):
                    dve.wait_ge(silu_done, m + 1)
                    dve.wait_ge(ws.used, 2 * m + 2)
                    if m >= 2:
                        dve.wait_ge(ghi_done, m - 1)
                        dve.wait_ge(glo_done, m - 1)
                    dve.tensor_tensor(hid[:, m % 2], sg[:, m % 2], env.ps[:, (2 * m + 1) % 4, 0:N],
                                      ALU.mult).then_inc(hid_done, 1)

                def hidden_lo(m):
                    dve.wait_ge(ghi_done, m + 1)
                    dve.tensor_tensor(g_lo[:, m], hid[:, m % 2], g_hi[:, m].bitcast(F32),
                                      ALU.subtract).then_inc(glo_done, 1)

                for m in range(FT):
                    hidden(m)
                    ws.split_lo(dve, 2 * m + 5)
                    if m:
                        hidden_lo(m - 1)
                hidden_lo(FT - 1)
                for mt in range(KT):
                    c, off = mt // 2, mt % 2
                    n = IN + 4 * c + 2 + off
                    if off == 0:
                        ws.split_lo(dve, n + 3)
                        ws.split_lo(dve, n + 5)
                    dve.wait_ge(ws.used, n + 1)
                    dve.scalar_tensor_tensor(out=env.x[:, mt], in0=env.ps[:, mt % 4, 0:N], scalar=0.5, in1=env.x[:, mt],
                                             op0=ALU.mult, op1=ALU.add).then_inc(x_added, 1)

            @block.tensor
            def _(pe):
                pe_mean(pe)
                pe_ready(pe)
                for n in range(IN):
                    m = n // 2
                    if m >= 2:
                        pe.wait_ge(hid_done, m - 1)
                    ws.product(pe, n, env.ps[:, n % 4, 0:N], h_hi, h_lo)
                pe.wait_ge(ghi_done, FT)
                pe.wait_ge(glo_done, FT)
                for n in range(IN, OUT):
                    c, kh, off = (n - IN) // 4, (n - IN) // 2 % 2, n % 2
                    mt = 2 * c + off
                    if mt >= 4 and kh == 0:
                        pe.wait_ge(x_added, mt - 3)
                    ws.product(pe, n, env.ps[:, mt % 4, 0:N], g_hi[:, kh * KP:(kh + 1) * KP],
                               g_lo[:, kh * KP:(kh + 1) * KP], start=kh == 0, stop=kh == 1)


def load_stage(nc, env, d):
    with Stage(nc, "load") as st:
        xp = st.sb("x_rows", [P, 2, D])
        xs = st.sb("x_sample_rows", [NS, D])
        cst_in, rows_in, turned = st.sem("cst_in"), st.sem("rows_in"), st.sem("x_turned")
        eps_set, copied = st.sem("eps_set"), st.sem("x_copied")
        with nc.Block() as block:
            @block.sync
            def _(sp):
                sp.dma_start(env.cst[:], d["cst"]).then_inc(cst_in, 16)
                sp.dma_start(xp[:], d["x_prompt"][0].rearrange("(a p) f -> p a f", p=P)).then_inc(rows_in, 16)
                sp.dma_start(xs[:], d["x_sample"].rearrange("b a f -> (b a) f")).then_inc(rows_in, 16)

            @block.gpsimd
            def _(pool):
                for i, v in enumerate((NORM_EPS, GN_EPS, 1.0)):
                    pool.memset(env.eps[:, i:i + 1], v).then_inc(eps_set, 1)

            @block.tensor
            def _(pe):
                pe.wait_ge(cst_in, 16)
                pe.wait_ge(rows_in, 32)
                for k in range(KT):
                    for a in range(2):
                        pe.transpose(env.ps[:, k, a * P:(a + 1) * P], xp[:, a, k * P:(k + 1) * P], env.const("ident"))
                    pe.transpose(env.ps[:, k, T:N], xs[:, k * P:(k + 1) * P],
                                 env.const("ident")[0:NS, 0:NS]).then_inc(turned, 1)

            @block.vector
            def _(dve):
                for k in range(KT):
                    dve.wait_ge(turned, k + 1)
                    dve.tensor_copy(env.x[:, k], env.ps[:, k, 0:N]).then_inc(copied, 1)


def vector_stage(nc, env, layer, d):
    with Stage(nc, "vec") as st:
        rows = st.sb("vector_rows", [P, 2, P])
        shift = st.sb("shift_rows", [NS, XT * P])
        scb = st.sb("sc_rows", [2 * NS, SC])
        conv = st.sb("conv_rows", [3 * NS, D])
        zeroed, landed = st.sem("rows_zeroed"), st.sem("rows_landed")
        turned, copied, derived = st.sem("rows_turned"), st.sem("cols_copied"), st.sem("cols_derived")
        a_done = st.sem("ssm_a_done")
        loads = []
        for which, group in ((0, ROWS_A), (1, ROWS_B)):
            for name, n in group:
                src = d[name][layer]
                at = COL[name] - which * P
                if name in ("rwkv_r_k", "sc_conv_w", "ssm_conv_w"):
                    src = src.rearrange("a b -> (a b)")
                full = n if name != "rwkv_mu" else n - 1
                loads.append((rows[at:at + full, which, :], src[0:full * P].rearrange("(r f) -> r f", f=P)))
                if full < n:
                    loads.append((rows[at + full:at + n, which, 0:RWKV_PROJ - full * P],
                                  src[full * P:RWKV_PROJ].rearrange("(r f) -> r f", r=1)))
        loads.append((shift[:, 0:RWKV_PROJ], d["state_rwkv_shift"][layer]))
        loads.append((scb[:], d["state_sc_buf"][layer].rearrange("b j f -> (b j) f")))
        loads.append((conv[:], d["state_ssm_conv"][layer].rearrange("b j f -> (b j) f")))
        for i, name in enumerate(("ssm_dt_bias", "ssm_A_log", "ssm_D")):
            loads.append((env.heads[:, i:i + 1], d[name][layer].rearrange("(h o) -> h o", o=1)))
        ps = env.ps
        nb = sum(n for _, n in ROWS_B)
        with nc.Block() as block:
            @block.gpsimd
            def _(pool):
                pool.memset(rows[:], 0.0).then_inc(zeroed, 1)
                pool.memset(shift[:, RWKV_PROJ:XT * P], 0.0).then_inc(zeroed, 1)

            @block.sync
            def _(sp):
                sp.wait_ge(zeroed, 2)
                for dst, src in loads[0::2]:
                    sp.dma_start(dst, src).then_inc(landed, 16)

            @block.scalar
            def _(act):
                act.wait_ge(zeroed, 2)
                for dst, src in loads[1::2]:
                    act.dma_start(dst, src).then_inc(landed, 16)
                act.wait_ge(landed, 16 * len(loads))
                act.activation(env.heads[:, 3:4], env.heads[:, 1:2], ACT.Exp).then_inc(a_done, 1)

            @block.tensor
            def _(pe):
                ident = env.const("ident")
                pe.wait_ge(landed, 16 * len(loads))
                pe.transpose(ps[:, 0, 0:P], rows[:, 0, :], ident)
                pe.transpose(ps[:, 0, P:P + nb], rows[0:nb, 1, :], ident[0:nb, 0:nb])
                for m in range(XT):
                    pe.transpose(ps[:, 1, m * NS:(m + 1) * NS], shift[:, m * P:(m + 1) * P], ident[0:NS, 0:NS])
                for m in range(ST):
                    pe.transpose(ps[:, 2, m * 16:(m + 1) * 16], scb[:, m * P:(m + 1) * P], ident[0:16, 0:16])
                for m in range(8):
                    pe.transpose(ps[:, 3, m * 24:(m + 1) * 24], conv[:, m * P:(m + 1) * P], ident[0:24, 0:24])
                for m in range(4):
                    mm = pe.matmul(ps[:, 4, m:m + 1], env.const("pair8")[0:8, m * P:(m + 1) * P], env.heads[:, 2:3],
                                   start=True, stop=True)
                mm.then_inc(turned, 1)

            @block.vector
            def _(dve):
                dve.wait_ge(turned, 1)
                dve.tensor_copy(env.cols[:, 0:P + nb], ps[:, 0, 0:P + nb]).then_inc(copied, 1)
                dve.tensor_copy(env.shift[:], ps[:, 1, 0:XT * NS].rearrange("p (m b) -> p m b", b=NS)).then_inc(copied, 1)
                dve.tensor_copy(env.scb[:], ps[:, 2, 0:64].rearrange("p (m j) -> p m j", m=ST)).then_inc(copied, 1)
                dve.tensor_copy(env.conv[:], ps[:, 3, 0:192].rearrange("p (m j) -> p m j", m=8)).then_inc(copied, 1)
                dve.tensor_copy(env.dcol[:], ps[:, 4, 0:4]).then_inc(copied, 1)
                dve.wait_ge(copied, 5)
                dve.tensor_scalar(env.omu[:], env.col("rwkv_mu", 0, XT), -1.0, 1.0, ALU.mult, ALU.add).then_inc(derived, 1)
                dve.tensor_scalar(env.oka[:], env.col("rwkv_k_a", 0, RT), -1.0, 1.0, ALU.mult, ALU.add).then_inc(derived, 1)
                dve.wait_ge(a_done, 1)
                dve.tensor_scalar(env.heads[:, 4:5], env.heads[:, 3:4], -1.0, None, ALU.mult).then_inc(derived, 1)


def final_stage(nc, env, d):
    with Stage(nc, "fin") as st:
        sq, rt, rs = st.sb("fin_sq", [P, KT, N]), st.sb("fin_root", [P, N]), st.sb("fin_rs", [P, N])
        rows, gain = st.sb("gain_rows", [KT, P]), st.sb("gain_cols", [P, KT])
        yp, ys = st.sb("y_rows", [P, 2, D]), st.sb("y_sample_rows", [NS, D])
        squared, summed, rooted, gain_in = st.sem("squared"), st.sem("summed"), st.sem("rooted"), st.sem("gain_in")
        gain_turned, ready, scaled = st.sem("gain_turned"), st.sem("rs_ready"), st.sem("y_scaled")
        turned, copied, stored = st.sem("y_turned"), st.sem("y_copied"), st.sem("y_stored")
        ps = env.ps
        with nc.Block() as block:
            @block.sync
            def _(sp):
                sp.dma_start(rows[:], d["norm_final"].rearrange("(r f) -> r f", f=P)).then_inc(gain_in, 16)
                sp.wait_ge(copied, KT)
                sp.dma_start(d["y_prompt"][0].rearrange("(a p) f -> p a f", p=P), yp[:]).then_inc(stored, 16)
                sp.dma_start(d["y_sample"].rearrange("b a f -> (b a) f"), ys[:]).then_inc(stored, 16)
                sp.wait_ge(stored, 32)

            @block.scalar
            def _(act):
                act.activation(sq[:], env.x[:], ACT.Square).then_inc(squared, 1)
                act.wait_ge(summed, 1)
                act.activation(rt[:], ps[:, 6, 0:N], ACT.Sqrt, bias=env.eps[:, 0:1]).then_inc(rooted, 1)

            @block.tensor
            def _(pe):
                ident = env.const("ident")
                pe.wait_ge(gain_in, 16)
                pe.transpose(ps[:, 7, 0:KT], rows[:], ident[0:KT, 0:KT]).then_inc(gain_turned, 1)
                pe.wait_ge(squared, 1)
                for k in range(KT):
                    mm = pe.matmul(ps[:, 6, 0:N], env.const("mean"), sq[:, k], start=k == 0, stop=k == KT - 1)
                mm.then_inc(summed, 1)
                for k in range(KT):
                    pe.wait_ge(scaled, k + 1)
                    if k >= 2:
                        pe.wait_ge(copied, k - 1)
                    b = 3 * (k % 2)
                    for a in range(2):
                        pe.transpose(ps[:, b + a, 0:P], sq[:, k, a * P:(a + 1) * P], ident)
                    pe.transpose(ps[0:NS, b + 2, 0:P], sq[:, k, T:N], ident).then_inc(turned, 1)

            @block.vector
            def _(dve):
                dve.wait_ge(gain_turned, 1)
                dve.tensor_copy(gain[:], ps[:, 7, 0:KT]).then_inc(ready, 1)
                dve.wait_ge(rooted, 1)
                dve.reciprocal(rs[:], rt[:]).then_inc(ready, 1)
                dve.wait_ge(ready, 2)
                for k in range(KT):
                    dve.scalar_tensor_tensor(out=sq[:, k], in0=env.x[:, k], scalar=gain[:, k:k + 1], in1=rs[:],
                                             op0=ALU.mult, op1=ALU.mult).then_inc(scaled, 1)
                for k in range(KT):
                    dve.wait_ge(turned, k + 1)
                    b = 3 * (k % 2)
                    dve.tensor_copy(yp[:, :, k * P:(k + 1) * P], ps[:, b:b + 2, 0:P])
                    dve.tensor_copy(ys[:, k * P:(k + 1) * P], ps[0:NS, b + 2, 0:P]).then_inc(copied, 1)


def projection_stage(nc, env, mix, layer, d):
    with Stage(nc, "proj") as st:
        w = d["w_in"][layer].rearrange("(k p) c -> p k c", p=P)
        pieces, halves, tiles = [], [], []

        def add(c0, widths, kinds):
            for i, (wd, kind) in enumerate(zip(widths, kinds)):
                halves.append((len(pieces), sum(widths[:i]), wd, KT))
                tiles.append(kind)

        for m in range(0, XT - 1, 2):
            add(m * P, (P, P), (("rwkv", m), ("rwkv", m + 1)))
            pieces.append([((KT, 0, 2 * P), w[:, :, m * P:(m + 2) * P])])
        add(0, (32, 8), (("rwkv", XT - 1), ("dt", 0)))
        pieces.append([((KT, 0, 32), w[:, :, RWKV_PROJ - 32:RWKV_PROJ]), ((KT, 32, 8), w[:, :, IN_COLS - 8:IN_COLS])])
        for m in range(0, 24, 2):
            c0 = RWKV_PROJ + m * P
            kind = "sc" if m < 12 else ("z" if m < 16 else "xbc")
            add(c0, (P, P), ((kind, m), (kind, m + 1)))
            pieces.append([((KT, 0, 2 * P), w[:, :, c0:c0 + 2 * P])])
        ws = Stream(st, KT, pieces, halves)
        h_hi, h_lo, act_square, pe_mean, act_root, dve_scale, act_hi, dve_lo, pe_ready = normed_input(
            st, env, "norm_mix", 7)
        prev = st.sb("prev", [P, 2, 1 + N])
        shift_mu = st.sb("shift_mu", [P, XT, NS])
        zeroed, prev_in, act_read = st.sem("zeroed"), st.sem("prev_in"), st.sem("act_read")
        last_in, shifted, mu_done = st.sem("last_in"), st.sem("shifted"), st.sem("shift_mu_done")
        H = len(halves)
        ps = env.ps

        with nc.Block() as block:
            @block.sync
            def _(sp):
                for p in range(len(pieces)):
                    ws.load(sp, p)

            @block.gpsimd
            def _(pool):
                pool.memset(prev[:, :, 0:1], 0.0).then_inc(zeroed, 1)
                pool.memset(mix.xs[:, XT - 1], 0.0).then_inc(zeroed, 1)
                pool.memset(mix.last[:, XT - 1], 0.0).then_inc(zeroed, 1)
                pool.memset(mix.xbc[:, :, 0:3], 0.0).then_inc(zeroed, 1)
                for n in range(0, H, 2):
                    ws.split_lo(pool, n)

            @block.scalar
            def _(act):
                act_square(act)
                for n in range(4):
                    ws.split_hi(act, n)
                act_root(act)
                act_hi(act)
                act.wait_ge(zeroed, 4)
                for n, (kind, m) in enumerate(tiles):
                    ws.split_hi(act, n + 4)
                    act.wait_ge(ws.used, n + 1)
                    bank, r = ps[:, n % 4, 0:N], halves[n][2]
                    if kind == "rwkv":
                        if m >= 2:
                            act.wait_ge(shifted, m - 1)
                            act.wait_ge(last_in, m - 1)
                        act.activation(prev[0:r, m % 2, 1:1 + N], bank[0:r], ACT.Copy).then_inc(prev_in, 1)
                        act.activation(mix.xs[0:r, m], bank[0:r], ACT.Copy,
                                       scale=env.omu[0:r, m:m + 1]).then_inc(act_read, 1)
                    else:
                        dst = {"dt": lambda: mix.dt[:], "sc": lambda: mix.sc[:, m], "z": lambda: mix.z[:, m - 12],
                               "xbc": lambda: mix.xbc[:, m - 16, 3:3 + N]}[kind]()
                        act.activation(dst, bank[0:r], ACT.Copy).then_inc(act_read, 1)

            @block.vector
            def _(dve):
                ws.split_lo(dve, 1)
                ws.split_lo(dve, 3)
                dve_scale(dve)
                dve_lo(dve)
                dve.wait_ge(zeroed, 4)
                for n, (kind, m) in enumerate(tiles):
                    r = halves[n][2]
                    if kind == "rwkv":
                        dve.wait_ge(prev_in, m + 1)
                        dve.tensor_copy(mix.last[0:r, m], prev[0:r, m % 2, T:T + 9]).then_inc(last_in, 1)
                        dve.wait_ge(act_read, n + 1)
                        dve.scalar_tensor_tensor(out=mix.xs[0:r, m, 0:T], in0=prev[0:r, m % 2, 0:T],
                                                 scalar=env.col("rwkv_mu", m)[0:r], in1=mix.xs[0:r, m, 0:T],
                                                 op0=ALU.mult, op1=ALU.add).then_inc(shifted, 1)
                    if n % 2 == 0:
                        ws.split_lo(dve, n + 5)
                mu = env.col("rwkv_mu", 0, XT).unsqueeze(2).to_broadcast([P, XT, NS])
                dve.tensor_tensor(shift_mu[:], env.shift[:], mu, ALU.mult).then_inc(mu_done, 1)
                dve.wait_ge(mu_done, 1)
                dve.wait_ge(shifted, XT)
                dve.tensor_tensor(mix.xs[:, :, T:N], mix.xs[:, :, T:N], shift_mu[:], ALU.add).then_inc(shifted, 1)

            @block.tensor
            def _(pe):
                pe_mean(pe)
                pe_ready(pe)
                for n in range(H):
                    if n >= 4:
                        pe.wait_ge(act_read, n - 3)
                    ws.product(pe, n, ps[0:halves[n][2], n % 4, 0:N], h_hi, h_lo)


def causal_conv(dve, st, name, dst, src, state, taps, m, width, after):
    s = st.s(name)
    base = after
    for j in range(width):
        last_of_samples = src[:, width - 1 + T:width - 1 + N]
        smp = state[:, :, j] if j < width - 1 else last_of_samples
        for out, x in ((dst[:, 0:T], src[:, j:j + T]), (dst[:, T:N], smp)):
            if j == 0:
                dve.tensor_scalar(out, x, taps(j), None, ALU.mult).then_inc(s, 1)
            else:
                dve.scalar_tensor_tensor(out=out, in0=x, scalar=taps(j), in1=out, op0=ALU.mult,
                                         op1=ALU.add).then_inc(s, 1)
        base += 2
        if j < width - 1:
            dve.wait_ge(s, base)
    return base


def short_mixers_stage(nc, env, mix, layer, d):
    with Stage(nc, "ssm") as st:
        s, ps = st.s, env.ps
        ident, ones, mean = env.const("ident"), env.const("ones"), env.const("mean")
        neg, row8, pair8 = env.const("neg"), env.const("row8"), env.const("pair8")
        u = st.sb("gated", [P, ST, 2 + N])
        acc = st.sb("sc_conv", [P, ST, N])
        sq = st.sb("squares", [P, ST, N])
        root, rs = st.sb("root", [P, 2, N]), st.sb("rs", [P, 2, N])
        xa = st.sb("xbc_conv", [P, 8, N])
        dv, da = st.sb("dt_abs", [8, N]), st.sb("dt_a", [8, N])
        one_row, cum = st.sb("one_row", [8, T]), st.sb("cum", [8, T])
        das = st.sb("dt_sample", [8, 2 * NS])
        tok = st.sb("tok_cum_dt", [P, 4, 8])
        lastc, dend = st.sb("cum_last", [P, 8]), st.sb("decay_end", [P, 2, 8])
        xdt, xde = st.sb("xdt", [P, 2, 8, HS]), st.sb("xdt_end", [P, 2, 8, HS])
        btok = st.sb("b_tok", [P, 2, 2, P])
        seg, score = st.sb("segments", [P, 2, 384]), st.sb("scores", [P, 2, 384])
        hst = st.sb("sample_state", [P, 4, NS, P])
        outer = st.sb("outer", [P, NS, P])
        diag = st.sb("diag", [P, NS, P])
        spread, xs_dt = st.sb("spread", [P, 4, 2 * NS]), st.sb("sample_xdt", [P, 4, NS])
        ym, hfin = st.sb("y_ssm", [P, 4, N]), st.sb("p_state", [P, 4, P])
        scn, cvn = st.sb("sc_new", [P, ST, 18]), st.sb("conv_new", [P, 8, 27])
        sc_rows, cv_rows = st.sb("sc_new_rows", [18, SC]), st.sb("conv_new_rows", [27, D])
        sh_rows = st.sb("shift_new_rows", [9, XT * P])
        hs_in = d["state_ssm"][layer].rearrange("b (m h) p n -> m (h p) b n", h=2)
        hs_out = d["s_ssm"][layer].rearrange("b (m h) p n -> m (h p) b n", h=2)
        stores = []

        with nc.Block() as block:
            @block.sync
            def _(sp):
                for m in range(4):
                    sp.dma_start(hst[:, m], hs_in[m]).then_inc(s("state_in"), 16)

                def store(dst, src):
                    sp.dma_start(dst, src).then_inc(s("stored"), 16)
                    stores.append(1)

                sp.wait_ge(s("hfin_done"), 1)
                store(d["p_ssm"][layer, 0].rearrange("(m h) p n -> (h p) m n", h=2), hfin[:])
                for m in range(4):
                    sp.wait_ge(s("hst_done"), m + 1)
                    store(hs_out[m], hst[:, m])
                sp.wait_ge(s("rows_done"), 3)
                store(d["p_sc"][layer, 0], sc_rows[0:2, :])
                store(d["s_sc"][layer].rearrange("b j f -> (b j) f"), sc_rows[2:18, :])
                store(d["p_conv"][layer, 0], cv_rows[0:3, :])
                store(d["s_conv"][layer].rearrange("b j f -> (b j) f"), cv_rows[3:27, :])
                sp.wait_ge(s("shift_rows_done"), 7)
                store(d["p_shift"][layer], sh_rows[0:1, 0:RWKV_PROJ])
                store(d["s_shift"][layer], sh_rows[1:9, 0:RWKV_PROJ])
                sp.wait_ge(s("stored"), 16 * len(stores))

            @block.gpsimd
            def _(pool):
                pool.memset(u[:, :, 0:2], 0.0).then_inc(s("u_zero"), 1)
                pool.memset(one_row[:], 1.0).then_inc(s("one_row"), 1)
                pool.wait_ge(s("spread_in"), 1)
                pool.wait_ge(s("state_in"), 64)
                for m in range(4):
                    dec = spread[:, m, 0:NS].unsqueeze(2).to_broadcast([P, NS, P])
                    pool.tensor_tensor(hst[:, m], hst[:, m], dec, ALU.mult).then_inc(s("hst_decayed"), 1)

            @block.scalar
            def _(act):
                for i in range(8):
                    act.wait_ge(s("xconv"), 8 * (i + 1))
                    act.activation(xa[:, i], xa[:, i], ACT.Silu, bias=env.col("ssm_conv_b", i)).then_inc(s("xa_done"), 1)
                act.activation(mix.z[:], mix.z[:], ACT.Silu).then_inc(s("z_silu"), 1)
                act.wait_ge(s("dt_step"), 2)
                act.activation(da[:], dv[:], ACT.Exp, scale=-1.0).then_inc(s("dt_act"), 1)
                act.wait_ge(s("dt_act"), 1)
                act.activation(dv[:], da[:], ACT.Ln, bias=env.eps[0:8, 2:3]).then_inc(s("dt_act"), 1)
                act.wait_ge(s("dt_step"), 4)
                act.activation(das[:, 0:NS], da[:, T:N], ACT.Exp).then_inc(s("das_exp"), 1)
                for h in range(8):
                    act.wait_ge(s("seg_done"), 2 * h + 2)
                    act.activation(seg[:, h % 2], seg[:, h % 2], ACT.Exp).then_inc(s("seg_exp"), 1)
                act.wait_ge(s("dend_sub"), 1)
                act.activation(dend[:], dend[:], ACT.Exp).then_inc(s("dend_exp"), 1)
                act.wait_ge(s("hfin_ps"), 1)
                act.activation(hfin[:], ps[:, 3, :].rearrange("p (m n) -> p m n", m=4), ACT.Copy).then_inc(s("hfin_done"), 1)
                act.wait_ge(s("sc_gated"), 1)
                act.activation(sq[:], acc[:], ACT.Square).then_inc(s("sc_sq"), 1)
                act.wait_ge(s("sc_ms"), 1)
                act.activation(root[:, 0], ps[:, 0, 0:N], ACT.Sqrt, bias=env.eps[:, 0:1], scale=D / SC).then_inc(s("sc_root"), 1)
                for i in range(ST):
                    act.wait_ge(s("sc_scaled"), i + 1)
                    act.activation(mix.ys_hi[:, i], acc[:, i], ACT.Copy).then_inc(s("sc_hi"), 1)
                act.wait_ge(s("y_gated"), 1)
                act.wait_ge(s("sc_ms"), 1)
                act.activation(sq[:], ym[:], ACT.Square).then_inc(s("ssm_sq"), 1)
                for g in range(2):
                    act.wait_ge(s("ssm_ms"), g + 1)
                    act.wait_ge(s("sc_inv"), 1)
                    act.activation(root[:, g], ps[:, 4 + g, 0:N], ACT.Sqrt, bias=env.eps[:, 0:1],
                                   scale=D / 256).then_inc(s("ssm_root"), 1)
                for m in range(4):
                    act.wait_ge(s("ssm_scaled"), m + 1)
                    act.activation(mix.ys_hi[:, ST + m], ym[:, m], ACT.Copy).then_inc(s("ssm_hi"), 1)

            @block.vector
            def _(dve):
                n = 0
                for i in range(8):
                    n = causal_conv(dve, st, "xconv", xa[:, i], mix.xbc[:, i],
                                    env.conv[:, i].rearrange("p (b j) -> p b j", j=3),
                                    lambda j: env.col("ssm_conv_w", 8 * j + i), i, 4, n)
                dve.tensor_scalar(mix.dt[:], mix.dt[:], env.heads[:, 0:1], None, ALU.add).then_inc(s("dt_step"), 1)
                dve.wait_ge(s("dt_step"), 1)
                dve.scalar_tensor_tensor(out=dv[:], in0=mix.dt[:], scalar=-1.0, in1=mix.dt[:], op0=ALU.mult,
                                         op1=ALU.max).then_inc(s("dt_step"), 1)
                dve.wait_ge(s("dt_act"), 2)
                dve.scalar_tensor_tensor(out=mix.dt[:], in0=mix.dt[:], scalar=0.0, in1=dv[:], op0=ALU.max,
                                         op1=ALU.add).then_inc(s("dt_step"), 1)
                dve.wait_ge(s("dt_step"), 3)
                dve.tensor_scalar(da[:], mix.dt[:], env.heads[:, 4:5], None, ALU.mult).then_inc(s("dt_step"), 1)
                dve.wait_ge(s("dt_step"), 4)
                dve.wait_ge(s("one_row"), 1)
                dve.tensor_tensor_scan(cum[:], one_row[:], da[:, 0:T], 0.0, ALU.mult, ALU.add).then_inc(s("cum_done"), 1)
                dve.tensor_copy(das[:, NS:2 * NS], mix.dt[:, T:N]).then_inc(s("das_dt"), 1)
                dve.wait_ge(s("tok_ps"), 1)
                dve.tensor_copy(tok[:], ps[:, 4, 0:32].rearrange("p (a h) -> p a h", a=4)).then_inc(s("tok_in"), 1)
                dve.wait_ge(s("tok_in"), 1)
                dve.wait_ge(s("xtok_ps"), 1)
                for c in range(2):
                    dve.tensor_tensor(xdt[:, c], ps[:, 1 + c, :].rearrange("p (h e) -> p h e", h=8),
                                      tok[:, 2 + c].unsqueeze(2).to_broadcast([P, 8, HS]), ALU.mult).then_inc(s("xdt_done"), 1)
                dve.tensor_copy(btok[:].rearrange("p c g n -> p (c g n)"), ps[:, 3, :]).then_inc(s("btok_done"), 1)
                for h in range(8):
                    g, b = h // 4, 7 if h % 2 else 0
                    dve.wait_ge(s("row_ps"), h + 1)
                    dve.scalar_tensor_tensor(out=seg[:, h % 2, 0:T], in0=ps[:, b, 0:T], scalar=tok[:, 0, h:h + 1],
                                             in1=neg[:, 0:T], op0=ALU.subtract, op1=ALU.add).then_inc(s("seg_done"), 1)
                    dve.scalar_tensor_tensor(out=seg[:, h % 2, T:384], in0=ps[:, b, P:T], scalar=tok[:, 1, h:h + 1],
                                             in1=neg[:, T:384], op0=ALU.subtract, op1=ALU.add).then_inc(s("seg_done"), 1)
                    dve.tensor_copy(lastc[:, h:h + 1], ps[:, b, T - 1:T]).then_inc(s("row_read"), 1)
                    dve.wait_ge(s("seg_exp"), h + 1)
                    if h >= 2:
                        dve.wait_ge(s("y_ps"), h - 1)
                    if h == 0:
                        dve.wait_ge(s("g_ps"), 1)
                    dve.tensor_tensor(score[:, h % 2], ps[:, 5 + g, 0:384], seg[:, h % 2], ALU.mult).then_inc(s("score_done"), 1)
                dve.wait_ge(s("row_read"), 8)
                dve.tensor_tensor(dend[:], lastc[:].unsqueeze(1).to_broadcast([P, 2, 8]), tok[:, 0:2],
                                  ALU.subtract).then_inc(s("dend_sub"), 1)
                dve.wait_ge(s("dend_exp"), 1)
                dve.wait_ge(s("xdt_done"), 2)
                for c in range(2):
                    dve.tensor_tensor(xde[:, c], xdt[:, c], dend[:, c].unsqueeze(2).to_broadcast([P, 8, HS]),
                                      ALU.mult).then_inc(s("xde_done"), 1)
                for m in range(4):
                    dve.wait_ge(s("y_ps"), 4 * (m // 2) + 4)
                    dve.scalar_tensor_tensor(out=ym[:, m, 0:T], in0=xa[:, m, 0:T], scalar=env.dcol[:, m:m + 1],
                                             in1=ps[:, 1 + m // 2, (m % 2) * T:(m % 2) * T + T], op0=ALU.mult,
                                             op1=ALU.add).then_inc(s("y_done"), 1)
                dve.wait_ge(s("spread_ps"), 1)
                dve.tensor_copy(spread[:], ps[:, 4, 0:64].rearrange("p (m e) -> p m e", m=4)).then_inc(s("spread_in"), 1)
                dve.wait_ge(s("spread_in"), 1)
                dve.tensor_tensor(xs_dt[:], xa[:, 0:4, T:N], spread[:, :, NS:2 * NS], ALU.mult).then_inc(s("xs_dt"), 1)
                dve.wait_ge(s("xs_dt"), 1)
                for v in range(4):
                    g, bc = v // 2, v % 2
                    if v:
                        dve.wait_ge(s("bc_ps"), v)
                    dve.tensor_tensor(diag[:], ident.unsqueeze(1).to_broadcast([P, NS, P]),
                                      xa[:, 4 + 2 * bc + g, T:N].unsqueeze(2).to_broadcast([P, NS, P]),
                                      ALU.mult).then_inc(s("diag_done"), 1)
                    if bc == 0:
                        continue
                    dve.wait_ge(s("bc_ps"), 2 * g + 2)
                    for m in (2 * g, 2 * g + 1):
                        k = 3 * m
                        brow = ps[:, 5:7, :].rearrange("p a (b n) -> p (a b) n", n=P)
                        dve.wait_ge(s("smp"), k)
                        dve.tensor_tensor(outer[:], brow, xs_dt[:, m].unsqueeze(2).to_broadcast([P, NS, P]),
                                          ALU.mult).then_inc(s("smp"), 1)
                        dve.wait_ge(s("smp"), k + 1)
                        dve.wait_ge(s("hst_decayed"), m + 1)
                        dve.tensor_tensor(hst[:, m], hst[:, m], outer[:], ALU.add).then_inc(s("hst_done"), 1)
                        dve.wait_ge(s("hst_done"), m + 1)
                        for half in range(2):
                            crow = ps[:, 7 if half else 0, :].rearrange("p (b n) -> p b n", n=P)
                            dve.tensor_tensor(outer[:, 4 * half:4 * half + 4], hst[:, m, 4 * half:4 * half + 4], crow,
                                              ALU.mult).then_inc(s("smp_c"), 1)
                        dve.wait_ge(s("smp_c"), 2 * m + 2)
                        dve.tensor_reduce(ym[:, m, T:N], outer[:], AX.X, ALU.add).then_inc(s("smp"), 1)
                        dve.wait_ge(s("smp"), k + 2)
                        dve.scalar_tensor_tensor(out=ym[:, m, T:N], in0=xa[:, m, T:N], scalar=env.dcol[:, m:m + 1],
                                                 in1=ym[:, m, T:N], op0=ALU.mult, op1=ALU.add).then_inc(s("smp"), 1)
                dve.wait_ge(s("smp"), 12)
                dve.wait_ge(s("y_done"), 4)
                dve.wait_ge(s("z_silu"), 1)
                dve.tensor_tensor(ym[:], ym[:], mix.z[:], ALU.mult).then_inc(s("y_gated"), 1)
                dve.wait_ge(s("u_zero"), 1)
                dve.tensor_tensor(u[:, :, 2:2 + N], mix.sc[:, 4:8], mix.sc[:, 8:12], ALU.mult).then_inc(s("u_done"), 1)
                dve.wait_ge(s("u_done"), 1)
                n = 0
                for i in range(ST):
                    n = causal_conv(dve, st, "uconv", acc[:, i], u[:, i], env.scb[:, i].rearrange("p (b j) -> p b j", j=2),
                                    lambda j: env.col("sc_conv_w", 4 * j + i), i, 3, n)
                dve.wait_ge(s("uconv"), n)
                dve.tensor_tensor(acc[:], acc[:], mix.sc[:, 0:4], ALU.mult).then_inc(s("sc_gated"), 1)
                scb = env.scb[:].rearrange("p m (b j) -> p m b j", j=2)
                cvb = env.conv[:].rearrange("p m (b j) -> p m b j", j=3)
                scw = scn[:, :, 2:18].rearrange("p m (b j) -> p m b j", j=2)
                cvw = cvn[:, :, 3:27].rearrange("p m (b j) -> p m b j", j=3)
                dve.tensor_copy(scn[:, :, 0:2], u[:, :, T:T + 2]).then_inc(s("new_in"), 1)
                dve.tensor_copy(scw[:, :, :, 0], scb[:, :, :, 1]).then_inc(s("new_in"), 1)
                dve.tensor_copy(scw[:, :, :, 1], u[:, :, T + 2:N + 2]).then_inc(s("new_in"), 1)
                dve.tensor_copy(cvn[:, :, 0:3], mix.xbc[:, :, T:T + 3]).then_inc(s("new_in"), 1)
                dve.tensor_copy(cvw[:, :, :, 0], cvb[:, :, :, 1]).then_inc(s("new_in"), 1)
                dve.tensor_copy(cvw[:, :, :, 1], cvb[:, :, :, 2]).then_inc(s("new_in"), 1)
                dve.tensor_copy(cvw[:, :, :, 2], mix.xbc[:, :, T + 3:N + 3]).then_inc(s("new_in"), 1)
                dve.wait_ge(s("sc_root"), 1)
                dve.reciprocal(rs[:, 0], root[:, 0]).then_inc(s("sc_inv"), 1)
                dve.wait_ge(s("sc_inv"), 1)
                dve.wait_ge(s("sc_gated"), 1)
                for i in range(ST):
                    dve.scalar_tensor_tensor(out=acc[:, i], in0=acc[:, i], scalar=env.col("sc_norm", i), in1=rs[:, 0],
                                             op0=ALU.mult, op1=ALU.mult).then_inc(s("sc_scaled"), 1)
                for i in range(ST):
                    dve.wait_ge(s("sc_hi"), i + 1)
                    dve.tensor_tensor(mix.ys_lo[:, i], acc[:, i], mix.ys_hi[:, i].bitcast(F32),
                                      ALU.subtract).then_inc(s("sc_lo"), 1)
                dve.wait_ge(s("sc_scaled"), ST)
                for g in range(2):
                    dve.wait_ge(s("ssm_root"), g + 1)
                    dve.reciprocal(rs[:, g], root[:, g]).then_inc(s("ssm_inv"), 1)
                    dve.wait_ge(s("ssm_inv"), g + 1)
                    for m in (2 * g, 2 * g + 1):
                        dve.scalar_tensor_tensor(out=ym[:, m], in0=ym[:, m], scalar=env.col("ssm_norm", m), in1=rs[:, g],
                                                 op0=ALU.mult, op1=ALU.mult).then_inc(s("ssm_scaled"), 1)
                for m in range(4):
                    dve.wait_ge(s("ssm_hi"), m + 1)
                    dve.tensor_tensor(mix.ys_lo[:, ST + m], ym[:, m], mix.ys_hi[:, ST + m].bitcast(F32),
                                      ALU.subtract).then_inc(s("ssm_lo"), 1)
                dve.wait_ge(s("new_ps"), 1)
                dve.tensor_copy(sc_rows[:], ps[0:18, 1, :]).then_inc(s("rows_done"), 1)
                for a in range(2):
                    dve.tensor_copy(cv_rows[:, a * 512:(a + 1) * 512], ps[0:27, 2 + a, :]).then_inc(s("rows_done"), 1)
                for q in range(7):
                    w = min(4, XT - 4 * q) * P
                    dve.wait_ge(s("shift_ps"), q + 1)
                    dve.tensor_copy(sh_rows[:, 512 * q:512 * q + w], ps[0:9, 4 + q % 4, 0:w]).then_inc(s("shift_rows_done"), 1)

            @block.tensor
            def _(pe):
                pe.wait_ge(s("cum_done"), 1)
                for c in range(2):
                    pe.transpose(ps[:, 4, 8 * c:8 * c + 8], cum[:, c * P:(c + 1) * P], ident[0:8, 0:8])
                    mm = pe.transpose(ps[:, 4, 16 + 8 * c:24 + 8 * c], mix.dt[:, c * P:(c + 1) * P], ident[0:8, 0:8])
                mm.then_inc(s("tok_ps"), 1)
                pe.wait_ge(s("xa_done"), 8)
                for c in range(2):
                    for m in range(4):
                        pe.transpose(ps[:, 1 + c, m * P:(m + 1) * P], xa[:, m, c * P:(c + 1) * P], ident)
                    for g in range(2):
                        mm = pe.transpose(ps[:, 3, (2 * c + g) * P:(2 * c + g + 1) * P], xa[:, 4 + g, c * P:(c + 1) * P], ident)
                mm.then_inc(s("xtok_ps"), 1)
                for g in range(2):
                    pe.matmul(ps[:, 5 + g, 0:T], xa[:, 4 + g, 0:P], xa[:, 6 + g, 0:T], start=True, stop=True)
                    mm = pe.matmul(ps[:, 5 + g, T:384], xa[:, 4 + g, P:T], xa[:, 6 + g, P:T], start=True, stop=True)
                mm.then_inc(s("g_ps"), 1)

                def row(h):
                    if h >= 2:
                        pe.wait_ge(s("row_read"), h - 1)
                        pe.wait_ge(s("seg_done"), 2 * (h - 1))
                    pe.matmul(ps[:, 7 if h % 2 else 0, 0:T], row8[0:8, h * P:(h + 1) * P], cum[:], start=True,
                              stop=True).then_inc(s("row_ps"), 1)

                row(0)
                row(1)
                pe.wait_ge(s("xdt_done"), 2)
                for h in range(8):
                    if h + 2 < 8:
                        row(h + 2)
                    pe.wait_ge(s("score_done"), h + 1)
                    m, q = h // 2, (h % 2) * HS
                    y = ps[q:q + HS, 1 + m // 2, (m % 2) * T:(m % 2) * T + T]
                    pe.matmul(y, xdt[:, 0, h], score[:, h % 2, 0:T], start=True, stop=False, skip_group_check=True)
                    pe.matmul(y[:, P:T], xdt[:, 1, h], score[:, h % 2, T:384], start=False, stop=True,
                              skip_group_check=True).then_inc(s("y_ps"), 1)
                pe.wait_ge(s("das_exp"), 1)
                pe.wait_ge(s("das_dt"), 1)
                pe.wait_ge(s("tok_in"), 1)
                for m in range(4):
                    mm = pe.matmul(ps[:, 4, 16 * m:16 * m + 16], pair8[0:8, m * P:(m + 1) * P], das[:], start=True, stop=True)
                mm.then_inc(s("spread_ps"), 1)
                pe.wait_ge(s("xde_done"), 2)
                pe.wait_ge(s("btok_done"), 1)
                for m in range(4):
                    for c in range(2):
                        mm = pe.matmul(ps[:, 3, m * P:(m + 1) * P], xde[:, c, 2 * m:2 * m + 2].rearrange("p h e -> p (h e)"),
                                       btok[:, c, m // 2], start=c == 0, stop=c == 1)
                mm.then_inc(s("hfin_ps"), 1)
                for v in range(4):
                    pe.wait_ge(s("diag_done"), v + 1)
                    if v == 0:
                        pe.wait_ge(s("score_done"), 8)
                        pe.wait_ge(s("row_read"), 8)
                    if v == 2:
                        pe.wait_ge(s("smp"), 6)
                    for half in range(2):
                        b = 5 + half if v % 2 == 0 else (7 if half else 0)
                        mm = pe.matmul(ps[:, b, :], ones, diag[:, 4 * half:4 * half + 4].rearrange("p b n -> p (b n)"),
                                       start=True, stop=True)
                    mm.then_inc(s("bc_ps"), 1)
                pe.wait_ge(s("sc_sq"), 1)
                pe.wait_ge(s("smp"), 12)
                for i in range(ST):
                    mm = pe.matmul(ps[:, 0, 0:N], mean, sq[:, i], start=i == 0, stop=i == ST - 1)
                mm.then_inc(s("sc_ms"), 1)
                pe.wait_ge(s("ssm_sq"), 1)
                pe.wait_ge(s("spread_in"), 1)
                for g in range(2):
                    for i in range(2):
                        mm = pe.matmul(ps[:, 4 + g, 0:N], mean, sq[:, 2 * g + i], start=i == 0, stop=i == 1)
                    mm.then_inc(s("ssm_ms"), 1)
                pe.wait_ge(s("new_in"), 7)
                pe.wait_ge(s("y_done"), 4)
                pe.wait_ge(s("hfin_done"), 1)
                for i in range(ST):
                    pe.transpose(ps[0:18, 1, i * P:(i + 1) * P], scn[:, i], ident)
                for i in range(8):
                    mm = pe.transpose(ps[0:27, 2 + i // 4, (i % 4) * P:(i % 4 + 1) * P], cvn[:, i], ident)
                mm.then_inc(s("new_ps"), 1)
                pe.wait_ge(s("ssm_root"), 2)
                for q in range(7):
                    if q >= 4:
                        pe.wait_ge(s("shift_rows_done"), q - 3)
                    for i in range(4 * q, min(4 * q + 4, XT)):
                        mm = pe.transpose(ps[0:9, 4 + q % 4, (i % 4) * P:(i % 4 + 1) * P], mix.last[:, i], ident)
                    mm.then_inc(s("shift_ps"), 1)


def output_stage(nc, env, mix, layer, d):
    with Stage(nc, "out") as st:
        w = d["w_out"][layer].rearrange("(k p) c -> p k c", p=P)
        yr_hi = st.sb("y_rwkv_hi", [P, RT, N], F32R)
        yr_lo = st.sb("y_rwkv_lo", [P, RT, N], F32R)
        y_hi_done, y_lo_done = st.sem("y_hi_done"), st.sem("y_lo_done")
        pieces, halves = [], []
        for c in range(KT // 2):
            for kh in (1, 0):
                halves += [(len(pieces), off * P, P, KT) for off in range(2)]
                pieces.append([((KT, 0, 2 * P), w[:, kh * KT:(kh + 1) * KT, c * 2 * P:(c + 1) * 2 * P])])
        ws = Stream(st, KT, pieces, halves)
        x_added = st.sem("x_added")
        with nc.Block() as block:
            @block.sync
            def _(sp):
                for p in range(len(pieces)):
                    ws.load(sp, p)

            @block.gpsimd
            def _(pool):
                for n in range(0, len(halves), 2):
                    ws.split_lo(pool, n)

            @block.scalar
            def _(act):
                for n in range(len(halves)):
                    ws.split_hi(act, n)
                    if n < 4:
                        act.activation(yr_hi[:, 2 * n:2 * n + 2], mix.xs[:, 2 * n:2 * n + 2], ACT.Copy).then_inc(y_hi_done, 1)

            @block.vector
            def _(dve):
                ws.split_lo(dve, 1)
                for n in range(4):
                    dve.wait_ge(y_hi_done, n + 1)
                    dve.tensor_tensor(yr_lo[:, 2 * n:2 * n + 2], mix.xs[:, 2 * n:2 * n + 2],
                                      yr_hi[:, 2 * n:2 * n + 2].bitcast(F32), ALU.subtract).then_inc(y_lo_done, 1)
                for mt in range(KT):
                    n = 4 * (mt // 2) + 2 + mt % 2
                    if mt % 2 == 0:
                        ws.split_lo(dve, n + 1)
                        ws.split_lo(dve, n + 3)
                    dve.wait_ge(ws.used, n + 1)
                    dve.tensor_tensor(env.x[:, mt], env.ps[:, mt % 4, 0:N], env.x[:, mt], ALU.add).then_inc(x_added, 1)

            @block.tensor
            def _(pe):
                for n in range(len(halves)):
                    c, second, off = n // 4, n // 2 % 2, n % 2
                    mt = 2 * c + off
                    if mt >= 4 and not second:
                        pe.wait_ge(x_added, mt - 3)
                    if n == 2:
                        pe.wait_ge(y_hi_done, 4)
                        pe.wait_ge(y_lo_done, 4)
                    ws.product(pe, n, env.ps[:, mt % 4, 0:N], (mix.ys_hi, yr_hi)[second], (mix.ys_lo, yr_lo)[second],
                               start=not second, stop=second == 1)


class Mix:
    pass


def mix_stages(nc, env, layer, d):
    mix = Mix()

    def make(ctx, name, shape, dt=F32):
        return ctx.enter_context(nc.sbuf_tensor(name, shape, dt))

    with ExitStack() as ctx:
        mix.xs = make(ctx, "xs", [P, XT, N])
        mix.last = make(ctx, "last_rows", [P, XT, 9])
        mix.ys_hi = make(ctx, "y_short_hi", [P, MT - RT, N], F32R)
        mix.ys_lo = make(ctx, "y_short_lo", [P, MT - RT, N], F32R)
        with ExitStack() as short:
            mix.sc = make(short, "sc_proj", [P, 12, N])
            mix.z = make(short, "z", [P, 4, N])
            mix.xbc = make(short, "xbc", [P, 8, 3 + N])
            mix.dt = make(short, "dt", [8, N])
            projection_stage(nc, env, mix, layer, d)
            short_mixers_stage(nc, env, mix, layer, d)
        rwkv_stage(nc, env, mix, layer, d)
        output_stage(nc, env, mix, layer, d)


def rwkv_stage(nc, env, mix, layer, d):
    with ExitStack() as ctx:
        def make(name, shape, dt=F32):
            return ctx.enter_context(nc.sbuf_tensor(name, shape, dt))

        mix.kkn = make("kk_normed", [P, RT, N])
        mix.nb = make("minus_b", [P, RT, N])
        mix.cum = make("cum_decay", [P, RT, NCH, C + 1])
        mix.sws = make("decay_gate_sample", [P, RT, NS])
        mix.g = make("gate", [P, RT, N])
        mix.bonus = make("bonus", [P, RT, N])
        rwkv_prepare(nc, env, mix, layer, d)
        rwkv_pairs(nc, env, mix, layer, d)
        rwkv_finish(nc, env, mix, layer, d)


def rwkv_prepare(nc, env, mix, layer, d):
    with Stage(nc, "rprep") as st:
        s, ps = st.s, env.ps
        wa2 = st.sb("w2_a2", [P, D])
        g2, g2b = st.sb("g2", [P, D]), st.sb("g2_tail", [32, D])
        gates = st.sb("decay_gate", [P, RT, NCH, C + 1])
        sq, nrm = st.sb("kk_sq", [P, RT, N]), st.sb("kk_norm", [P, RT, N])
        fac, rk = st.sb("key_factor", [P, 2, N]), st.sb("r_k", [P, 2, N])
        lnb = st.sb("ln_bias", [P, 1])
        r, k, v = mix.xs[:, 0:8], mix.xs[:, 8:16], mix.xs[:, 16:24]
        head = env.const("head")

        with nc.Block() as block:
            @block.sync
            def _(sp):
                sp.dma_start(wa2[0:64, :], d["rwkv_w2"][layer]).then_inc(s("lora_in"), 16)
                sp.dma_start(wa2[64:P, :], d["rwkv_a2"][layer]).then_inc(s("lora_in"), 16)
                sp.dma_start(g2[:], d["rwkv_g2"][layer][0:P]).then_inc(s("lora_in"), 16)
                sp.dma_start(g2b[:], d["rwkv_g2"][layer][P:160]).then_inc(s("lora_in"), 16)

            @block.gpsimd
            def _(pool):
                pool.memset(gates[:, :, :, 0:1], 0.0).then_inc(s("gates_zero"), 1)
                pool.memset(lnb[:], 0.5 * float(np.log(LN_SCALE))).then_inc(s("ln_bias"), 1)

            @block.scalar
            def _(act):
                act.activation(mix.xs[0:64, 24], mix.xs[0:64, 24], ACT.Tanh).then_inc(s("lr_done"), 1)
                act.activation(mix.xs[:, 25], mix.xs[:, 25], ACT.Sigmoid).then_inc(s("lr_done"), 1)
                act.activation(mix.xs[0:32, 26], mix.xs[0:32, 26], ACT.Sigmoid).then_inc(s("lr_done"), 1)
                act.wait_ge(s("gates_zero"), 1)
                for p in range(RT):
                    w_ps, a_ps, g_ps = (ps[:, 2 * i + p % 2, 0:N] for i in range(3))
                    act.wait_ge(s("lora_ps"), 3 * p + 1)
                    act.activation(gates[:, p, :, 1:C + 1], w_ps[:, 0:T].rearrange("p (c t) -> p c t", c=NCH),
                                   ACT.Sigmoid, bias=env.col("rwkv_w0", p)).then_inc(s("gate_in"), 1)
                    act.activation(mix.sws[:, p], w_ps[:, T:N], ACT.Sigmoid,
                                   bias=env.col("rwkv_w0", p)).then_inc(s("lora_read"), 1)
                    act.wait_ge(s("lora_ps"), 3 * p + 2)
                    act.activation(mix.nb[:, p], a_ps, ACT.Sigmoid, bias=env.col("rwkv_a0", p)).then_inc(s("lora_read"), 1)
                    act.wait_ge(s("lora_ps"), 3 * p + 3)
                    act.activation(mix.g[:, p], g_ps, ACT.Copy).then_inc(s("lora_read"), 1)
                act.wait_ge(s("kk_done"), 1)
                act.activation(sq[:], mix.kkn[:], ACT.Square).then_inc(s("kk_sq"), 1)
                act.wait_ge(s("norm_max"), RT)
                act.wait_ge(s("ln_bias"), 1)
                act.activation(nrm[:], nrm[:], ACT.Ln, scale=LN_SCALE).then_inc(s("norm_ln"), 1)
                act.wait_ge(s("norm_ln"), 1)
                act.activation(nrm[:], nrm[:], ACT.Exp, scale=-0.5, bias=lnb[:, 0:1]).then_inc(s("norm_inv"), 1)

            @block.tensor
            def _(pe):
                pe.wait_ge(s("lora_in"), 64)
                pe.wait_ge(s("lr_done"), 3)
                for p in range(RT):
                    w_ps, a_ps, g_ps = (ps[:, 2 * i + p % 2, 0:N] for i in range(3))
                    c = slice(p * P, (p + 1) * P)
                    if p >= 2:
                        pe.wait_ge(s("lora_read"), 3 * (p - 1))
                    pe.matmul(w_ps, wa2[0:64, c], mix.xs[0:64, 24], start=True, stop=True).then_inc(s("lora_ps"), 1)
                    pe.matmul(a_ps, wa2[64:P, c], mix.xs[64:P, 24], start=True, stop=True).then_inc(s("lora_ps"), 1)
                    pe.matmul(g_ps, g2[:, c], mix.xs[:, 25], start=True, stop=False)
                    pe.matmul(g_ps, g2b[:, c], mix.xs[0:32, 26], start=False, stop=True).then_inc(s("lora_ps"), 1)
                pe.wait_ge(s("kk_sq"), 1)
                for p in range(RT):
                    if p >= 2:
                        pe.wait_ge(s("norm_max"), p - 1)
                    pe.matmul(ps[:, 6 + p % 2, 0:N], head, sq[:, p], start=True, stop=True).then_inc(s("norm_ps"), 1)
                pe.wait_ge(s("norm_max"), RT)
                for p in range(RT):
                    pe.wait_ge(s("rk_done"), p + 1)
                    if p >= 2:
                        pe.wait_ge(s("bonus_done"), p - 1)
                    pe.matmul(ps[:, 6 + p % 2, 0:N], head, rk[:, p % 2], start=True, stop=True).then_inc(s("bonus_ps"), 1)

            @block.vector
            def _(dve):
                dve.tensor_tensor(mix.kkn[:], k, env.col("rwkv_k_k", 0, RT).unsqueeze(2).to_broadcast([P, RT, N]),
                                  ALU.mult).then_inc(s("kk_done"), 1)
                for p in range(RT):
                    dve.wait_ge(s("norm_ps"), p + 1)
                    dve.tensor_scalar(nrm[:, p], ps[:, 6 + p % 2, 0:N], 1e-24, None, ALU.max).then_inc(s("norm_max"), 1)
                dve.wait_ge(s("gate_in"), RT)
                for p in range(RT):
                    dve.tensor_tensor_scan(mix.cum[:, p].rearrange("p c t -> p (c t)"), env.const("scan"),
                                           gates[:, p].rearrange("p c t -> p (c t)"), 0.0, ALU.mult,
                                           ALU.add).then_inc(s("cum_done"), 1)
                dve.wait_ge(s("lora_read"), 3 * RT)
                for p in range(RT):
                    if p >= 2:
                        dve.wait_ge(s("k_done"), p - 1)
                    dve.tensor_scalar(fac[:, p % 2], mix.nb[:, p], env.col("rwkv_k_a", p), env.oka[:, p:p + 1],
                                      ALU.mult, ALU.add).then_inc(s("fac_done"), 1)
                    dve.wait_ge(s("fac_done"), p + 1)
                    dve.wait_ge(s("kk_done"), 1)
                    dve.tensor_tensor(k[:, p], k[:, p], fac[:, p % 2], ALU.mult).then_inc(s("k_done"), 1)
                    dve.wait_ge(s("k_done"), p + 1)
                    if p >= 2:
                        dve.wait_ge(s("bonus_ps"), p - 1)
                    dve.scalar_tensor_tensor(out=rk[:, p % 2], in0=r[:, p], scalar=env.col("rwkv_r_k", p), in1=k[:, p],
                                             op0=ALU.mult, op1=ALU.mult).then_inc(s("rk_done"), 1)
                    if p:
                        dve.wait_ge(s("bonus_ps"), p)
                        dve.tensor_tensor(mix.bonus[:, p - 1], v[:, p - 1], ps[:, 6 + (p - 1) % 2, 0:N],
                                          ALU.mult).then_inc(s("bonus_done"), 1)
                dve.wait_ge(s("bonus_ps"), RT)
                dve.tensor_tensor(mix.bonus[:, RT - 1], v[:, RT - 1], ps[:, 6 + (RT - 1) % 2, 0:N],
                                  ALU.mult).then_inc(s("bonus_done"), 1)
                dve.wait_ge(s("norm_inv"), 1)
                dve.tensor_tensor(mix.kkn[:], mix.kkn[:], nrm[:], ALU.mult).then_inc(s("kkn_done"), 1)
                dve.wait_ge(s("kkn_done"), 1)
                dve.scalar_tensor_tensor(out=mix.nb[:], in0=mix.kkn[:], scalar=-1.0, in1=mix.nb[:], op0=ALU.mult,
                                         op1=ALU.mult).then_inc(s("nb_done"), 1)


def rwkv_pairs(nc, env, mix, layer, d):
    LV, V = len(LEVELS), 5
    KK, DEC, MB, KEY, REC = range(V)
    with Stage(nc, "pair") as st:
        s, ps = st.s, env.ps
        pq = st.sb("decays", [P, 2, 2, NCH, C + 1])
        ar = st.sb("a_r", [P, 4, 2, T])
        bk = st.sb("b_k", [P, 2, 2, T])
        cend = st.sb("chunk_decay", [P, RT, NCH])
        tok = st.sb("tok", [P, 3, 3, 2, P])
        gm = st.sb("products", [P, 3, 4, 4, P])
        lev = st.sb("n_levels", [P, 2, 4, P])
        x = st.sb("inverse", [P, 2, 4, P])
        xt = st.sb("inverse_t", [P, 3, 4, P])
        t1 = st.sb("n_x", [P, 4, P])
        rhs = st.sb("rhs", [P, P])
        sa = st.sb("sa", [P, 2, 2, P])
        s0 = st.sb("state", [P, P])
        fin = st.sb("final_state", [P, 2, C])
        vecs = st.sb("sample_vecs", [P, RT, V, NS])
        rows = st.sb("sample_rows", [P, V, NS, HS])
        state = st.sb("sample_wkv", [P, 2, NS, HS])
        prod, outer = st.sb("prod", [P, NS, HS]), st.sb("outer", [P, 2, NS, HS])
        sav = st.sb("sample_sa", [P, NS])
        r, k, v = mix.xs[:, 0:8], mix.xs[:, 8:16], mix.xs[:, 16:24]
        ident, cau = env.const("ident"), env.const("cau2")
        first, levels = env.const("first"), env.const("levels")
        half = (slice(0, C), slice(C, P))
        sin = d["state_rwkv_wkv"][layer].rearrange("b (m h) i j -> m (h i) b j", h=2)
        sout = d["s_wkv"][layer].rearrange("b (m h) i j -> m (h i) b j", h=2)
        fout = d["p_wkv"][layer, 0].rearrange("(m h) i j -> m (h i) j", h=2)
        STEPS = 8

        def load_row(e, m, n):
            for h in range(2):
                e.dma_start(rows[half[h], n].rearrange("p b j -> p (b j)"),
                            d["row_scratch"][n, 2 * m + h].rearrange("b j -> (b j)").unsqueeze(0).to_broadcast([C, NS * HS])
                            ).then_inc(s(f"row{n}_in"), 16)
        T1B, UB, GB, YB, TB, SB = 0, 1, 3, 5, 6, 7

        with nc.Block() as block:
            @block.sync
            def _(sp):
                row_mem = d["row_scratch"]
                sp.wait_ge(s("turned"), 2)
                flat = rows[:].rearrange("p v b j -> p (v b j)")
                for n in range(V):
                    sp.dma_start(row_mem[n].rearrange("f b j -> b f j"),
                                 flat[n * NS:(n + 1) * NS, 0:D].rearrange("b (f j) -> b f j", j=HS)).then_inc(s("scratch"), 16)
                sp.wait_ge(s("scratch"), 16 * V)
                for n in range(V):
                    load_row(sp, 0, n)
                for m in range(2):
                    sp.dma_start(state[:, m], sin[m]).then_inc(s(f"state{m}_in"), 16)
                for m in range(RT):
                    for n, used in ((KK, 1), (DEC, 3), (MB, 4), (KEY, 0), (REC, 7)):
                        if n == KEY:
                            sp.wait_ge(s("key_row_used"), m + 1)
                        else:
                            sp.wait_ge(s("step"), STEPS * m + used)
                        if m + 1 < RT:
                            load_row(sp, m + 1, n)
                        if n == KEY:
                            sp.wait_ge(s("step"), STEPS * m + 6)
                            sp.dma_start(sout[m], state[:, m % 2]).then_inc(s("stored"), 16)
                    if m + 2 < RT:
                        sp.wait_ge(s("stored"), 16 * (m + 1))
                        sp.dma_start(state[:, m % 2], sin[m + 2]).then_inc(s(f"state{m % 2}_in"), 16)
                sp.wait_ge(s("stored"), 16 * RT)

            @block.gpsimd
            def _(pool):
                pool.tensor_copy(vecs[:, :, KK], mix.kkn[:, :, T:N]).then_inc(s("vecs"), 1)
                pool.tensor_copy(vecs[:, :, MB], mix.nb[:, :, T:N]).then_inc(s("vecs"), 1)
                pool.tensor_copy(vecs[:, :, KEY], k[:, :, T:N]).then_inc(s("vecs"), 1)
                pool.tensor_copy(vecs[:, :, REC], r[:, :, T:N]).then_inc(s("vecs"), 1)

                def weigh(p):
                    b4 = p % 4
                    pool.wait_ge(s("pq_done"), 2 * p + 2)
                    if p >= 4:
                        pool.wait_ge(s("y_ps"), p - 3)
                    if p >= 2:
                        pool.wait_ge(s("tok_ps"), 2 * (p - 1))
                    c4 = lambda a: a.rearrange("p (c t) -> p c t", c=NCH)
                    dec, inv = pq[:, p % 2, 0], pq[:, p % 2, 1, :, 1:C + 1]
                    for out, x0, x1 in ((ar[:, b4, 0], mix.kkn[:, p, 0:T], dec[:, :, 0:C]),
                                        (bk[:, p % 2, 0], mix.nb[:, p, 0:T], inv),
                                        (ar[:, b4, 1], r[:, p, 0:T], dec[:, :, 1:C + 1]),
                                        (bk[:, p % 2, 1], k[:, p, 0:T], inv)):
                        pool.tensor_tensor(c4(out), c4(x0), x1, ALU.mult).then_inc(s("weighed"), 1)

                pool.memset(s0[:], 0.0).then_inc(s("zeroed"), 1)
                def level(p, i):
                    n = LV * p + i
                    if n >= 2:
                        pool.wait_ge(s("t1_ps"), n - 1)
                    pool.tensor_tensor(lev[:, n % 2], gm[:, p % 3, :, 0],
                                       levels[:, i * P:(i + 1) * P].unsqueeze(1).to_broadcast([P, 4, P]),
                                       ALU.mult).then_inc(s("lev_done"), 1)

                def key_row(m):
                    pool.wait_ge(s(f"row{KEY}_in"), 32 * (m + 1))
                    if m:
                        pool.wait_ge(s("step"), STEPS * (m - 1) + 6)
                    pool.tensor_tensor(outer[:, 1], rows[:, KEY], v[:, m, T:N].unsqueeze(2).to_broadcast([P, NS, HS]),
                                       ALU.mult).then_inc(s("key_row_used"), 1)

                weigh(0)
                for g in range(RT + 1):
                    l = g - 1
                    if l >= 0:
                        level(l, 1)
                    if g + 1 < RT:
                        weigh(g + 1)
                    if l >= 0:
                        level(l, 2)
                        level(l, 3)
                        key_row(l)
                        level(l, 4)
                    if g < RT:
                        pool.wait_ge(s("masked"), 4 * g + 4)
                        if g >= 3:
                            pool.wait_ge(s("sa_ps"), 4 * (g - 2))
                        pool.tensor_tensor(xt[:, g % 3], gm[:, g % 3, :, 0], first[:].unsqueeze(1).to_broadcast([P, 4, P]),
                                           ALU.mult).then_inc(s("first_done"), 1)
                        level(g, 0)

            @block.scalar
            def _(act):
                def decays(p):
                    if p >= 2:
                        act.wait_ge(s("weighed"), 4 * (p - 1))
                    for i, sign in enumerate((-DECAY, DECAY)):
                        act.activation(pq[:, p % 2, i], mix.cum[:, p], ACT.Exp, scale=sign).then_inc(s("pq_done"), 1)

                def tokens(p, part):
                    act.wait_ge(s("tok_ps"), 2 * p + part + 1)
                    dst, w = (tok[:, p % 3, 0:2], 512) if part == 0 else (tok[:, p % 3, 2:3], T)
                    act.activation(dst.rearrange("p a c f -> p (a c f)"), ps[:, TB, 0:w], ACT.Copy).then_inc(s("tok_in"), 1)

                def t1_copy(p, i):
                    n = LV * p + i
                    act.wait_ge(s("t1_ps"), n + 1)
                    if n:
                        act.wait_ge(s("ut_ps"), n)
                    act.activation(t1[:].rearrange("p q t -> p (q t)"), ps[:, T1B, :], ACT.Copy).then_inc(s("t1_in"), 1)

                def x_copy(p):
                    act.wait_ge(s("x_ps"), p + 1)
                    act.activation(x[:, p % 2].rearrange("p q t -> p (q t)"), ps[:, T1B, :], ACT.Copy).then_inc(s("x_in"), 1)

                def rhs_copy(p, c):
                    w, n = half[c % 2], 4 * p + c
                    act.wait_ge(s("rhs_ps"), n + 1)
                    act.activation(rhs[w], ps[w, SB, 0:P], ACT.Copy).then_inc(s("rhs_in"), 1)

                def sa_copy(p, c):
                    w, n = half[c % 2], 4 * p + c
                    act.wait_ge(s("sa_ps"), n + 1)
                    act.activation(sa[w, p % 2, c // 2], ps[w, TB, 0:P], ACT.Copy).then_inc(s("sa_in"), 1)

                def state_copy(p, c):
                    n = 4 * p + c
                    act.wait_ge(s("st_ps"), n + 1)
                    act.wait_ge(s("zeroed"), 1)
                    if p and c == 0:
                        act.wait_ge(s("fin_ps"), p)
                    for h in range(2):
                        q = half[h]
                        act.activation(s0[q, q], ps[q, SB, q], ACT.Copy,
                                       scale=cend[q, p, c:c + 1]).then_inc(s("st_in"), 1)

                def final_copy(p):
                    act.wait_ge(s("fin_ps"), p + 1)
                    if p >= 2:
                        act.wait_ge(s(f"fin{p % 2}_stored"), 16 * (p // 2))
                    for h in range(2):
                        q = half[h]
                        act.activation(fin[q, p % 2], ps[q, SB, q], ACT.Copy).then_inc(s("fin_in"), 1)
                    act.wait_ge(s("fin_in"), 2 * p + 2)
                    act.dma_start(fout[p], fin[:, p % 2]).then_inc(s(f"fin{p % 2}_stored"), 16)

                decays(0)
                act.activation(vecs[:, :, DEC], mix.sws[:], ACT.Exp, scale=-DECAY).then_inc(s("vecs"), 1)
                act.activation(cend[:], mix.cum[:, :, :, C], ACT.Exp, scale=-DECAY).then_inc(s("cend"), 1)
                act.wait_ge(s("vecs_ps"), 1)
                for i in range(2):
                    act.activation(rows[0:V * NS].rearrange("p v b j -> p (v b j)")[:, i * 512:(i + 1) * 512],
                                   ps[0:V * NS, UB + i, :], ACT.Copy).then_inc(s("turned"), 1)
                act.wait_ge(s("cend"), 1)
                for g in range(RT + 2):
                    l, c = g - 1, g - 2
                    if g + 1 < RT:
                        decays(g + 1)
                    for i in range(LV):
                        if 0 <= l < RT and i:
                            t1_copy(l, i)
                        if c >= 0 and i:
                            state_copy(c, i - 1)
                        if c >= 0 and i < NCH:
                            rhs_copy(c, i)
                        if 0 <= l < RT and i == 0:
                            t1_copy(l, i)
                        if g < RT and i == LV - 1:
                            tokens(g, 0)
                            tokens(g, 1)
                        if c >= 0 and i < NCH:
                            sa_copy(c, i)
                    if c >= 0:
                        final_copy(c)
                    if g < RT:
                        x_copy(g)
                for i in range(2):
                    act.wait_ge(s(f"fin{i}_stored"), 16 * (RT // 2))

            @block.vector
            def _(dve):
                def mask(p, j):
                    dve.wait_ge(s("g_ps"), 4 * p + j + 1)
                    if p >= 3 and j == 0:
                        dve.wait_ge(s("y_ps"), p - 2)
                    dve.tensor_tensor(gm[:, p % 3, j].rearrange("p (a k) t -> p a (k t)", a=2),
                                      ps[:, GB + j % 2, :].rearrange("p (a t) -> p a t", a=2),
                                      cau[:].unsqueeze(1).to_broadcast([P, 2, 2 * P]), ALU.mult).then_inc(s("masked"), 1)

                def start(p):
                    dve.wait_ge(s("first_done"), p + 1)
                    dve.tensor_tensor(xt[:, p % 3], xt[:, p % 3], ident.unsqueeze(1).to_broadcast([P, 4, P]),
                                      ALU.add).then_inc(s("start"), 1)

                def update(p, i):
                    four = lambda b: ps[:, b, :].rearrange("p (q t) -> p q t", q=4)
                    if i < LV - 1:
                        dve.wait_ge(s("u_ps"), (LV - 1) * p + i + 1)
                        if i:
                            dve.wait_ge(s("x_up"), (LV - 1) * p + i)
                        else:
                            dve.wait_ge(s("x_in"), p + 1)
                        dve.tensor_tensor(x[:, p % 2], x[:, p % 2], four(UB), ALU.add).then_inc(s("x_up"), 1)
                    dve.wait_ge(s("ut_ps"), LV * p + i + 1)
                    if i:
                        dve.wait_ge(s("xt_up"), LV * p + i)
                    dve.tensor_tensor(xt[:, p % 3], xt[:, p % 3], four(UB + 1), ALU.add).then_inc(s("xt_up"), 1)

                wide = lambda a: a.unsqueeze(2).to_broadcast([P, NS, HS])

                def step(m, i):
                    st0, n = state[:, m % 2], STEPS * m + i
                    if n:
                        dve.wait_ge(s("step"), n)
                    if i == 0:
                        dve.wait_ge(s(f"state{m % 2}_in"), 16 * (m // 2 + 1))
                        dve.wait_ge(s(f"row{KK}_in"), 32 * (m + 1))
                        op = dve.tensor_tensor(prod[:], st0, rows[:, KK], ALU.mult)
                    elif i == 1:
                        op = dve.tensor_reduce(sav[:], prod[:], AX.X, ALU.add)
                    elif i == 2:
                        dve.wait_ge(s(f"row{DEC}_in"), 32 * (m + 1))
                        op = dve.tensor_tensor(st0, st0, rows[:, DEC], ALU.mult)
                    elif i == 3:
                        dve.wait_ge(s(f"row{MB}_in"), 32 * (m + 1))
                        op = dve.tensor_tensor(outer[:, 0], rows[:, MB], wide(sav[:]), ALU.mult)
                    elif i == 4:
                        op = dve.tensor_tensor(st0, st0, outer[:, 0], ALU.add)
                    elif i == 5:
                        dve.wait_ge(s("key_row_used"), m + 1)
                        op = dve.tensor_tensor(st0, st0, outer[:, 1], ALU.add)
                    elif i == 6:
                        dve.wait_ge(s(f"row{REC}_in"), 32 * (m + 1))
                        op = dve.tensor_tensor(prod[:], st0, rows[:, REC], ALU.mult)
                    else:
                        op = dve.tensor_reduce(r[:, m, T:N], prod[:], AX.X, ALU.add)
                    op.then_inc(s("step"), 1)

                for g in range(RT + 2):
                    l, c = g - 1, g - 2
                    for i in range(LV):
                        if g < RT and i < 4:
                            mask(g, i)
                        if 0 <= l < RT:
                            update(l, i)
                            for n in ((), (0, 1), (2, 3), (4,), (5,))[i]:
                                step(l, n)
                    if g < RT:
                        start(g)
                    if c >= 0:
                        dve.wait_ge(s("y_ps"), c + 1)
                        dve.tensor_copy(r[:, c, 0:T], ps[:, YB, 0:T]).then_inc(s("y_in"), 1)
                    if 0 <= l < RT:
                        step(l, 6)
                        step(l, 7)

            @block.tensor
            def _(pe):
                def turn(p, part):
                    if part:
                        pe.wait_ge(s("tok_in"), 2 * p + 1)
                    elif p >= 2:
                        pe.wait_ge(s("sa_in"), 4 * (p - 1))
                    src = [bk[:, p % 2, 0], bk[:, p % 2, 1]] if part == 0 else [v[:, p]]
                    for i, x0 in enumerate(src):
                        for cp in range(2):
                            at = (2 * i + cp) * P
                            mm = pe.transpose(ps[:, TB, at:at + P], x0[:, cp * P:(cp + 1) * P], ident)
                    mm.then_inc(s("tok_ps"), 1)

                def gram(p, j):
                    h, cp, bank = half[j // 2], j % 2, GB + j % 2
                    c, n = slice(cp * P, cp * P + P), 4 * p + j
                    if n >= 2:
                        pe.wait_ge(s("masked"), n - 1)
                    if j == 0:
                        pe.wait_ge(s("weighed"), 4 * p + 4)
                    pe.matmul(ps[:, bank, 0:T], bk[h, p % 2, 0, c], ar[h, p % 4, :, c], start=True, stop=True)
                    pe.matmul(ps[:, bank, T:2 * T], bk[h, p % 2, 1, c], ar[h, p % 4, :, c], start=True,
                              stop=True).then_inc(s("g_ps"), 1)

                def turn_x(p):
                    pe.wait_ge(s("start"), p + 1)
                    if p:
                        pe.wait_ge(s("t1_in"), LV * p)
                    for q in range(4):
                        mm = pe.transpose(ps[:, T1B, q * P:(q + 1) * P], xt[:, p % 3, q], ident)
                    mm.then_inc(s("x_ps"), 1)

                def level_t1(p, i):
                    n = LV * p + i
                    pe.wait_ge(s("lev_done"), n + 1)
                    if i:
                        pe.wait_ge(s("x_up"), (LV - 1) * p + i)
                        pe.wait_ge(s("t1_in"), n)
                    else:
                        pe.wait_ge(s("x_in"), p + 1)
                    for q in range(4):
                        mm = pe.matmul(ps[:, T1B, q * P:(q + 1) * P], lev[:, n % 2, q], x[:, p % 2, q], start=True, stop=True)
                    mm.then_inc(s("t1_ps"), 1)

                def level_u(p, i):
                    n = LV * p + i
                    pe.wait_ge(s("t1_in"), n + 1)
                    if n:
                        pe.wait_ge(s("xt_up"), n)
                    if i < LV - 1:
                        for q in range(4):
                            mm = pe.matmul(ps[:, UB, q * P:(q + 1) * P], xt[:, p % 3, q], t1[:, q], start=True, stop=True)
                        mm.then_inc(s("u_ps"), 1)
                    for q in range(4):
                        mm = pe.matmul(ps[:, UB + 1, q * P:(q + 1) * P], t1[:, q], xt[:, p % 3, q], start=True, stop=True)
                    mm.then_inc(s("ut_ps"), 1)

                def chunk_rhs(p, c):
                    cp, w, n = c // 2, half[c % 2], 4 * p + c
                    if c == 0:
                        pe.wait_ge(s("xt_up"), LV * (p + 1))
                        pe.wait_ge(s("tok_in"), 2 * p + 2)
                        if p:
                            pe.wait_ge(s("fin_in"), 2 * p)
                    else:
                        pe.wait_ge(s("st_in"), 2 * n)
                    for h in range(2):
                        f = half[h]
                        mm = pe.matmul(ps[w, SB, f], gm[:, p % 3, 2 * h + cp, 2, w], tok[:, p % 3, 2, cp, f], start=h == 0,
                                       stop=c == 0, skip_group_check=True)
                    if c:
                        mm = pe.matmul(ps[w, SB, 0:P], ar[:, p % 4, 0, c * C:c * C + C], s0[:], start=False, stop=True,
                                       skip_group_check=True)
                    mm.then_inc(s("rhs_ps"), 1)
                    if c % 2 == 0:
                        if p and c == 0:
                            pe.wait_ge(s("y_in"), p)
                        for h in range(2):
                            f = half[h]
                            pe.matmul(ps[f, YB, cp * P:cp * P + P], tok[:, p % 3, 2, cp, f], gm[:, p % 3, 2 * h + cp, 3],
                                      start=c == 0, stop=False, skip_group_check=True)
                    if c:
                        pe.matmul(ps[:, YB, c * C:c * C + C], s0[:], ar[:, p % 4, 1, c * C:c * C + C], start=False, stop=False,
                                  skip_group_check=True)

                def chunk_sa(p, c):
                    cp, w, n = c // 2, half[c % 2], 4 * p + c
                    pe.wait_ge(s("rhs_in"), n + 1)
                    if n:
                        pe.wait_ge(s("sa_in"), n)
                    if c == 0:
                        pe.wait_ge(s("tok_in"), 2 * min(p + 2, RT))
                    for h in range(2):
                        f = half[h]
                        mm = pe.matmul(ps[w, TB, f], xt[w, p % 3, 2 * h + cp, w], rhs[w, f], start=True, stop=True)
                    mm.then_inc(s("sa_ps"), 1)

                def chunk_state(p, c):
                    cp, w, n = c // 2, half[c % 2], 4 * p + c
                    if c:
                        pe.matmul(ps[:, SB, 0:P], ident, s0[:], start=True, stop=False)
                    pe.matmul(ps[:, SB, 0:P], tok[w, p % 3, 1, cp], tok[w, p % 3, 2, cp], start=c == 0, stop=False)
                    pe.wait_ge(s("sa_in"), n + 1)
                    pe.matmul(ps[:, SB, 0:P], tok[w, p % 3, 0, cp], sa[w, p % 2, cp], start=False,
                              stop=True).then_inc(s("st_ps"), 1)
                    if c % 2:
                        for h in range(2):
                            f = half[h]
                            mm = pe.matmul(ps[f, YB, cp * P:cp * P + P], sa[:, p % 2, cp, f], gm[:, p % 3, 2 * h + cp, 1],
                                           start=False, stop=c == 3, skip_group_check=True)
                        if c == 3:
                            mm.then_inc(s("y_ps"), 1)

                pe.wait_ge(s("vecs"), V)
                for m in range(RT):
                    mm = pe.transpose(ps[0:V * NS, UB + m // 4, m % 4 * P:m % 4 * P + P],
                                      vecs[:, m].rearrange("p v b -> p (v b)"), ident)
                mm.then_inc(s("vecs_ps"), 1)
                pe.wait_ge(s("turned"), 2)
                for g in range(RT + 2):
                    l, c = g - 1, g - 2
                    for i in range(LV):
                        if 0 <= l < RT and i:
                            level_t1(l, i)
                        if c >= 0 and i:
                            chunk_state(c, i - 1)
                        if g < RT and i < 4:
                            gram(g, i)
                        if c >= 0 and i < NCH:
                            chunk_rhs(c, i)
                        if 0 <= l < RT and i == 0:
                            level_t1(l, i)
                        if g < RT and i == LV - 1:
                            turn(g, 0)
                        if 0 <= l < RT:
                            level_u(l, i)
                        if c >= 0 and i < NCH:
                            chunk_sa(c, i)
                        if g < RT and i == LV - 1:
                            turn(g, 1)
                    if c >= 0:
                        pe.wait_ge(s("st_in"), 8 * (c + 1))
                        pe.transpose(ps[:, SB, 0:P], s0[:], ident).then_inc(s("fin_ps"), 1)
                    if g < RT:
                        turn_x(g)


def rwkv_finish(nc, env, mix, layer, d):
    with Stage(nc, "rfin") as st:
        s, ps = st.s, env.ps
        dev, sq = st.sb("deviation", [P, RT, N]), st.sb("dev_sq", [P, RT, N])
        y, head = mix.xs[:, 0:8], env.const("head")

        with nc.Block() as block:
            @block.scalar
            def _(act):
                act.wait_ge(s("dev_done"), RT)
                act.activation(sq[:], dev[:], ACT.Square).then_inc(s("dev_sq"), 1)
                for m in range(RT):
                    act.wait_ge(s("var_ps"), m + 1)
                    act.activation(sq[:, m], ps[:, m % 4, 0:N], ACT.Ln, bias=env.eps[:, 1:2], scale=1.0 / HS).then_inc(s("var_ln"), 1)
                act.wait_ge(s("var_ln"), RT)
                act.activation(sq[:], sq[:], ACT.Exp, scale=-0.5).then_inc(s("rstd"), 1)

            @block.tensor
            def _(pe):
                for m in range(RT):
                    if m >= 4:
                        pe.wait_ge(s("dev_done"), m - 3)
                    pe.matmul(ps[:, 4 + m % 4, 0:N], head, y[:, m], start=True, stop=True).then_inc(s("mean_ps"), 1)
                pe.wait_ge(s("dev_sq"), 1)
                for m in range(RT):
                    if m >= 4:
                        pe.wait_ge(s("var_ln"), m - 3)
                    pe.matmul(ps[:, m % 4, 0:N], head, sq[:, m], start=True, stop=True).then_inc(s("var_ps"), 1)

            @block.vector
            def _(dve):
                for m in range(RT):
                    dve.wait_ge(s("mean_ps"), m + 1)
                    dve.scalar_tensor_tensor(out=dev[:, m], in0=ps[:, 4 + m % 4, 0:N], scalar=-1.0 / HS, in1=y[:, m],
                                             op0=ALU.mult, op1=ALU.add).then_inc(s("dev_done"), 1)
                dve.wait_ge(s("rstd"), 1)
                dve.tensor_tensor(dev[:], dev[:], sq[:], ALU.mult).then_inc(s("normed"), 1)
                dve.wait_ge(s("normed"), 1)
                for m in range(RT):
                    dve.tensor_scalar(dev[:, m], dev[:, m], env.col("rwkv_ln_w", m), env.col("rwkv_ln_b", m), ALU.mult,
                                      ALU.add).then_inc(s("affine"), 1)
                dve.wait_ge(s("affine"), RT)
                dve.tensor_tensor(dev[:], dev[:], mix.bonus[:], ALU.add).then_inc(s("with_bonus"), 1)
                dve.wait_ge(s("with_bonus"), 1)
                for m in range(RT):
                    dve.tensor_tensor(y[:, m], dev[:, m], mix.g[:, m], ALU.mult).then_inc(s("y_out"), 1)


OUTS = {
    "y_prompt": (1, T, D), "y_sample": (NS, 1, D),
    "p_shift": (DEPTH, 1, RWKV_PROJ), "p_wkv": (DEPTH, 1, 16, HS, HS), "p_sc": (DEPTH, 1, 2, SC),
    "p_conv": (DEPTH, 1, 3, D), "p_ssm": (DEPTH, 1, 8, HS, P),
    "s_shift": (DEPTH, NS, RWKV_PROJ), "s_wkv": (DEPTH, NS, 16, HS, HS), "s_sc": (DEPTH, NS, 2, SC),
    "s_conv": (DEPTH, NS, 3, D), "s_ssm": (DEPTH, NS, 8, HS, P),
}


def trunk(nc, d, stages=("ffn1", "mix", "ffn2")):
    with ExitStack() as ctx:
        def sb(name, shape, dt=F32):
            return ctx.enter_context(nc.sbuf_tensor(name, shape, dt))

        env = Env()
        env.cst = sb("cst", [P, sum(n for _, n in CONST_WHERE.values())])
        env.x = sb("x", [P, KT, N])
        env.eps = sb("eps", [P, 3])
        env.cols = sb("cols", [P, NCOLS])
        env.omu = sb("one_minus_mu", [P, XT])
        env.oka = sb("one_minus_ka", [P, RT])
        env.shift = sb("shift_state", [P, XT, NS])
        env.scb = sb("sc_state", [P, ST, 2 * NS])
        env.conv = sb("conv_state", [P, 8, 3 * NS])
        env.heads = sb("ssm_heads", [8, 5])
        env.dcol = sb("ssm_d", [P, 4])
        env.ps = ctx.enter_context(nc.psum_tensor("ps", [P, 8, 512], F32))
        d["row_scratch"] = nc.dram_tensor("row_scratch", (5, 16, NS, HS), F32, kind="Internal").ap()
        load_stage(nc, env, d)
        with nc.Fori(0, DEPTH) as layer:
            vector_stage(nc, env, layer, d)
            if "ffn1" in stages:
                ffn_stage(nc, env, layer, "ffn1", "norm_ffn1", d["ffn1_w_in"], d["ffn1_w_out"])
            if "mix" in stages:
                mix_stages(nc, env, layer, d)
            if "ffn2" in stages:
                ffn_stage(nc, env, layer, "ffn2", "norm_ffn2", d["ffn2_w_in"], d["ffn2_w_out"])
        final_stage(nc, env, d)


def kernel(**inputs):
    import concourse.bacc as bacc
    from concourse.bass_utils import run_bass_kernel_spmd

    nc = bacc.Bacc("TRN2", target_bir_lowering=False, num_devices=1)
    arrays, d = {}, {}
    for name, a in inputs.items():
        a = np.ascontiguousarray(a)
        arrays[f"in_{name}"] = a
        d[name] = nc.dram_tensor(f"in_{name}", a.shape, mybir.dt.from_np(a.dtype), kind="ExternalInput").ap()
    cst = shape_constants()[0]
    arrays["in_cst"] = cst
    d["cst"] = nc.dram_tensor("in_cst", cst.shape, F32, kind="ExternalInput").ap()
    for name, shape in OUTS.items():
        d[name] = nc.dram_tensor(f"out_{name}", shape, F32, kind="ExternalOutput").ap()
    trunk(nc, d)
    r = run_bass_kernel_spmd(nc, [arrays], core_ids=[0])
    return tuple(r.results[0][f"out_{name}"] for name in OUTS)
```
